# Optimizing a Trainium2 kernel written in Bass

```python
import jax, jax.numpy as jnp
from jax import lax
import numpy as np
import math, functools

D_MODEL = 1024
BATCH = 1
SEQ = 1024
DEPTH = 1

GRID_W = 64
CTX_LEN = 256
N_FOURIER_GROUPS = 4
FOURIER_GROUP_W = 128
FOURIER_W = N_FOURIER_GROUPS * FOURIER_GROUP_W
N_HEADS = 8
QK_NOPE = 64
QK_ROPE = 32
HEAD_QK = QK_NOPE + QK_ROPE
V_DIM = 64
Q_LORA = 256
KV_LORA = 128
MLA_W = N_HEADS * V_DIM
N_BRANCH = 2
D_FF = 4 * D_MODEL
D_IN = FOURIER_W + Q_LORA + KV_LORA + QK_ROPE + N_BRANCH * D_MODEL
ROPE_THETA = 10000.0
Q_BLOCK = 128
EPS = 1e-6


def rmsnorm(x, g):
    xf = x.astype(jnp.float32)
    y = xf * lax.rsqrt(jnp.mean(xf * xf, axis=-1, keepdims=True) + EPS)
    return (y * g.astype(jnp.float32)).astype(x.dtype)

def modulate(h, shift, scale):
    return h * (1 + scale) + shift

def axial_rope_tables(n):
    rows = n // GRID_W
    row = jnp.repeat(jnp.arange(rows, dtype=jnp.float32), GRID_W)
    col = jnp.tile(jnp.arange(GRID_W, dtype=jnp.float32), rows)
    n_freq = QK_ROPE // 4
    freqs = ROPE_THETA ** (-jnp.arange(n_freq, dtype=jnp.float32) / n_freq)
    ang_r = row[:, None] * freqs[None, :]
    ang_c = col[:, None] * freqs[None, :]
    ang = jnp.concatenate([ang_r, ang_r, ang_c, ang_c], axis=-1)
    return jnp.cos(ang), jnp.sin(ang)

def apply_rope(x, cos, sin):
    a1, a2, b1, b2 = jnp.split(x, 4, axis=-1)
    rot = jnp.concatenate([-a2, a1, -b2, b1], axis=-1)
    return x * cos[None, :, None, :].astype(x.dtype) + rot * sin[None, :, None, :].astype(x.dtype)

def split_proj(p):
    o1 = FOURIER_W
    o2 = o1 + Q_LORA
    o3 = o2 + KV_LORA
    o4 = o3 + QK_ROPE
    return p[..., :o1], p[..., o1:o2], p[..., o2:o3], p[..., o3:o4], p[..., o4:]

def fourier_mix(f):
    B, N, _ = f.shape
    fg = f.reshape(B, N, N_FOURIER_GROUPS, FOURIER_GROUP_W).astype(jnp.float32)
    y = jnp.fft.fft2(fg, axes=(1, 3), norm="ortho").real
    return y.reshape(B, N, FOURIER_W).astype(f.dtype)

def mla_kv(kv_lat, k_rope, kv_norm_g, w_kvb, k_gain, rope):
    B, N, _ = kv_lat.shape
    kv = (rmsnorm(kv_lat, kv_norm_g) @ w_kvb).reshape(B, N, N_HEADS, QK_NOPE + V_DIM)
    k_nope, v = kv[..., :QK_NOPE], kv[..., QK_NOPE:]
    k_r = jnp.broadcast_to(k_rope[:, :, None, :], (B, N, N_HEADS, QK_ROPE))
    k = rmsnorm(jnp.concatenate([k_nope, k_r], axis=-1), k_gain)
    if rope is not None:
        k = jnp.concatenate([k[..., :QK_NOPE], apply_rope(k[..., QK_NOPE:], *rope)], axis=-1)
    return k, v

def mla_q(q_lat, q_norm_g, w_qb, q_gain, rope):
    B, N, _ = q_lat.shape
    q = (rmsnorm(q_lat, q_norm_g) @ w_qb).reshape(B, N, N_HEADS, HEAD_QK)
    q = rmsnorm(q, q_gain)
    if rope is not None:
        q = jnp.concatenate([q[..., :QK_NOPE], apply_rope(q[..., QK_NOPE:], *rope)], axis=-1)
    return q

def latent_attention(q, k_all, v_all):
    B, S, H, Dh = q.shape
    nb = S // Q_BLOCK
    qb = q.reshape(B, nb, Q_BLOCK, H, Dh).transpose(1, 0, 2, 3, 4)
    scale = HEAD_QK ** -0.5

    def one_block(qblk):
        s = jnp.einsum('bqhd,bkhd->bhqk', qblk, k_all, preferred_element_type=jnp.float32) * scale
        p = jax.nn.softmax(s, axis=-1).astype(v_all.dtype)
        return jnp.einsum('bhqk,bkhd->bqhd', p, v_all)

    o = lax.map(one_block, qb)
    return o.transpose(1, 0, 2, 3, 4).reshape(B, S, H * V_DIM)

def context_attention(q, k, v):
    B, N = q.shape[0], q.shape[1]
    s = jnp.einsum('bqhd,bkhd->bhqk', q, k, preferred_element_type=jnp.float32) * (HEAD_QK ** -0.5)
    p = jax.nn.softmax(s, axis=-1).astype(v.dtype)
    return jnp.einsum('bhqk,bkhd->bqhd', p, v).reshape(B, N, N_HEADS * V_DIM)

def merge_branches(f_mix, att, gates, w_fourier, w_mla_o, b_gate, w_out):
    g = jax.nn.sigmoid(gates + b_gate)
    g_f, g_a = g[..., :D_MODEL], g[..., D_MODEL:]
    y = g_f * (f_mix @ w_fourier) + g_a * (att @ w_mla_o)
    return y @ w_out

def sq_relu_mlp(h, w_up, w_down):
    return jnp.square(jax.nn.relu(h @ w_up)) @ w_down

def first_inputs(seed: int = 0) -> dict:
    key = jax.random.key(seed)
    ks = jax.random.split(key, 24)
    D, L = D_MODEL, DEPTH

    def w(k, shape, fan_in, mult=1.0):
        return jax.random.normal(k, shape, jnp.float32) * (mult * fan_in ** -0.5)

    def gain(k, shape):
        return 1.0 + 0.05 * jax.random.normal(k, shape, jnp.float32)

    return {
        "x": jax.random.normal(ks[0], (BATCH, SEQ, D), jnp.float32),
        "c": jax.random.normal(ks[1], (BATCH, D), jnp.float32),
        "ctx": jax.random.normal(ks[2], (BATCH, CTX_LEN, D), jnp.float32),
        "c_ctx": jax.random.normal(ks[3], (D,), jnp.float32),
        "ada_w": w(ks[4], (L, D, 6 * D), D, 0.5),
        "ada_b": 0.02 * jax.random.normal(ks[5], (L, 6 * D), jnp.float32),
        "norm1_g": gain(ks[6], (L, D)),
        "norm2_g": gain(ks[7], (L, D)),
        "w_in": w(ks[8], (L, D, D_IN), D),
        "b_gate": 0.02 * jax.random.normal(ks[9], (L, N_BRANCH * D), jnp.float32),
        "w_fourier": w(ks[10], (L, FOURIER_W, D), FOURIER_W),
        "q_norm_g": gain(ks[11], (L, Q_LORA)),
        "w_qb": w(ks[12], (L, Q_LORA, N_HEADS * HEAD_QK), Q_LORA),
        "kv_norm_g": gain(ks[13], (L, KV_LORA)),
        "w_kvb": w(ks[14], (L, KV_LORA, N_HEADS * (QK_NOPE + V_DIM)), KV_LORA),
        "q_gain": gain(ks[15], (L, HEAD_QK)),
        "k_gain": gain(ks[16], (L, HEAD_QK)),
        "w_mla_o": w(ks[17], (L, MLA_W, D), MLA_W),
        "w_out": w(ks[18], (L, D, D), D),
        "w_up": w(ks[19], (L, D, D_FF), D),
        "w_down": w(ks[20], (L, D_FF, D), D_FF),
    }

def first_block(x, c, ctx, c_ctx, ada_w, ada_b, norm1_g, norm2_g, w_in, b_gate, w_fourier, q_norm_g, w_qb,
              kv_norm_g, w_kvb, q_gain, k_gain, w_mla_o, w_out, w_up, w_down):
    rope = axial_rope_tables(x.shape[1])
    for l in range(DEPTH):
        last = l == DEPTH - 1
        mod_x = jax.nn.silu(c) @ ada_w[l] + ada_b[l]
        sh1, sc1, g1, sh2, sc2, g2 = jnp.split(mod_x[:, None, :], 6, axis=-1)
        mod_c = jax.nn.silu(c_ctx) @ ada_w[l] + ada_b[l]
        csh1, csc1, cg1, csh2, csc2, cg2 = jnp.split(mod_c, 6, axis=-1)

        hc = modulate(rmsnorm(ctx, norm1_g[l]), csh1, csc1)
        pc = hc @ w_in[l]
        fc, qlc, kvlc, krc, gc = split_proj(pc)
        kc, vc = mla_kv(kvlc, krc, kv_norm_g[l], w_kvb[l], k_gain[l], None)

        hx = modulate(rmsnorm(x, norm1_g[l]), sh1, sc1)
        px = hx @ w_in[l]
        fx, qlx, kvlx, krx, gx = split_proj(px)
        kx, vx = mla_kv(kvlx, krx, kv_norm_g[l], w_kvb[l], k_gain[l], rope)
        qx = mla_q(qlx, q_norm_g[l], w_qb[l], q_gain[l], rope)
        att_x = latent_attention(qx, jnp.concatenate([kx, kc], axis=1), jnp.concatenate([vx, vc], axis=1))
        y_x = merge_branches(fourier_mix(fx), att_x, gx, w_fourier[l], w_mla_o[l], b_gate[l], w_out[l])

        if not last:
            qc = mla_q(qlc, q_norm_g[l], w_qb[l], q_gain[l], None)
            att_c = context_attention(qc, kc, vc)
            y_c = merge_branches(fourier_mix(fc), att_c, gc, w_fourier[l], w_mla_o[l], b_gate[l], w_out[l])
            ctx = ctx + cg1 * y_c
            hc2 = modulate(rmsnorm(ctx, norm2_g[l]), csh2, csc2)
            ctx = ctx + cg2 * sq_relu_mlp(hc2, w_up[l], w_down[l])

        x = x + g1 * y_x
        h2 = modulate(rmsnorm(x, norm2_g[l]), sh2, sc2)
        x = x + g2 * sq_relu_mlp(h2, w_up[l], w_down[l])
    return x


DEPTH_2 = 2

N_MEM = 256
D_MAIN = D_MODEL
N_POOL_GROUPS = 4
POOL_WINDOWS = (2, 4, 8, 16)
POOL_GROUP = D_MAIN // N_POOL_GROUPS
FOX_HEADS = 16
FOX_HEAD_DIM = D_MAIN // FOX_HEADS
MEM_HEADS = 4
MEM_HEAD_DIM = 128
D_MEM = MEM_HEADS * MEM_HEAD_DIM
D_MIX = D_MAIN + D_MEM
D_IN_2 = 2 * D_MIX
N_A = DEPTH_2 // 2
N_B = DEPTH_2 - N_A
ALPHA = (2 * DEPTH_2) ** 0.25
BETA = (8 * DEPTH_2) ** -0.25
LN_EPS = 1e-5


def layer_norm(x, g, b):
    xf = x.astype(jnp.float32)
    mu = jnp.mean(xf, axis=-1, keepdims=True)
    var = jnp.mean(jnp.square(xf - mu), axis=-1, keepdims=True)
    y = (xf - mu) * lax.rsqrt(var + LN_EPS) * g.astype(jnp.float32) + b.astype(jnp.float32)
    return y.astype(x.dtype)

def causal_multiscale_pool(u, pool_w, pool_scale):
    B, S, _ = u.shape
    ug = u.reshape(B, S, N_POOL_GROUPS, POOL_GROUP)
    cs = jnp.cumsum(ug.astype(jnp.float32), axis=1)
    cs = jnp.pad(cs, ((0, 0), (1, 0), (0, 0), (0, 0)))
    t = jnp.arange(S)
    outs = []
    for gi, w in enumerate(POOL_WINDOWS):
        c = cs[:, :, gi]
        upper = c[:, 1:]
        lower = jnp.concatenate(
            [jnp.zeros((B, w - 1, POOL_GROUP), jnp.float32), c[:, :S + 1 - w]], axis=1)
        count = jnp.minimum(t + 1, w).astype(jnp.float32)[None, :, None]
        outs.append((upper - lower) / count - ug[:, :, gi].astype(jnp.float32))
    pm = jnp.stack(outs, axis=2).astype(u.dtype)
    mixed = jnp.einsum('bsgc,gcd->bsgd', pm, pool_w)
    return mixed.reshape(B, S, D_MAIN) * pool_scale

def shared_kv(x, w_kv_shared, b_forget):
    B, S, _ = x.shape
    h = x @ w_kv_shared
    k = h[..., :D_MAIN].reshape(B, S, FOX_HEADS, FOX_HEAD_DIM)
    v = h[..., D_MAIN:2 * D_MAIN].reshape(B, S, FOX_HEADS, FOX_HEAD_DIM)
    f_logit = h[..., 2 * D_MAIN:].astype(jnp.float32) + b_forget.astype(jnp.float32)
    log_f = jax.nn.log_sigmoid(f_logit)
    cum = jnp.cumsum(log_f, axis=1)
    return k, v, cum

def forgetting_attention(u, k, v, cum):
    B, S, _ = u.shape
    q = u.reshape(B, S, FOX_HEADS, FOX_HEAD_DIM)
    nb = S // Q_BLOCK
    qb = q.reshape(B, nb, Q_BLOCK, FOX_HEADS, FOX_HEAD_DIM).transpose(1, 0, 2, 3, 4)
    cb = cum.reshape(B, nb, Q_BLOCK, FOX_HEADS).transpose(1, 0, 3, 2)
    cum_k = cum.transpose(0, 2, 1)
    starts = jnp.arange(nb) * Q_BLOCK
    kpos = jnp.arange(S)
    scale = FOX_HEAD_DIM ** -0.5

    def block(args):
        qi, ci, s0 = args
        logits = jnp.einsum('bqhd,bkhd->bhqk', qi, k,
                            preferred_element_type=jnp.float32) * scale
        logits = logits + (ci[..., :, None] - cum_k[:, :, None, :])
        qpos = s0 + jnp.arange(Q_BLOCK)
        mask = kpos[None, :] <= qpos[:, None]
        logits = jnp.where(mask[None, None], logits, -jnp.inf)
        p = jax.nn.softmax(logits, axis=-1)
        return jnp.einsum('bhqk,bkhd->bqhd', p.astype(v.dtype), v)

    out = lax.map(block, (qb, cb, starts))
    return out.transpose(1, 0, 2, 3, 4).reshape(B, S, D_MAIN)

def memory_attention(q_mem, mem, w_mem_kv):
    B, S, _ = q_mem.shape
    M = mem.shape[1]
    mkv = mem @ w_mem_kv
    mk = mkv[..., :D_MEM].reshape(B, M, MEM_HEADS, MEM_HEAD_DIM)
    mv = mkv[..., D_MEM:].reshape(B, M, MEM_HEADS, MEM_HEAD_DIM)
    q = q_mem.reshape(B, S, MEM_HEADS, MEM_HEAD_DIM)
    logits = jnp.einsum('bshd,bmhd->bhsm', q, mk,
                        preferred_element_type=jnp.float32) * (MEM_HEAD_DIM ** -0.5)
    p = jax.nn.softmax(logits, axis=-1)
    return jnp.einsum('bhsm,bmhd->bshd', p.astype(mv.dtype), mv).reshape(B, S, D_MEM)

def mixer_sublayer(x, mem, w_in, w_mem_kv, w_out, main_fn):
    h = x @ w_in
    u_main = h[..., :D_MAIN]
    q_mem = h[..., D_MAIN:D_MIX]
    g_main = h[..., D_MIX:D_MIX + D_MAIN]
    g_mem = h[..., D_MIX + D_MAIN:]
    y_main = main_fn(u_main)
    y_mem = memory_attention(q_mem, mem, w_mem_kv)
    y = jnp.concatenate([y_main * jax.nn.silu(g_main), y_mem * jax.nn.silu(g_mem)], axis=-1)
    return y @ w_out

def second_inputs(seed: int = 0) -> dict:
    key = jax.random.key(seed)
    ks = jax.random.split(key, 12)
    x = jax.random.normal(ks[0], (BATCH, SEQ, D_MODEL), jnp.float32)
    mem = jax.random.normal(ks[1], (BATCH, N_MEM, D_MODEL), jnp.float32)
    w_in = jax.random.normal(ks[2], (DEPTH_2, D_MODEL, D_IN_2), jnp.float32) * D_MODEL ** -0.5
    w_mem_kv = jax.random.normal(ks[3], (DEPTH_2, D_MODEL, 2 * D_MEM), jnp.float32) * D_MODEL ** -0.5
    w_out = jax.random.normal(ks[4], (DEPTH_2, D_MIX, D_MODEL), jnp.float32) * (D_MIX ** -0.5 * BETA)
    ln_g = 1.0 + 0.02 * jax.random.normal(ks[5], (DEPTH_2, D_MODEL), jnp.float32)
    ln_b = 0.02 * jax.random.normal(ks[6], (DEPTH_2, D_MODEL), jnp.float32)
    pool_w = jax.random.normal(ks[7], (N_A, N_POOL_GROUPS, POOL_GROUP, POOL_GROUP), jnp.float32) * POOL_GROUP ** -0.5
    pool_scale = 1.0 + 0.1 * jax.random.normal(ks[8], (N_A, D_MAIN), jnp.float32)
    w_kv_shared = jax.random.normal(ks[9], (D_MODEL, 2 * D_MAIN + FOX_HEADS), jnp.float32) * D_MODEL ** -0.5
    b_forget = jax.random.uniform(ks[10], (FOX_HEADS,), jnp.float32, 1.0, 5.0)
    return {"x": x, "mem": mem, "w_in": w_in, "w_mem_kv": w_mem_kv, "w_out": w_out,
            "ln_g": ln_g, "ln_b": ln_b, "pool_w": pool_w, "pool_scale": pool_scale,
            "w_kv_shared": w_kv_shared, "b_forget": b_forget}

def second_block(x, mem, w_in, w_mem_kv, w_out, ln_g, ln_b, pool_w, pool_scale,
              w_kv_shared, b_forget):
    k_sh = v_sh = cum_sh = None
    for layer in range(DEPTH_2):
        if layer < N_A:
            main_fn = functools.partial(causal_multiscale_pool,
                                        pool_w=pool_w[layer], pool_scale=pool_scale[layer])
        else:
            if layer == N_A:
                k_sh, v_sh, cum_sh = shared_kv(x, w_kv_shared, b_forget)
            main_fn = functools.partial(forgetting_attention, k=k_sh, v=v_sh, cum=cum_sh)
        y = mixer_sublayer(x, mem, w_in[layer], w_mem_kv[layer], w_out[layer], main_fn)
        x = layer_norm(ALPHA * x + y, ln_g[layer], ln_b[layer])
    return x


def setup_inputs(seed=0):
    out = dict(first_inputs(seed))
    for name, value in second_inputs(seed + 1).items():
        if name != "x":
            out[name + "_2"] = value
    return out


def reference(
    x, c, ctx, c_ctx, ada_w, ada_b, norm1_g, norm2_g, w_in, b_gate, w_fourier, q_norm_g, w_qb,
    kv_norm_g, w_kvb, q_gain, k_gain, w_mla_o, w_out, w_up, w_down, mem_2, w_in_2, w_mem_kv_2,
    w_out_2, ln_g_2, ln_b_2, pool_w_2, pool_scale_2, w_kv_shared_2, b_forget_2,
):
    x = first_block(
        x, c, ctx, c_ctx, ada_w, ada_b, norm1_g, norm2_g, w_in, b_gate, w_fourier, q_norm_g,
        w_qb, kv_norm_g, w_kvb, q_gain, k_gain, w_mla_o, w_out, w_up, w_down,
    )
    return second_block(
        x, mem_2, w_in_2, w_mem_kv_2, w_out_2, ln_g_2, ln_b_2, pool_w_2, pool_scale_2,
        w_kv_shared_2, b_forget_2,
    )


_drawn_inputs = setup_inputs


def setup_inputs(seed=0):
    import zlib

    import numpy as np

    out = dict(_drawn_inputs(seed))
    spreads = {}
    factors = {'ctx': 8.0,
     'c_ctx': 6.529,
     'norm1_g': 7.826,
     'b_gate': 8.0,
     'q_norm_g': 8.0,
     'w_qb': 3.868,
     'kv_norm_g': 8.0,
     'q_gain': 8.0,
     'k_gain': 8.0,
     'mem_2': 3.037,
     'w_mem_kv_2': 2.868,
     'pool_scale_2': 3.3}
    for name, (base, spread) in spreads.items():
        noise = np.random.default_rng([zlib.crc32(name.encode()), seed]).standard_normal(out[name].shape)
        drawn = base * np.exp(spread * noise) if base else spread * noise
        out[name] = __import__('jax').numpy.asarray(drawn.astype(out[name].dtype))
    for name, factor in factors.items():
        out[name] = (out[name] * factor).astype(out[name].dtype)
    return out
```

```python
import math
from contextlib import ExitStack

import concourse.bass as bass
import numpy as np
from concourse import mybir

ALU = mybir.AluOpType
ACT = mybir.ActivationFunctionType
AXX = mybir.AxisListType.X
F = mybir.dt.float32
R = mybir.dt.float32r

P = 128
T = 1024
CTX = 256
KEYS = T + CTX
D = 1024
KT = D // P
HALF = 512
PW = 1024
NH, NOPE, ROPE, VD = 8, 64, 32, 64
QK = NOPE + ROPE
FW = 512
NG = 4
QL = 256
FF = 4 * D
FOX = 16
MH = 4
MIX = D + MH * P
MT = MIX // P
EPS, LN_EPS = 1e-6, 1e-5
ALPHA = 4 ** 0.25
LEAD = 4
SPLIT_LEAD = 2

COLS = {}
_n = 0
for _name, _w in (("c", 8), ("cc", 8), ("ada_b", 48), ("n1", 8), ("n2", 8), ("b_gate", 16), ("qng", 2),
                  ("kvng", 1), ("qg", 1), ("kg", 1), ("ln_g", 16), ("ln_b", 16), ("pscale", 8), ("bf", 1)):
    COLS[_name] = _n
    _n += _w
NCOLS = _n

PANELS = (("mem", 16), ("lat", 4), ("f", 4), ("gates", 32), ("v", 1), ("dft", 20), ("merge", 8), ("wout", 8),
          ("mlp", 64), ("pool", 20), ("mem1", 8), ("out1", 12), ("forget", 1), ("fox", 32), ("mem2", 8), ("out2", 12))
P0 = {}
_n = 0
for _name, _w in PANELS:
    P0[_name] = _n
    _n += _w
NP = _n
NPAN = dict(PANELS)

TILES = (("mem", 8), ("lat", 4), ("gates", 16), ("merge", 16), ("wout", 8), ("mlp", 64), ("pool", 24),
         ("mem1", 8), ("out1", 8), ("fox", 32), ("mem2", 8), ("out2", 8))
T0 = {}
_n = 0
for _name, _w in TILES:
    T0[_name] = _n
    _n += _w

SHUFFLE = [(i + 8) % 16 + 16 * (i // 16) for i in range(32)]


ORDER = ["mem", "lat", "f", "gates", "v", "dft", "mla", "merge", "wout", "mlp", "pool", "mem1", "out1", "forget", "fox", "mem2", "out2"]


def build(nc, d, out, upto=99, dbg=None):
    ctx = ExitStack()
    with ctx:
        def sb(name, shape, dt=F):
            return ctx.enter_context(nc.sbuf_tensor(name, shape, dt))

        raw = [sb(f"raw{i}", [P, PW]) for i in range(2)]
        whi = [sb(f"whi{i}", [P, PW], R) for i in range(2)]
        wlo = [sb(f"wlo{i}", [P, PW], R) for i in range(2)]
        ident, maskc, onesf = sb("ident", [P, P]), sb("maskc", [P, P]), sb("onesf", [P, P])
        cols = sb("cols", [P, NCOLS])
        modx, modc = sb("modx", [P, 48]), sb("modc", [P, 16])
        scx, scc, sc2 = sb("scx", [P, 8]), sb("scc", [P, 8]), sb("sc2", [P, 8])
        silc, sigc = sb("silc", [P, 16]), sb("sigc", [P, 16])
        stat = sb("stat", [P, 16])
        stat_pool = sb("stat_pool", [P, 16])
        poolc = sb("poolc", [P, 4, 16])
        rs, acc = sb("rs", [P, KEYS]), sb("acc", [P, KEYS])
        tmp = [sb(f"tmp{i}", [P, KEYS]) for i in range(2)]
        ZONE = 160 * 1024
        zone = sb("zone", [P, ZONE // 4])
        zbase = nc.sbuf_base - ZONE

        def at(name, kb, shape, dt=F):
            n = 4
            for s in shape[1:]:
                n *= s
            assert kb * 1024 + n <= ZONE, (name, kb, n)
            return nc.alloc_sbuf_tensor_at(name, shape, dt, offset=zbase + int(kb * 1024))

        Hhi, Hlo = at("Hhi", 0, [P, KT, T], R), at("Hlo", 32, [P, KT, T], R)
        Mhi, Mlo = at("Mhi", 0, [P, KT, CTX], R), at("Mlo", 8, [P, KT, CTX], R)
        Mraw = at("Mraw", 16, [P, KT, CTX])
        accx, accc = at("accx", 24, [P, 2048]), at("accc", 32, [P, 2048])
        mks = [at("mks_hi", 40, [P, MH, CTX], R), at("mks_lo", 44, [P, MH, CTX], R)]
        mvs = [at("mvs_hi", 48, [P, 2, HALF], R), at("mvs_lo", 52, [P, 2, HALF], R)]
        XT = at("XT", 64, [P, KT, T])
        CT = at("CT", 96, [P, KT, CTX])
        HChi, HClo = at("HChi", 104, [P, KT, CTX], R), at("HClo", 112, [P, KT, CTX], R)
        adas = [at(f"adas{i}", 122 + 8 * i, [P, KT, 256]) for i in range(2)]
        acc2 = at("acc2", 138, [P, 4096])
        ql, kvl, kr = at("ql", 64, [P, 2, T]), at("kvl", 72, [P, KEYS]), at("kr", 77, [P, KEYS])
        Fhi, Flo = at("Fhi", 90, [P, KT, FW], R), at("Flo", 106, [P, KT, FW], R)
        qnhi, qnlo = at("qnhi", 122, [P, 2, T], R), at("qnlo", 130, [P, 2, T], R)
        kvhi, kvlo = at("kvhi", 138, [P, KEYS], R), at("kvlo", 143, [P, KEYS], R)
        cosT, sinT = at("cosT", 148, [P, KEYS]), at("sinT", 153, [P, KEYS])
        gst = [at(f"gst{i}", 82 + 4 * i, [P, T]) for i in range(2)]
        phd = [at("prep_hi", 64, [P, KEYS], R), at("prep_lo", 69, [P, KEYS], R)]
        ABhi, ABlo = at("ABhi", 0, [P, NG, 2, HALF], R), at("ABlo", 16, [P, NG, 2, HALF], R)
        fms = [at("fms_hi", 32, [P, NG, HALF], R), at("fms_lo", 40, [P, NG, HALF], R)]
        Vhi, Vlo = at("Vhi", 48, [P, 10, FW], R), at("Vlo", 69, [P, 10, FW], R)
        Vp = [at("Vp_hi", 48, [P, 10, P], R), at("Vp_lo", 53, [P, 10, P], R)]
        Qp = [[at(f"Qp{j}{n}", 0 + 4 * (2 * j + n), [P, T], R) for n in range(2)] for j in range(2)]
        Kp = [[at(f"Kp{j}{n}", 16 + 5 * (2 * j + n), [P, KEYS], R) for n in range(2)] for j in range(2)]
        ats = [at("ats_hi", 36, [P, T], R), at("ats_lo", 40, [P, T], R)]
        E0 = [at(f"E0{i}", 90 + 5 * i, [P, KEYS]) for i in range(2)]
        PThi = [at(f"PThi{i}", 100 + 20 * i, [P, 10, 256], R) for i in range(2)]
        PTlo = [at(f"PTlo{i}", 110 + 20 * i, [P, 10, 256], R) for i in range(2)]
        Fm = [at("Fm_hi", 64, [P, NG, T], R), at("Fm_lo", 80, [P, NG, T], R)]
        At = [at("At_hi", 96, [P, NG, T], R), at("At_lo", 112, [P, NG, T], R)]
        sg = [[at(f"sg{i}{j}", 128 + 8 * i + 4 * j, [P, T]) for j in range(2)] for i in range(2)]
        mm1, mm2 = at("mm1", 144, [P, T]), at("mm2", 148, [P, T])
        Yhi, Ylo = at("Yhi", 0, [P, KT, T], R), at("Ylo", 32, [P, KT, T], R)
        X1 = at("X1", 64, [P, KT, T])
        Hb = [at("Hb_hi", 96, [P, KT, T], R), at("Hb_lo", 128, [P, KT, T], R)]
        Uhi, Ulo = at("Uhi", 0, [P, KT, T], R), at("Ulo", 32, [P, KT, T], R)
        pu = [at(f"pu{i}", 0 + 4.25 * i, [P, T + 16]) for i in range(2)]
        pa = [at(f"pa{i}", 8.5 + 4.25 * i, [P, T + 16]) for i in range(2)]
        PMhi, PMlo = at("PMhi", 17, [P, 2, T], R), at("PMlo", 25, [P, 2, T], R)
        sil = [at(f"sil{i}", 33 + 4 * i, [P, T]) for i in range(2)]
        sgm = at("sgm", 41, [P, T])
        yf = at("yf", 45, [P, T])
        ys = [[at(f"ys{i}{n}", 49 + 4 * (2 * i + n), [P, T], R) for n in range(2)] for i in range(2)]
        Qm = [at("Qm_hi", 0, [P, T], R), at("Qm_lo", 4, [P, T], R)]
        Km = [at("Km_hi", 8, [P, CTX], R), at("Km_lo", 9, [P, CTX], R)]
        Vm = [at("Vm_hi", 10, [P, 2, P], R), at("Vm_lo", 11, [P, 2, P], R)]
        Em = [at(f"Em{i}", 12 + i, [P, CTX]) for i in range(2)]
        PMThi = [at(f"PMThi{i}", 14 + 2 * i, [P, 2, 256], R) for i in range(2)]
        PMTlo = [at(f"PMTlo{i}", 18 + 2 * i, [P, 2, 256], R) for i in range(2)]
        Qf = [[at(f"Qf{j}{n}", 0 + 4 * (2 * j + n), [P, T], R) for n in range(2)] for j in range(2)]
        Kf = [[at(f"Kf{j}{n}", 16 + 4 * (2 * j + n), [P, T], R) for n in range(2)] for j in range(2)]
        yff = at("yff", 32, [P, T])
        ysf = [at("ysf_hi", 36, [P, T], R), at("ysf_lo", 40, [P, T], R)]
        Vf = [at("Vf_hi", 44, [P, KT, P], R), at("Vf_lo", 48, [P, KT, P], R)]
        PFThi = [at(f"PFThi{i}", 52 + 8 * i, [P, KT, 256], R) for i in range(2)]
        PFTlo = [at(f"PFTlo{i}", 68 + 8 * i, [P, KT, 256], R) for i in range(2)]
        vtf = at("vtf", 84, [P, T])
        ncum = at("ncum", 88, [P, T])
        nch = [at("nch_hi", 52, [P, T], R), at("nch_lo", 56, [P, T], R)]
        mch = [at("mch_hi", 60, [P, T], R), at("mch_lo", 64, [P, T], R)]
        Z = at("Z", 96, [P, KT, T])
        Yb = [at("Yb_hi", 0, [P, MT, T], R), at("Yb_lo", 48, [P, MT, T], R)]
        ps = ctx.enter_context(nc.psum_tensor("ps", [P, 8 * HALF], F))
        G = [ps[:, 0:1024], ps[:, 1024:2048]]

        def scratch(name, *shape):
            return nc.dram_tensor(name, shape, F, kind="Internal").ap()

        mk_d = scratch("mk_d", 2, 2, P, MH, CTX)
        mv_d = scratch("mv_d", 2, 2, P, 2, HALF)
        gate_d = scratch("gate_d", 16, P, T)
        q_d, k_d = scratch("q_d", NH, 2, QK, T), scratch("k_d", NH, 2, QK, KEYS)
        v_d = scratch("v_d", 2, 4, P, 10, P)
        fm_d, at_d = scratch("fm_d", 2, NG, P, T), scratch("at_d", 2, NG, P, T)
        y_d = [scratch(f"y_d{l}", MT, 2, P, T) for l in range(2)]
        cum_d = scratch("cum_d", FOX, 2, 2, T)

        sems = {}

        def S(name):
            if name not in sems:
                sems[name] = ctx.enter_context(nc.semaphore(name))
            return sems[name]

        g_free = [S("g_free0"), S("g_free1")]
        f32 = lambda ap: ap.bitcast(F)
        block = ctx.enter_context(nc.Block())
        SCALE = {"mla": QK ** -0.5, "fox": 1.0, "mem": P ** -0.5}

        class Att:

            def __init__(self, name, heads, rows, nkt, E, PT, scale, causal=False):
                self.name, self.heads, self.rows, self.nkt = name, heads, rows, nkt
                self.E, self.PT, self.scale, self.causal = E, PT, scale, causal
                self.U = 8 * len(heads)
                self.lag = 1 if name == "mla" else 2

                self.ub = {"mla": 0, "mem1": 64, "fox": 96, "mem2": 224}[name]

        mla = Att("mla", [(Qp[j], Kp[j], Vp, 64 * j) for j in range(2)], QK, [10] * 8, E0, (PThi, PTlo), SCALE["mla"])
        fox = Att("fox", [(Qf[j], Kf[j], Vf, 64 * j) for j in range(2)], 66, list(range(1, 9)), tmp, (PFThi, PFTlo),
                  SCALE["fox"], causal=True)
        mem = [Att(f"mem{l + 1}", [(Qm, Km, Vm, 0)], P, [2] * 8, Em, (PMThi, PMTlo), SCALE["mem"]) for l in range(2)]

        def mm3(o, wh, wl, xh, xl, start, stop):
            nc.tensor.matmul(o, wh, xh, start=start, stop=False)
            nc.tensor.matmul(o, wh, xl, start=False, stop=False)
            return nc.tensor.matmul(o, wl, xh, start=False, stop=stop)

        def att_pe(pe, a, i):
            U = a.U

            def scores(n):
                (Q, K, V, r0), qt = a.heads[n // 8], n % 8
                if n == 0:
                    a.qk(i)
                pe.wait_ge(S("att_exp"), a.ub + U * i + n)
                w = a.nkt[qt] * P
                for c in range(0, w, HALF):
                    e = min(c + HALF, w)
                    q = [x[0:a.rows, qt * P:qt * P + P] for x in Q]
                    k = [x[0:a.rows, c:e] for x in K]
                    last = mm3(ps[:, c:e], q[0], q[1], k[0], k[1], True, True)
                last.then_inc(S("att_scores"), 1)

            def flip(n):
                pe.wait_ge(S("att_prob"), a.ub + U * i + n + 1)
                pe.wait_ge(S("att_ptlo"), a.ub + U * i + n)
                for kt in range(a.nkt[n % 8]):
                    last = nc.tensor.transpose(ps[:, 3 * HALF + kt * P:3 * HALF + kt * P + P],
                                               a.E[n % 2][:, kt * P:kt * P + P], ident[:, :])
                last.then_inc(S("att_flip"), 1)

            def pv(g):
                (Q, K, V, r0), gg = a.heads[g // 4], g % 4
                pe.wait_ge(S("att_ptlo"), a.ub + U * i + 2 * g + 2)
                if g == 0:
                    a.v(i)
                if gg == 0:
                    pe.wait_ge(S("att_out"), a.ub // 8 + len(a.heads) * i + g // 4)
                o = ps[:, 6 * HALF + 256 * gg:6 * HALF + 256 * gg + 256]
                hi, lo = a.PT[0][g % 2], a.PT[1][g % 2]
                full, part = a.nkt[2 * gg], a.nkt[2 * gg + 1]
                nc.tensor.matmul(o, V[0][:, 0, :], hi[:, 0, :], start=True, stop=False)
                for kt in range(full, part):
                    mm3(o[:, P:256], V[0][:, kt, :], V[1][:, kt, :], hi[:, kt, P:256], lo[:, kt, P:256], False, False)
                for kt in range(1, full):
                    mm3(o, V[0][:, kt, :], V[1][:, kt, :], hi[:, kt, :], lo[:, kt, :], False, False)
                nc.tensor.matmul(o, V[0][:, 0, :], lo[:, 0, :], start=False, stop=False)
                nc.tensor.matmul(o, V[1][:, 0, :], hi[:, 0, :], start=False, stop=True).then_inc(S("att_pv"), 1)

            scores(0)
            for n in range(U):
                if n + 1 < U:
                    scores(n + 1)
                flip(n)
                if n % 2 == 0 and n >= 2:
                    pv(n // 2 - 1)
            pv(U // 2 - 1)

        def att_dve(dve, a, i, evict):
            U = a.U

            def maximum(n):
                qt = n % 8
                w = a.nkt[qt] * P
                dve.wait_ge(S("att_scores"), a.ub + U * i + n + 1)
                if a.causal:
                    dg = ps[:, qt * P:qt * P + P]
                    nc.vector.tensor_tensor(dg, dg, maskc[:, :], ALU.add).then_inc(S("att_masked"), 1)
                    dve.wait_ge(S("att_masked"), U * i + n + 1)
                nc.vector.reduce_max(stat[:, n % 2:n % 2 + 1], ps[:, 0:w], AXX).then_inc(S("att_max"), 1)
                dve.wait_ge(S("att_max"), a.ub + U * i + n + 1)
                nc.vector.tensor_scalar(stat[:, 2 + n % 2:3 + n % 2], stat[:, n % 2:n % 2 + 1], -a.scale, None,
                                        ALU.mult).then_inc(S("att_negmax"), 1)

            def low(n):
                g, c = n // 2, n % 2 * P
                k = a.nkt[n % 8]
                dve.wait_ge(S("att_pthi"), a.ub + U * i + n + 1)
                hi, lo = a.PT[0][g % 2][:, 0:k, c:c + P], a.PT[1][g % 2][:, 0:k, c:c + P]
                src = ps[:, 3 * HALF:3 * HALF + k * P].rearrange("p (k q) -> p k q", k=k)
                nc.vector.tensor_tensor(lo, src, f32(hi), ALU.subtract).then_inc(S("att_ptlo"), 1)

            maximum(0)
            for n in range(U):
                dve.wait_ge(S("att_exp"), a.ub + U * i + n + 1)
                nc.vector.reciprocal(stat[:, 6 + n % 2:7 + n % 2], stat[:, 4 + n % 2:5 + n % 2]).then_inc(S("att_rec"), 1)
                if n + 1 < U:
                    maximum(n + 1)
                if n >= 1:
                    low(n - 1)
                if n == 9 and U > 8:
                    evict(0, 0)
                if n == 9 + a.lag:
                    evict(0, 1)
            low(U - 1)
            evict(len(a.heads) - 1, 0)
            evict(len(a.heads) - 1, 1)

        def att_act(act, a, i, evict):
            U = a.U

            def exp(n):
                w = a.nkt[n % 8] * P
                act.wait_ge(S("att_negmax"), a.ub + U * i + n + 1)
                nc.scalar.activation(a.E[n % 2][:, 0:w], ps[:, 0:w], ACT.Exp, bias=stat[:, 2 + n % 2:3 + n % 2],
                                     scale=a.scale, accum_out=stat[:, 4 + n % 2:5 + n % 2]).then_inc(S("att_exp"), 1)

            def high(n):
                g, c = n // 2, n % 2 * P
                k = a.nkt[n % 8]
                act.wait_ge(S("att_flip"), a.ub + U * i + n + 1)
                src = ps[:, 3 * HALF:3 * HALF + k * P].rearrange("p (k q) -> p k q", k=k)
                if g >= 2 and n % 2 == 0:
                    act.wait_ge(S("att_pv"), a.ub // 2 + U // 2 * i + g - 1)
                nc.scalar.activation(a.PT[0][g % 2][:, 0:k, c:c + P], src, ACT.Copy).then_inc(S("att_pthi"), 1)

            exp(0)
            for n in range(U):
                w = a.nkt[n % 8] * P
                act.wait_ge(S("att_rec"), a.ub + U * i + n + 1)
                nc.scalar.activation(a.E[n % 2][:, 0:w], a.E[n % 2][:, 0:w], ACT.Copy,
                                     scale=stat[:, 6 + n % 2:7 + n % 2]).then_inc(S("att_prob"), 1)
                if n >= 1:
                    high(n - 1)
                if n + 1 < U:
                    exp(n + 1)
                if n == 8 + a.lag and U > 8:
                    evict(0)
            high(U - 1)
            evict(len(a.heads) - 1)

        def evicted(eng, stage, tiles, i, t):
            if isinstance(i, int):
                t, i = t + tiles * i, 0
            n = T0[stage] + t
            eng.wait_ge(g_free[n % 2], n // 2 + 1 + (tiles // 2) * i)

        def pair_of(stage, t):
            n = T0[stage] + t
            return G[n % 2], g_free[n % 2]

        def panels_done(eng, stage, per, i, j):
            eng.wait_ge(S("panel_done"), P0[stage] + per * i + j + 1)

        def whi_of(w, k):
            return w[:, k * HALF:(k + 1) * HALF]

        def pm_buf(g, t):
            return pa[1]

        def pool_count(g, t, s):
            return g * (g + 1) + t * (g + 1) + s + 1


        def on(stage):
            return ORDER.index(stage) <= upto

        def sp_program(sp):
            def load_panel(stage, per, i, j):
                if isinstance(i, int):
                    j, i = j + per * i, 0
                n = P0[stage] + LEAD + j
                q = n + per * i
                sp.wait_ge(S("split"), q - 1)
                sp.dma_start(raw[n % 2][:, :], d["w"][q]).then_inc(S(f"loaded{n % 2}"), 16)

            def ada_chunk(c, slot):
                sp.dma_start(adas[slot][:, :, :], d["ada"][c]).then_inc(S(f"ada_loaded{slot}"), 16)

            sp.dma_start(cols[:, :], d["cols"]).then_inc(S("cols_loaded"), 16)
            sp.dma_start(Mraw[:, :, :], d["mem"]).then_inc(S("memt_loaded"), 16)
            for q in range(2):
                sp.dma_start(raw[q][:, :], d["w"][q]).then_inc(S(f"loaded{q}"), 16)
            ada_chunk(0, 0)
            ada_chunk(1, 1)
            sp.dma_start(XT[:, :, :], d["x"]).then_inc(S("x_loaded"), 16)
            sp.dma_start(CT[:, :, :], d["ctx"]).then_inc(S("ctx_loaded"), 16)
            for name, t in (("ident", ident), ("mask", maskc)):
                sp.dma_start(t[:, :], d[name]).then_inc(S("consts"), 16)
            sp.dma_start(poolc[:, :, :], d["poolc"]).then_inc(S("consts"), 16)
            for q in range(2, LEAD):
                sp.wait_ge(S("split"), q - 1)
                sp.dma_start(raw[q % 2][:, :], d["w"][q]).then_inc(S(f"loaded{q % 2}"), 16)

            with sp.Fori(0, 2) as l:
                for j in range(4):
                    load_panel("mem", 8, l, j)
                    sp.wait_ge(S("ada_used"), 4 * l + j + 1)
                    ada_chunk(4 * l + j + 2, j % 2)
                for t in (2, 3):
                    evicted(sp, "mem", 4, l, t)
                for n in range(2):
                    sp.dma_start(mk_d[l, n], f32(mks[n][:, :, :])).then_inc(S("mk_stored"), 16)
                for j in range(4, 8):
                    load_panel("mem", 8, l, j)
                sp.wait_ge(S("mv_lo"), l + 1)
                for n in range(2):
                    sp.dma_start(mv_d[l, n], f32(mvs[n][:, :, :])).then_inc(S("mv_stored"), 16)
            c = 10
            for stage in ("lat", "f"):
                if on(stage):
                    for j in range(4):
                        load_panel(stage, 4, 0, j)
                        for _ in range(2):
                            if c < 24:
                                sp.wait_ge(S("ada_used"), c - 1)
                                ada_chunk(c, c % 2)
                                c += 1
            if on("gates"):
                sp.wait_ge(S("ada_cols"), 2)
                sp.dma_start(cosT[0:QK, :], d["cos"]).then_inc(S("rope_loaded"), 16)
                sp.dma_start(sinT[0:QK, :], d["sin"]).then_inc(S("rope_loaded"), 16)

                def store_unit(i, u):
                    sp.wait_ge(S("prep_lo"), 4 * i + u + 1)
                    dst = (q_d, k_d)[u % 2]
                    w = (T, KEYS)[u % 2]
                    for n in range(2):
                        sp.dma_start(dst[2 * i + u // 2, n], f32(phd[n][0:QK, 0:w])).then_inc(S("prep_stored"), 16)

                def store_gate(i, t):
                    evicted(sp, "gates", 4, i, t)
                    sp.dma_start(gate_d[4 * i + t], gst[t % 2][:, :]).then_inc(S(f"gate_stored{t % 2}"), 16)

                with sp.Fori(0, 4) as i:
                    for j in range(8):
                        load_panel("gates", 8, i, j)
                        if j == 2:
                            store_unit(i, 0)
                        if j == 3:
                            store_gate(i, 0)
                        if j == 5:
                            store_unit(i, 1)
                            store_gate(i, 1)
                        if j == 6:
                            store_unit(i, 2)
                        if j == 7:
                            store_gate(i, 2)
                    store_unit(i, 3)
                    store_gate(i, 3)
            if on("v"):
                load_panel("v", 1, 0, 0)
                sp.wait_ge(S("v_lo"), 10)
                for n, t in enumerate((Vhi, Vlo)):
                    for r in range(4):
                        sp.dma_start(v_d[n, r], f32(t[:, :, P * r:P * r + P])).then_inc(S("v_stored"), 16)
            if on("dft"):
                with sp.Fori(0, 2) as h:
                    for j in range(10):
                        load_panel("dft", 10, h, j)
                    sp.wait_ge(S("fm_lo"), 4 * h + 4)
                    for n in range(2):
                        sp.dma_start(fm_d[n].rearrange("g p f -> p g f")[:, :, bass.ds(h * HALF, HALF)],
                                     f32(fms[n][:, :, :])).then_inc(S("fm_stored"), 16)
            if on("mla"):
                sp.wait_ge(S("prep_stored"), 16 * 32)
                sp.wait_ge(S("v_stored"), 16 * 8)
                sp.wait_ge(S("fm_stored"), 16 * 4)
                with sp.Fori(0, 4) as i:
                    sp.wait_ge(S("att_pv"), 8 * i)
                    for j in range(2):
                        for n in range(2):
                            sp.dma_start(f32(Qp[j][n][0:QK, :]), q_d[2 * i + j, n]).then_inc(S("mla_loaded"), 16)
                            sp.dma_start(f32(Kp[j][n][0:QK, :]), k_d[2 * i + j, n]).then_inc(S("mla_loaded"), 16)
                    for n in range(2):
                        sp.dma_start(f32(Vp[n][:, :, :]), v_d[n, i]).then_inc(S("mla_loaded"), 16)
                    sp.wait_ge(S("att_out"), 2 * i + 2)
                    for n in range(2):
                        sp.dma_start(at_d[n, i], f32(ats[n][:, :])).then_inc(S("at_stored"), 16)
            if on("merge"):
                sp.wait_ge(S("att_pv"), 32)
                sp.wait_ge(S("at_stored"), 16 * 8)
                for n in range(2):
                    sp.dma_start(f32(Fm[n][:, :, :]), fm_d[n].rearrange("g p t -> p g t")).then_inc(S("fa_loaded"), 16)
                    sp.dma_start(f32(At[n][:, :, :]), at_d[n].rearrange("g p t -> p g t")).then_inc(S("fa_loaded"), 16)
                sp.wait_ge(S("gate_stored0"), 16 * 8)
                sp.wait_ge(S("gate_stored1"), 16 * 8)
                with sp.Fori(0, 4) as i:
                    for j in range(2):
                        for q in range(2):
                            sp.wait_ge(g_free[q], T0["merge"] // 2 + 2 * i + j - 1)
                        for n in range(2):
                            sp.dma_start(sg[j][n][:, :], gate_d[2 * i + j + 8 * n]).then_inc(S(f"sg_loaded{j}"), 16)
                        load_panel("merge", 2, i, j)
            if on("wout"):
                sp.wait_ge(S("panel_done"), P0["merge"] + 8)
                sp.dma_start(X1[:, :, :], d["x"]).then_inc(S("x_loaded"), 16)
                with sp.Fori(0, 4) as i:
                    for j in range(2):
                        load_panel("wout", 2, i, j)
            if on("mlp"):
                with sp.Fori(0, 4) as i:
                    for j in range(16):
                        load_panel("mlp", 16, i, j)

            def store_y(l, f, slot, sem):
                for n in range(2):
                    sp.dma_start(y_d[l][f, n], f32(slot[n][:, :])).then_inc(S(sem), 16)

            def mem_heads(l):
                a = mem[l]
                st = f"mem{l + 1}"
                sp.wait_ge(S("mk_stored"), 64)
                sp.wait_ge(S("mv_stored"), 64)
                if l == 0:
                    sp.wait_ge(S("pool_ylo"), 8)
                    sp.wait_ge(S("pool_stored0"), 16 * 8)
                    sp.wait_ge(S("pool_stored1"), 16 * 8)
                else:
                    sp.wait_ge(S("att_pv"), fox.ub // 2 + 64)
                    sp.wait_ge(S("fox_stored"), 16 * 16)
                with sp.Fori(0, MH) as i:
                    sp.wait_ge(S("att_pv"), a.ub // 2 + 4 * i)
                    for n in range(2):
                        sp.dma_start(f32(Km[n][:, :]), mk_d[l, n][:, i, :]).then_inc(S("mem_kv"), 16)
                        sp.dma_start(f32(Vm[n][:, :, :]), mv_d[l, n][:, :, bass.ds(i * P, P)]).then_inc(S("mem_kv"), 16)
                    for j in range(2):
                        load_panel(st, 2, i, j)
                    sp.wait_ge(S("mem_ylo"), 4 * l + i + 1)
                    for n in range(2):
                        sp.dma_start(y_d[l][8 + i, n], f32(ys[1][n][:, :])).then_inc(S("mem_stored"), 16)

            def out_proj(l):
                a = mem[l]
                st = f"out{l + 1}"
                sp.wait_ge(S("mem_stored"), 128 * (l + 1))
                sp.wait_ge(S("att_pv"), a.ub // 2 + 16)
                for n in range(2):
                    sp.dma_start(f32(Yb[n][:, :, :]), y_d[l][:, n].rearrange("f p t -> p f t")).then_inc(S("yb"), 16)
                with sp.Fori(0, 2) as i:
                    for j in range(6):
                        load_panel(st, 6, i, j)

            if on("pool"):
                for g in range(4):
                    for j in range(5):
                        load_panel("pool", 5, g, j)
                    for t in range(2):
                        sp.wait_ge(S("pool_ylo"), 2 * g + t + 1)
                        store_y(0, 2 * g + t, ys[t], f"pool_stored{t}")
            if on("mem1"):
                mem_heads(0)
            if on("out1"):
                out_proj(0)
            if on("forget"):
                load_panel("forget", 1, 0, 0)
                sp.wait_ge(S("cum"), 4)
                for s_, t in enumerate((nch, mch)):
                    for n in range(2):
                        sp.dma_start(cum_d[:, s_, n], f32(t[n][0:FOX, :])).then_inc(S("cum_stored"), 16)
                sp.wait_ge(S("cum_stored"), 64)
                sp.wait_ge(S("aug"), 8)
            if on("fox"):
                with sp.Fori(0, 8) as i:
                    sp.wait_ge(S("att_pv"), fox.ub // 2 + 8 * i)
                    for j in range(2):
                        for n in range(2):
                            sp.dma_start(f32(Kf[j][n][64:65, :]), cum_d[bass.ds(2 * i + j, 1), 0, n]).then_inc(S("fox_cum"), 16)
                            sp.dma_start(f32(Qf[j][n][65:66, :]), cum_d[bass.ds(2 * i + j, 1), 1, n]).then_inc(S("fox_cum"), 16)
                    for j in range(4):
                        load_panel("fox", 4, i, j)
                    sp.wait_ge(S("fox_ylo"), 2 * i + 2)
                    for n in range(2):
                        sp.dma_start(y_d[1][i, n], f32(ysf[n][:, :])).then_inc(S("fox_stored"), 16)
            if on("mem2"):
                mem_heads(1)
            if on("out2"):
                out_proj(1)
                with sp.Fori(0, 4) as i:
                    for j in range(2):
                        sp.wait_ge(S("ln2_out"), 2 * i + j + 1)
                        sp.dma_start(out[2 * i + j], tmp[j][:, 0:T]).then_inc(S(f"out_stored{j}"), 16)
                for j in range(2):
                    sp.wait_ge(S(f"out_stored{j}"), 64)
            if dbg is not None:
                dbg(sp, S, at)

        def pool_program(gp):
            def split(n, i=0, per=0, after=None):
                q = n + per * i
                b = n % 2
                gp.wait_ge(S(f"loaded{b}"), 16 * (n // 2 + 1 + (per // 2) * i))
                if n >= 2:
                    gp.wait_ge(S("panel_done"), q - 1)
                if after is not None:
                    gp.wait_ge(*after)
                nc.gpsimd.tensor_tensor(whi[b][:, :], raw[b][:, :], onesf[:, 0:1].to_broadcast([P, PW]), ALU.mult).then_inc(S("split_hi"), 1)
                gp.wait_ge(S("split_hi"), q + 1)
                nc.gpsimd.tensor_tensor(wlo[b][:, :], raw[b][:, :], f32(whi[b][:, :]), ALU.subtract).then_inc(S("split"), 1)

            def splits(stage, per, count, i=0, first=0, after=None):
                for j in range(first, first + count):
                    split(P0[stage] + SPLIT_LEAD + j, i, per, after if j == first else None)

            gp.wait_ge(S("ones"), 1)
            for n in range(SPLIT_LEAD):
                split(n)
            with gp.Fori(0, 2) as l:
                splits("mem", 8, 8, l)
            for stage in ("lat", "f"):
                if on(stage):
                    splits(stage, 0, 4)
            if on("gates"):
                gp.wait_ge(S("rope_loaded"), 32)

                def rope_unit(i, u):
                    w = (T, KEYS)[u % 2]
                    a, b = tmp[0], tmp[1]
                    r = slice(64, 96)
                    gp.wait_ge(S("split"), 8 * i + (P0["gates"] + SPLIT_LEAD + 2 * u))
                    gp.wait_ge(S("prep_swap"), 4 * i + u + 1)
                    nc.gpsimd.tensor_tensor(a[r, 0:w], a[r, 0:w], cosT[r, 0:w], ALU.mult).then_inc(S("prep_cos"), 1)
                    gp.wait_ge(S("prep_cos"), 4 * i + u + 1)
                    gp.wait_ge(S("prep_sin"), 4 * i + u + 1)
                    nc.gpsimd.tensor_tensor(a[r, 0:w], a[r, 0:w], b[r, 0:w], ALU.add).then_inc(S("prep_rot"), 1)

                with gp.Fori(0, 4) as i:
                    for u in range(4):
                        rope_unit(i, u)
                        splits("gates", 8, 2, i, 2 * u, after=(S("prep_rot"), 4 * i + u + 1))
            if on("v"):
                splits("v", 0, 1)
            if on("dft"):
                with gp.Fori(0, 2) as i:
                    splits("dft", 10, 10, i)
            for stage, per, n in (("merge", 2, 4), ("wout", 2, 4), ("mlp", 16, 4)):
                if on(stage):
                    with gp.Fori(0, n) as i:
                        splits(stage, per, per, i)
            if on("pool"):
                splits("pool", 0, 20)
            for stage, per, n in (("mem1", 2, 4), ("out1", 6, 2), ("forget", 1, 1), ("fox", 4, 8), ("mem2", 2, 4),
                                  ("out2", 6, 2)):
                if on(stage):
                    if n == 1:
                        splits(stage, 0, 1)
                    else:
                        with gp.Fori(0, n) as i:
                            splits(stage, per, per, i)

        def pe_program(pe):
            def panel(stage, per, i, j):
                if isinstance(i, int):
                    j, i = j + per * i, 0
                n = P0[stage] + j
                pe.wait_ge(S("split"), n + per * i + 1)
                return whi[n % 2], wlo[n % 2]

            def pair(stage, tiles, i, t):
                if isinstance(i, int):
                    t, i = t + tiles * i, 0
                n = T0[stage] + t
                pe.wait_ge(g_free[n % 2], n // 2 + (tiles // 2) * i)
                return G[n % 2]

            def done(last):
                last.then_inc(S("panel_done"), 1)

            def blocks(o, wh, wl, xh, xl, ks, first, last, k0=0, w=T, off=0, ready=None):
                for n, b in enumerate(ks):
                    c = off + P * b
                    if ready is not None:
                        ready(k0 + n)
                    for h in range(0, w, HALF):
                        e = min(h + HALF, w)
                        st, sp_ = first and n == 0, last and n == len(ks) - 1
                        ins = mm3(o[:, h:e], wh[:, c:c + P], wl[:, c:c + P], xh[:, k0 + n, h:e], xl[:, k0 + n, h:e], st, sp_)
                return ins

            def tile(stage, per, i, j, tiles, t, xh, xl, ready=None):
                wh, wl = panel(stage, per, i, j)
                o = pair(stage, tiles, i, t)
                done(blocks(o, wh, wl, xh, xl, range(KT), True, True, ready=ready))

            pe.wait_ge(S("memt_lo"), 1)
            with pe.Fori(0, 2) as l:
                for hd in range(MH):
                    wh, wl = panel("mem", 8, l, hd)
                    o = pair("mem", 4, l, hd)
                    done(blocks(o, wh, wl, Mhi, Mlo, range(KT), True, True, w=CTX))
                for n in range(4):
                    wh, wl = panel("mem", 8, l, 4 + n)
                    if n == 0:
                        pe.wait_ge(S("mv_lo"), l)
                    for tt in range(2):
                        for k in range(2):
                            kt = 2 * n + k
                            last = mm3(ps[:, (4 + tt) * HALF:(5 + tt) * HALF], Mhi[:, kt, tt * P:tt * P + P],
                                       Mlo[:, kt, tt * P:tt * P + P], whi_of(wh, k), whi_of(wl, k), kt == 0, kt == 7)
                    done(last)
            pe.wait_ge(S("ones"), 1)
            pe.wait_ge(S("ada_used"), 8)
            pe.wait_ge(S("ada_c"), 8)
            for n in range(16):
                nc.tensor.matmul(ps[:, 6 * HALF + n:6 * HALF + n + 1], accx[:, P * n:P * n + P], onesf[:, 0:1], start=True, stop=True)
            for n in range(16):
                last = nc.tensor.matmul(ps[:, 6 * HALF + 48 + n:6 * HALF + 49 + n], accc[:, P * n:P * n + P], onesf[:, 0:1], start=True, stop=True)
            last.then_inc(S("ada_cols"), 1)
            pe.wait_ge(S("mv_lo"), 2)
            pe.wait_ge(S("sq_acc"), 8)
            for h in range(2):
                nc.tensor.matmul(ps[:, (4 + h) * HALF:(5 + h) * HALF], onesf[:, :], acc[:, h * HALF:(h + 1) * HALF], start=True, stop=True)
            pe.wait_ge(S("sq_acc"), 16)
            nc.tensor.matmul(ps[:, 7 * HALF:7 * HALF + CTX], onesf[:, :], acc[:, T:KEYS], start=True, stop=True).then_inc(S("norm_sum"), 1)
            if on("lat"):
                for t in range(4):
                    if t < 2:
                        tile("lat", 4, 0, t, 4, t, Hhi, Hlo, ready=(lambda k: pe.wait_ge(S("ap_lo"), k + 1)) if t == 0 else None)
                    else:
                        wh, wl = panel("lat", 4, 0, t)
                        o = pair("lat", 4, 0, t)
                        blocks(o, wh, wl, Hhi, Hlo, range(KT), True, True)
                        pe.wait_ge(S("ap_lo"), 16)
                        o = ps[:, (2 + t) * HALF:(2 + t) * HALF + CTX]
                        done(blocks(o, wh, wl, HChi, HClo, range(KT), True, True, w=CTX))
            if on("f"):
                for n in range(4):
                    wh, wl = panel("f", 4, 0, n)
                    for tt in range(KT):
                        if n == 0:
                            if tt in (0, 2):
                                pe.wait_ge(g_free[tt // 2], (T0["lat"] + 4) // 2)
                            if tt == 4:
                                pe.wait_ge(S("lat_ctx"), 2)
                        for k in range(2):
                            kt = 2 * n + k
                            last = mm3(ps[:, tt * HALF:(tt + 1) * HALF], Hhi[:, kt, tt * P:tt * P + P], Hlo[:, kt, tt * P:tt * P + P],
                                       whi_of(wh, k), whi_of(wl, k), kt == 0, kt == 7)
                        if n == 3 and tt < 7:
                            last.then_inc(S("rows_full"), 1)
                    done(last)
                pe.wait_ge(S("f_lo"), 8)
                pe.wait_ge(S("ada_used"), 24)
                for n in range(32):
                    last = nc.tensor.matmul(ps[:, 6 * HALF + 16 + n:6 * HALF + 17 + n], acc2[:, P * n:P * n + P], onesf[:, 0:1], start=True, stop=True)
                last.then_inc(S("ada_cols"), 1)
                pe.wait_ge(S("lat_sq"), 1)
                for h in range(2):
                    last = nc.tensor.matmul(ps[:, (4 + h) * HALF:(5 + h) * HALF], onesf[:, :], acc[:, h * HALF:(h + 1) * HALF], start=True, stop=True)
                last.then_inc(S("norm_sum"), 1)
                pe.wait_ge(S("lat_kvsq"), 1)
                for h in range(0, KEYS, HALF):
                    e = min(h + HALF, KEYS)
                    last = nc.tensor.matmul(ps[:, h:e], onesf[:, :], tmp[1][:, h:e], start=True, stop=True)
                last.then_inc(S("norm_sum"), 1)
            if on("gates"):
                pe.wait_ge(S("norm_ms"), 4)
                with pe.Fori(0, 4) as i:
                    for hd in range(2):
                        for u in range(2):
                            n = 2 * hd + u
                            w = (T, KEYS)[u]
                            wh, wl = panel("gates", 8, i, 4 * hd + 2 * u)
                            if hd == 0 and u == 0:
                                pe.wait_ge(S("qn_lo"), 1)
                                pe.wait_ge(S("kvn_lo"), 1)
                            pe.wait_ge(S("prep_ms"), 4 * i + n)
                            for c in range(0, w, HALF):
                                e = min(c + HALF, w)
                                if u == 0:
                                    for k in range(2):
                                        last = mm3(ps[0:QK, 4 * HALF + c:4 * HALF + e], wh[:, QK * k:QK * k + QK], wl[:, QK * k:QK * k + QK],
                                                   qnhi[:, k, c:e], qnlo[:, k, c:e], k == 0, k == 1)
                                else:
                                    last = mm3(ps[:, 4 * HALF + c:4 * HALF + e], wh[:, 0:P], wl[:, 0:P], kvhi[:, c:e], kvlo[:, c:e], True, True)
                            done(last)
                            tile("gates", 8, i, 4 * hd + 2 * u + 1, 4, n, Hhi, Hlo)
                            pe.wait_ge(S("prep_sq"), 4 * i + n + 1)
                            for c in range(0, w, HALF):
                                e = min(c + HALF, w)
                                last = nc.tensor.matmul(ps[0:QK, 4 * HALF + c:4 * HALF + e], onesf[0:QK, 0:QK], acc[0:QK, c:e], start=True, stop=True)
                            last.then_inc(S("prep_ss"), 1)
            if on("v"):
                wh, wl = panel("v", 1, 0, 0)
                for tt in range(10):
                    if tt == 0:
                        for q in range(2):
                            pe.wait_ge(g_free[q], (T0["gates"] + 16) // 2)
                    if tt == 4:
                        pe.wait_ge(S("prep_ms"), 16)
                    if tt >= 8:
                        pe.wait_ge(S("v_lo"), tt - 7)
                    last = mm3(ps[:, (tt % 8) * HALF:(tt % 8 + 1) * HALF], kvhi[:, tt * P:tt * P + P], kvlo[:, tt * P:tt * P + P],
                               wh[:, 0:HALF], wl[:, 0:HALF], True, True)
                    if tt < 9:
                        last.then_inc(S("rows_full"), 1)
                done(last)
            if on("dft"):
                pe.wait_ge(S("v_lo"), 10)
                with pe.Fori(0, 2) as h:
                    for part in range(2):
                        for n in range(4):
                            wh, wl = panel("dft", 10, h, 4 * part + n)
                            if n == 0:
                                pe.wait_ge(S("fm_lo"), 4 * h)
                                pe.wait_ge(S("ab_lo"), 8 * h)
                            for g in range(NG):
                                for k in range(2):
                                    kt = 2 * n + k
                                    last = mm3(ps[:, (4 * part + g) * HALF:(4 * part + g + 1) * HALF], Fhi[:, kt, P * g:P * g + P],
                                               Flo[:, kt, P * g:P * g + P], whi_of(wh, k), whi_of(wl, k), kt == 0, kt == 7)
                            done(last)
                    for part in range(2):
                        wh, wl = panel("dft", 10, h, 8 + part)
                        for g in range(NG):
                            pe.wait_ge(S("ab_lo"), 8 * h + (4 if part == 0 else 5 + g))
                            last = mm3(ps[:, g * HALF:(g + 1) * HALF], wh[:, 0:P], wl[:, 0:P], ABhi[:, g, part, :], ABlo[:, g, part, :],
                                       part == 0, part == 1)
                        done(last)
            if on("mla"):
                pe.wait_ge(S("fm_lo"), 8)
                pe.wait_ge(S("consts"), 48)
                mla.qk = lambda i: pe.wait_ge(S("mla_loaded"), 160 * i + 160)
                mla.v = lambda i: None
                with pe.Fori(0, 4) as i:
                    att_pe(pe, mla, i)
            if on("merge"):
                pe.wait_ge(S("fa_loaded"), 64)
                pe.wait_ge(S("att_out"), 8)
                pe.wait_ge(S("att_ptlo"), 64)
                with pe.Fori(0, 4) as i:
                    for j in range(2):
                        wh, wl = panel("merge", 2, i, j)
                        for n, X in enumerate((Fm, At)):
                            o = pair("merge", 4, i, 2 * j + n)
                            last = blocks(o, wh, wl, X[0], X[1], range(4 * n, 4 * n + 4), True, True)
                        done(last)
            if on("wout"):
                with pe.Fori(0, 4) as i:
                    for j in range(2):
                        if j == 0:
                            pe.wait_ge(S("y_lo"), 8)
                        tile("wout", 2, i, j, 2, j, Yhi, Ylo)
                pe.wait_ge(S("n2_acc"), 8)
                for h in range(2):
                    last = nc.tensor.matmul(ps[:, (4 + h) * HALF:(5 + h) * HALF], onesf[:, :], acc[:, h * HALF:(h + 1) * HALF], start=True, stop=True)
                last.then_inc(S("norm_sum"), 1)
            if on("mlp"):
                with pe.Fori(0, 4) as i:
                    for t in range(8):
                        tile("mlp", 16, i, t, 16, t, Hb[0], Hb[1], ready=(lambda k: pe.wait_ge(S("ap_lo"), 16 + k + 1)) if t == 0 else None)
                    for t in range(8):
                        tile("mlp", 16, i, 8 + t, 16, 8 + t, Uhi, Ulo,
                             ready=(lambda k: pe.wait_ge(S("u_lo"), 8 * i + k + 1)) if t == 0 else None)
            if on("pool"):
                for g in range(4):
                    for t in range(4):
                        tile("pool", 5, g, t, 6, t, Hb[0], Hb[1], ready=(lambda k: pe.wait_ge(S("x2_lo"), k + 1)) if g == 0 and t == 0 else None)
                    wh, wl = panel("pool", 5, g, 4)
                    for t in range(2):
                        o = pair("pool", 6, g, 4 + t)
                        pe.wait_ge(S("pm_lo"), 2 * g + 2)
                        last = blocks(o, wh, wl, PMhi, PMlo, (2 * t, 2 * t + 1), True, True)
                    done(last)

            def mem_heads(l):
                a, st = mem[l], f"mem{l + 1}"
                a.qk = lambda i: pe.wait_ge(S("mem_kv"), 64 * i + 64 * (4 * l + 1))
                a.v = lambda i: None
                with pe.Fori(0, MH) as i:
                    for j in range(2):
                        tile(st, 2, i, j, 2, j, Hb[0], Hb[1])
                    pe.wait_ge(g_free[1], T0[st] // 2 + i + 1)
                    pe.wait_ge(g_free[0], T0[st] // 2 + i + 1)
                    att_pe(pe, a, i)
                pe.wait_ge(S("att_ptlo"), a.ub + 32)
                pe.wait_ge(S("att_out"), a.ub // 8 + 4)

            def out_proj(l):
                st = f"out{l + 1}"
                with pe.Fori(0, 2) as i:
                    pe.wait_ge(S("yb"), 32 * (l + 1))
                    have = -1
                    for t in range(4):
                        o = pair(st, 4, i, t)
                        b = 12 * t
                        while b < 12 * t + 12:
                            j = b // 8
                            if j != have:
                                wh, wl = panel(st, 6, i, j)
                                have = j
                            e = min(8 * j + 8, 12 * t + 12)
                            last = blocks(o, wh, wl, Yb[0], Yb[1], range(b - 8 * j, e - 8 * j), b == 12 * t, e == 12 * t + 12, k0=b - 12 * t)
                            if e == 8 * j + 8:
                                done(last)
                            else:
                                last.then_inc(S("out_mid"), 1)
                            b = e
                for n, what in enumerate(("ln_acc", "ln_vacc")):
                    pe.wait_ge(S(what), 8 * (l + 1))
                    for h in range(2):
                        last = nc.tensor.matmul(ps[:, (4 + h) * HALF:(5 + h) * HALF], onesf[:, :], acc[:, h * HALF:(h + 1) * HALF], start=True, stop=True)
                    last.then_inc(S("norm_sum"), 1)

            if on("mem1"):
                mem_heads(0)
            if on("out1"):
                out_proj(0)
            if on("forget"):
                wh, wl = panel("forget", 1, 0, 0)
                pe.wait_ge(S("norm_ms"), 6)
                done(blocks(ps[:, 4 * HALF:6 * HALF], wh, wl, Hb[0], Hb[1], range(KT), True, True,
                            ready=lambda k: pe.wait_ge(S("ap_lo"), 24 + k + 1)))
            if on("fox"):
                fox.qk = lambda i: pe.wait_ge(S("fox_cum"), 128 * i + 128)
                fox.v = lambda i: pe.wait_ge(S("fox_vlo"), i + 1)
                pe.wait_ge(S("logits_read"), 1)
                pe.wait_ge(S("aug"), 8)
                with pe.Fori(0, 8) as i:
                    pe.wait_ge(S("att_ptlo"), fox.ub + 16 * i)
                    for j in range(4):
                        tile("fox", 4, i, j, 4, j, Hb[0], Hb[1])
                        if j == 2:
                            evicted(pe, "fox", 4, i, 1)
                            for k in range(KT):
                                last = nc.tensor.transpose(ps[:, 4 * HALF + P * k:4 * HALF + P * k + P], vtf[:, P * k:P * k + P], ident[:, :])
                            last.then_inc(S("fox_vflip"), 1)
                    pe.wait_ge(g_free[0], T0["fox"] // 2 + 2 * i + 2)
                    pe.wait_ge(g_free[1], T0["fox"] // 2 + 2 * i + 2)
                    pe.wait_ge(S("fox_vlo"), i + 1)
                    att_pe(pe, fox, i)
                pe.wait_ge(S("att_ptlo"), fox.ub + 128)
                pe.wait_ge(S("att_out"), fox.ub // 8 + 16)
            if on("mem2"):
                mem_heads(1)
            if on("out2"):
                out_proj(1)

        def col(name, k=0):
            return cols[:, COLS[name] + k:COLS[name] + k + 1]

        NORM = {"n1": 0, "n1c": 1, "latq": 2, "latkv": 3, "n2": 4, "ln0": 5, "ln1": 6}
        APPLY = {"n1": 0, "n1c": 8, "n2": 16, "ln0": 24, "ln1": 32}

        def apply_dve(dve, s, n, src, w, lo, hi=None, c0=0):
            def scaled(k):
                if k >= 2:
                    dve.wait_ge(S("ap_lo"), APPLY[s] + k - 1)
                nc.vector.tensor_tensor(tmp[k % 2][:, c0:c0 + w], src(k), rs[:, c0:c0 + w], ALU.mult).then_inc(S("ap_t"), 1)

            def low(k):
                dve.wait_ge(S("ap_hi"), APPLY[s] + k + 1)
                nc.vector.tensor_tensor(lo(k), tmp[k % 2][:, c0:c0 + w], f32(hi(k)), ALU.subtract).then_inc(S("ap_lo"), 1)

            for k in range(n):
                scaled(k)
                if k >= 1:
                    low(k - 1)
            low(n - 1)

        def apply_act(act, s, n, w, hi, scale, shift, c0=0):
            for k in range(n):
                b = tmp[k % 2][:, c0:c0 + w]
                act.wait_ge(S("ap_t"), APPLY[s] + k + 1)
                nc.scalar.activation(b, b, ACT.Identity, scale=scale(k), bias=shift(k)).then_inc(S("ap_full"), 1)
                act.wait_ge(S("ap_full"), APPLY[s] + k + 1)
                nc.scalar.activation(hi(k), b, ACT.Copy).then_inc(S("ap_hi"), 1)

        def root(act, s, rows, a, b):
            act.wait_ge(S("norm_ms"), NORM[s] + 1)
            nc.scalar.activation(rs[0:rows, a:b], rs[0:rows, a:b], ACT.Sqrt).then_inc(S("norm_root"), 1)

        def mean_square(dve, s, src, count, eps, rows, a, b):
            nc.vector.tensor_scalar(rs[0:rows, a:b], src, 1.0 / count, eps, ALU.mult, ALU.add).then_inc(S("norm_ms"), 1)
            dve.wait_ge(S("norm_root"), NORM[s] + 1)
            nc.vector.reciprocal(rs[0:rows, a:b], rs[0:rows, a:b]).then_inc(S("norm_rs"), 1)
            dve.wait_ge(S("norm_rs"), NORM[s] + 1)

        def act_program(act):
            def copy(dst, src, sem, func=ACT.Copy, **kw):
                nc.scalar.activation(dst, src, func, **kw).then_inc(sem, 1)

            act.wait_ge(S("memt_loaded"), 16)
            copy(Mhi[:, :, :], Mraw[:, :, :], S("memt_hi"))
            act.wait_ge(S("cols_loaded"), 16)
            copy(sigc[:, :], cols[:, 0:16], S("sigc"), ACT.Sigmoid)
            act.wait_ge(S("x_loaded"), 16)
            for k in range(KT):
                if k >= 2:
                    act.wait_ge(S("sq_acc"), k - 1)
                copy(tmp[k % 2][:, 0:T], XT[:, k, :], S("sq"), ACT.Square)
            act.wait_ge(S("ctx_loaded"), 16)
            for k in range(KT):
                if k >= 2:
                    act.wait_ge(S("sq_acc"), 8 + k - 1)
                copy(tmp[k % 2][:, T:KEYS], CT[:, k, :], S("sq"), ACT.Square)
            with act.Fori(0, 2) as l:
                act.wait_ge(S("mk_stored"), 32 * l)
                for hd in range(MH):
                    panels_done(act, "mem", 8, l, hd)
                    copy(mks[0][:, hd, :], pair_of("mem", hd)[0][:, 0:CTX], S("mk_hi"))
                panels_done(act, "mem", 8, l, 7)
                act.wait_ge(S("mv_stored"), 32 * l)
                copy(mvs[0][:, :, :], ps[:, 4 * HALF:6 * HALF].rearrange("p (a b) -> p a b", a=2), S("mv_hi"))
            root(act, "n1", P, 0, T)
            root(act, "n1c", P, T, KEYS)
            act.wait_ge(S("mods"), 4)
            act.wait_ge(S("mk_stored"), 64)
            act.wait_ge(S("mv_stored"), 64)
            apply_act(act, "n1", KT, T, lambda k: Hhi[:, k, :], lambda k: scx[:, k:k + 1], lambda k: modx[:, k:k + 1])
            apply_act(act, "n1c", KT, CTX, lambda k: HChi[:, k, :], lambda k: scc[:, k:k + 1], lambda k: modc[:, k:k + 1], c0=T)
            if on("lat"):
                for t in range(4):
                    panels_done(act, "lat", 4, 0, t)
                    g, free = pair_of("lat", t)
                    if t < 2:
                        copy(ql[:, t, :], g, free)
                    else:
                        r, dst = ((slice(0, P), kvl), (slice(64, QK), kr))[t - 2]
                        copy(dst[r, 0:T], g[r, :], free)
                        copy(dst[r, T:KEYS], ps[r, (2 + t) * HALF:(2 + t) * HALF + CTX], S("lat_ctx"))
            if on("f"):
                for tt in range(KT):
                    if tt < 7:
                        act.wait_ge(S("rows_full"), tt + 1)
                    else:
                        panels_done(act, "f", 4, 0, 3)
                    copy(Fhi[:, tt, :], ps[:, tt * HALF:(tt + 1) * HALF], S("f_hi"))
                evicted(act, "lat", 4, 0, 0)
                evicted(act, "lat", 4, 0, 1)
                act.wait_ge(S("ap_lo"), 16)
                for k in range(2):
                    copy(tmp[k][:, 0:T], ql[:, k, :], S("lat_s"), ACT.Square)
                evicted(act, "lat", 4, 0, 2)
                act.wait_ge(S("lat_ctx"), 2)
                act.wait_ge(S("lat_sq"), 1)
                copy(tmp[1][:, :], kvl[:, :], S("lat_kvsq"), ACT.Square)
                root(act, "latq", P, 0, T)
                for k in range(2):
                    act.wait_ge(S("lat_t"), k + 1)
                    copy(ql[:, k, :], ql[:, k, :], S("lat_full"), scale=col("qng", k))
                    act.wait_ge(S("lat_full"), k + 1)
                    copy(qnhi[:, k, :], ql[:, k, :], S("lat_hi"))
                root(act, "latkv", P, 0, KEYS)
                act.wait_ge(S("lat_t"), 3)
                copy(kvl[:, :], kvl[:, :], S("lat_full"), scale=col("kvng"))
                act.wait_ge(S("lat_full"), 3)
                copy(kvhi[:, :], kvl[:, :], S("lat_hi"))
            if on("gates"):
                evicted(act, "lat", 4, 0, 3)
                with act.Fori(0, 4) as i:
                    for u in range(4):
                        w = (T, KEYS)[u % 2]
                        panels_done(act, "gates", 8, i, 2 * u)
                        act.wait_ge(S("prep_lo"), 4 * i + u)
                        raw_ = ps[:, 4 * HALF:4 * HALF + w]
                        if u % 2 == 0:
                            copy(tmp[0][0:QK, 0:w], raw_[0:QK, :], S("prep_a"), scale=cols[0:QK, COLS["qg"]:COLS["qg"] + 1])
                            copy(acc[0:QK, 0:w], raw_[0:QK, :], S("prep_sq"), ACT.Square)
                        else:
                            lo_, up = slice(0, NOPE), slice(NOPE, QK)
                            kg = COLS["kg"]
                            copy(tmp[0][lo_, 0:w], raw_[lo_, :], S("prep_x"), scale=cols[lo_, kg:kg + 1])
                            copy(tmp[0][up, 0:w], kr[up, :], S("prep_a"), scale=cols[up, kg:kg + 1])
                            copy(acc[up, 0:w], kr[up, :], S("prep_x"), ACT.Square)
                            copy(acc[lo_, 0:w], raw_[lo_, :], S("prep_sq"), ACT.Square)
                        panels_done(act, "gates", 8, i, 2 * u + 1)
                        g, free = pair_of("gates", u)
                        act.wait_ge(S(f"gate_stored{u % 2}"), 32 * i + 16 * (u // 2))
                        copy(gst[u % 2][:, :], g, free, ACT.Sigmoid, bias=cols[:, bass.ds(4 * i + (COLS["b_gate"] + u), 1)])
                        act.wait_ge(S("prep_ms"), 4 * i + u + 1)
                        copy(rs[0:QK, 0:w], rs[0:QK, 0:w], S("prep_root"), ACT.Sqrt)
                        act.wait_ge(S("prep_full"), 4 * i + u + 1)
                        act.wait_ge(S("prep_stored"), 128 * i + 32 * u)
                        copy(phd[0][0:QK, 0:w], tmp[0][0:QK, 0:w], S("prep_hi"))
            if on("v"):
                act.wait_ge(S("prep_stored"), 512)
                for n in range(2):
                    act.wait_ge(S(f"gate_stored{n}"), 128)
                for tt in range(10):
                    if tt < 9:
                        act.wait_ge(S("rows_full"), 7 + tt + 1)
                    else:
                        panels_done(act, "v", 1, 0, 0)
                    copy(Vhi[:, tt, :], ps[:, (tt % 8) * HALF:(tt % 8 + 1) * HALF], S("v_hi"))
            if on("dft"):
                with act.Fori(0, 2) as h:
                    for part in range(2):
                        panels_done(act, "dft", 10, h, 4 * part + 3)
                        for g in range(NG):
                            copy(ABhi[:, g, part, :], ps[:, (4 * part + g) * HALF:(4 * part + g + 1) * HALF], S("ab_hi"))
                    panels_done(act, "dft", 10, h, 9)
                    act.wait_ge(S("fm_stored"), 32 * h)
                    for g in range(NG):
                        copy(fms[0][:, g, :], ps[:, g * HALF:(g + 1) * HALF], S("fm_hi"))
            if on("mla"):
                with act.Fori(0, 4) as i:
                    def evict(j):
                        r = slice(64 * j, 64 * j + 64)
                        act.wait_ge(S("att_pv"), 8 * i + 4 * j + 4)
                        if j == 0:
                            act.wait_ge(S("at_stored"), 32 * i)
                        copy(ats[0][r, :], ps[r, 6 * HALF:8 * HALF], S("mla_ohi"))
                    att_act(act, mla, i, evict)
            if on("merge"):
                act.wait_ge(S("att_pv"), 32)
                with act.Fori(0, 4) as i:
                    for j in range(2):
                        act.wait_ge(S("y_full"), 2 * i + j + 1)
                        copy(Yhi[:, 2 * i + j, :], mm1[:, :], S("y_hi"))
            if on("wout"):
                with act.Fori(0, 4) as i:
                    for j in range(2):
                        evicted(act, "wout", 2, i, j)
                        copy(tmp[j][:, 0:T], X1[:, 2 * i + j, :], S("n2_sq"), ACT.Square)
                root(act, "n2", P, 0, T)
                act.wait_ge(S("mods"), 6)
                apply_act(act, "n2", KT, T, lambda k: Hb[0][:, k, :], lambda k: sc2[:, k:k + 1], lambda k: modx[:, 24 + k:25 + k])
            if on("mlp"):
                with act.Fori(0, 4) as i:
                    for t in range(8):
                        panels_done(act, "mlp", 16, i, t)
                        g, free = pair_of("mlp", t)
                        if t >= 2:
                            act.wait_ge(S("u_lo"), 8 * i + t - 1)
                        copy(tmp[t % 2][:, 0:T], g, free, ACT.Relu)
                        act.wait_ge(S("u_sq"), 8 * i + t + 1)
                        copy(Uhi[:, t, :], tmp[t % 2][:, 0:T], S("u_hi"))
                panels_done(act, "mlp", 64, 0, 63)
                for k in range(KT):
                    evicted(act, "mlp", 16, 3, 8 + k)
                    copy(Hb[0][:, k, :], X1[:, k, :], S("x2_hi"))
            if on("pool"):
                for g4 in range(4):
                    for t in range(2):
                        panels_done(act, "pool", 5, g4, t)
                        g, free = pair_of("pool", t)
                        act.wait_ge(S("pm_lo"), 2 * g4)
                        copy(pu[t][:, 16:], g, free)
                    for t in range(2):
                        panels_done(act, "pool", 5, g4, 2 + t)
                        g, free = pair_of("pool", 2 + t)
                        if t == 1:
                            evicted(act, "pool", 6, g4, 2)
                        copy(sgm[:, :], g, S("pool_sig"), ACT.Sigmoid)
                        act.wait_ge(S("pm_full"), 2 * g4 + t + 1)
                        copy(PMhi[:, t, :], pm_buf(g4, t)[:, 16:], S("pm_hi"))
                    for t in range(2):
                        evicted(act, "pool", 6, g4, 4 + t)
                        act.wait_ge(S(f"pool_stored{t}"), 32 * g4)
                        copy(ys[t][0][:, :], yf[:, :], S("pool_yhi"))

            def mem_heads(l):
                a, st = mem[l], f"mem{l + 1}"
                if l == 1:
                    act.wait_ge(S("fox_stored"), 256)
                with act.Fori(0, MH) as i:
                    panels_done(act, st, 2, i, 0)
                    g, free = pair_of(st, 0)
                    if l == 0:
                        act.wait_ge(S("pool_stored1"), 128)
                    copy(Qm[0][:, :], g, S("mem_qhi"))
                    panels_done(act, st, 2, i, 1)
                    g, free = pair_of(st, 1)
                    copy(sgm[:, :], g, S("mem_sig"), ACT.Sigmoid)

                    def evict(j):
                        act.wait_ge(S("att_out"), a.ub // 8 + i + 1)
                        act.wait_ge(S("mem_stored"), 32 * i + 128 * l)
                        copy(ys[1][0][:, :], yf[:, :], S("mem_yhi"))
                    att_act(act, a, i, evict)

            def out_proj(l):
                act.wait_ge(S("ln_acc"), 8 * (l + 1))
                for k in range(KT):
                    act.wait_ge(S("ln_zc"), 8 * l + k + 1)
                    if k >= 2:
                        act.wait_ge(S("ln_vacc"), 8 * l + k - 1)
                    copy(tmp[k % 2][:, 0:T], Z[:, k, :], S("ln_sq"), ACT.Square)
                root(act, f"ln{l}", P, 0, T)
                gcol, bcol = (lambda k: col("ln_g", 8 * l + k)), (lambda k: col("ln_b", 8 * l + k))
                if l == 0:
                    apply_act(act, "ln0", KT, T, lambda k: Hb[0][:, k, :], gcol, bcol)
                else:
                    for k in range(KT):
                        b = tmp[k % 2][:, 0:T]
                        act.wait_ge(S("ap_t"), APPLY["ln1"] + k + 1)
                        copy(b, b, S("ln2_out"), ACT.Identity, scale=gcol(k), bias=bcol(k))

            if on("mem1"):
                mem_heads(0)
            if on("out1"):
                out_proj(0)
            if on("forget"):
                r = slice(0, FOX)
                act.wait_ge(S("logits_read"), 1)
                copy(tmp[1][r, 0:T], tmp[0][r, 0:T], S("fg"), ACT.Abs)
                act.wait_ge(S("fg"), 1)
                copy(tmp[1][r, 0:T], tmp[1][r, 0:T], S("fg"), ACT.Exp, scale=-1.0)
                act.wait_ge(S("fg"), 2)
                copy(tmp[1][r, 0:T], tmp[1][r, 0:T], S("fg"), ACT.Ln, bias=1.0)
                act.wait_ge(S("cum"), 1)
                copy(nch[0][r, :], ncum[r, :], S("fg"))
            if on("fox"):
                act.wait_ge(S("cum_stored"), 64)
                with act.Fori(0, 8) as i:
                    for t in range(4):
                        panels_done(act, "fox", 4, i, t)
                        g, free = pair_of("fox", t)
                        if t == 0:
                            for j in range(2):
                                copy(Kf[j][0][0:64, :], g[64 * j:64 * j + 64, :], S("fox_hi"))
                        if t == 1:
                            copy(vtf[:, :], g, free)
                        if t == 2:
                            for j in range(2):
                                copy(Qf[j][0][0:64, :], g[64 * j:64 * j + 64, :], S("fox_hi"), scale=64 ** -0.5)
                            act.wait_ge(S("fox_vflip"), i + 1)
                            copy(Vf[0][:, :, :], ps[:, 4 * HALF:6 * HALF].rearrange("p (k d) -> p k d", d=P), S("fox_vhi"))
                        if t == 3:
                            copy(rs[:, 0:T], g, S("fox_sig"), ACT.Sigmoid)

                    def evict(j):
                        r = slice(64 * j, 64 * j + 64)
                        act.wait_ge(S("att_out"), fox.ub // 8 + 2 * i + j + 1)
                        if j == 0:
                            act.wait_ge(S("fox_stored"), 32 * i)
                        copy(ysf[0][r, :], yff[r, :], S("fox_yhi"))
                    att_act(act, fox, i, evict)
            if on("mem2"):
                mem_heads(1)
            if on("out2"):
                out_proj(1)

        def dve_program(dve):
            def sub(lo, x, hi, sem):
                nc.vector.tensor_tensor(lo, x, f32(hi), ALU.subtract).then_inc(sem, 1)

            def tt(o, a, b, op, sem):
                nc.vector.tensor_tensor(o, a, b, op).then_inc(sem, 1)

            nc.vector.memset(onesf[:, :], 1.0).then_inc(S("ones"), 1)
            dve.wait_ge(S("memt_hi"), 1)
            sub(Mlo[:, :, :], Mraw[:, :, :], Mhi[:, :, :], S("memt_lo"))
            dve.wait_ge(S("sigc"), 1)
            tt(silc[:, :], cols[:, 0:16], sigc[:, :], ALU.mult, S("silc"))
            dve.wait_ge(S("silc"), 1)

            def ada(c, dst, sil0, sem, wait_self):
                for k in range(KT):
                    o = dst
                    w_ = adas[c % 2][:, k, :]
                    s_ = silc[:, sil0 + k:sil0 + k + 1]
                    if k == 0:
                        ins = nc.vector.tensor_scalar(o, w_, s_, None, ALU.mult)
                    else:
                        dve.wait_ge(S("ada_link"), wait_self(k))
                        ins = nc.vector.scalar_tensor_tensor(o, w_, s_, o, ALU.mult, ALU.add)
                    ins.then_inc(S("ada_link") if k < KT - 1 else S(sem), 1)

            dve.wait_ge(S("x_loaded"), 16)
            for k in range(KT):
                dve.wait_ge(S("sq"), k + 1)
                if k == 0:
                    nc.vector.tensor_copy(acc[:, 0:T], tmp[0][:, 0:T]).then_inc(S("sq_acc"), 1)
                else:
                    dve.wait_ge(S("sq_acc"), k)
                    tt(acc[:, 0:T], acc[:, 0:T], tmp[k % 2][:, 0:T], ALU.add, S("sq_acc"))
            for k in range(KT):
                dve.wait_ge(S("sq"), 8 + k + 1)
                if k == 0:
                    nc.vector.tensor_copy(acc[:, T:KEYS], tmp[0][:, T:KEYS]).then_inc(S("sq_acc"), 1)
                else:
                    dve.wait_ge(S("sq_acc"), 8 + k)
                    tt(acc[:, T:KEYS], acc[:, T:KEYS], tmp[k % 2][:, T:KEYS], ALU.add, S("sq_acc"))
            with dve.Fori(0, 2) as l:
                for hd in range(MH):
                    dve.wait_ge(S(f"ada_loaded{hd % 2}"), 32 * l + 16 * (hd // 2 + 1))
                    c = 4 * l + hd
                    ada(hd, accc[:, bass.ds(256 * c, 256)], 8, "ada_c", lambda k: 14 * (4 * l + hd) + k)
                    ada(hd, accx[:, bass.ds(256 * c, 256)], 0, "ada_used", lambda k: 14 * (4 * l + hd) + 7 + k)
                    dve.wait_ge(S("mk_hi"), 4 * l + hd + 1)
                    g, free = pair_of("mem", hd)
                    sub(mks[1][:, hd, :], g[:, 0:CTX], mks[0][:, hd, :], free)
                dve.wait_ge(S("mv_hi"), l + 1)
                sub(mvs[1][:, :, :], ps[:, 4 * HALF:6 * HALF].rearrange("p (a b) -> p a b", a=2), mvs[0][:, :, :], S("mv_lo"))
            dve.wait_ge(S("ada_cols"), 1)
            m6 = 6 * HALF
            ab = COLS["ada_b"]
            tt(modx[:, 0:16], ps[:, m6:m6 + 16], cols[:, ab:ab + 16], ALU.add, S("mods"))
            tt(modc[:, 0:16], ps[:, m6 + 48:m6 + 64], cols[:, ab:ab + 16], ALU.add, S("mods"))
            dve.wait_ge(S("mods"), 2)
            n1 = cols[:, COLS["n1"]:COLS["n1"] + 8]
            nc.vector.scalar_tensor_tensor(scx[:, :], modx[:, 8:16], 1.0, n1, ALU.add, ALU.mult).then_inc(S("mods"), 1)
            nc.vector.scalar_tensor_tensor(scc[:, :], modc[:, 8:16], 1.0, n1, ALU.add, ALU.mult).then_inc(S("mods"), 1)
            dve.wait_ge(S("norm_sum"), 1)
            mean_square(dve, "n1", ps[:, 4 * HALF:6 * HALF], D, EPS, P, 0, T)
            mean_square(dve, "n1c", ps[:, 7 * HALF:7 * HALF + CTX], D, EPS, P, T, KEYS)
            apply_dve(dve, "n1", KT, lambda k: XT[:, k, :], T, lambda k: Hlo[:, k, :], lambda k: Hhi[:, k, :])
            apply_dve(dve, "n1c", KT, lambda k: CT[:, k, :], CTX, lambda k: HClo[:, k, :], lambda k: HChi[:, k, :], c0=T)
            if on("f"):
                for c in range(8, 24):
                    dve.wait_ge(S(f"ada_loaded{c % 2}"), 16 * (c // 2 + 1))
                    ada(c, acc2[:, 256 * (c - 8):256 * (c - 7)], 0, "ada_used", lambda k: 112 + 7 * (c - 8) + k)
                for tt_ in range(KT):
                    dve.wait_ge(S("f_hi"), tt_ + 1)
                    sub(Flo[:, tt_, :], ps[:, tt_ * HALF:(tt_ + 1) * HALF], Fhi[:, tt_, :], S("f_lo"))
                dve.wait_ge(S("lat_s"), 2)
                tt(acc[:, 0:T], tmp[0][:, 0:T], tmp[1][:, 0:T], ALU.add, S("lat_sq"))
                dve.wait_ge(S("ada_cols"), 2)
                tt(modx[:, 16:48], ps[:, m6 + 16:m6 + 48], cols[:, ab + 16:ab + 48], ALU.add, S("mods"))
                dve.wait_ge(S("mods"), 5)
                n2 = cols[:, COLS["n2"]:COLS["n2"] + 8]
                nc.vector.scalar_tensor_tensor(sc2[:, :], modx[:, 32:40], 1.0, n2, ALU.add, ALU.mult).then_inc(S("mods"), 1)
                dve.wait_ge(S("norm_sum"), 2)
                mean_square(dve, "latq", ps[:, 4 * HALF:6 * HALF], QL, EPS, P, 0, T)
                for k in range(2):
                    tt(ql[:, k, :], ql[:, k, :], rs[:, 0:T], ALU.mult, S("lat_t"))
                for k in range(2):
                    dve.wait_ge(S("lat_hi"), k + 1)
                    sub(qnlo[:, k, :], ql[:, k, :], qnhi[:, k, :], S("qn_lo"))
                dve.wait_ge(S("norm_sum"), 3)
                mean_square(dve, "latkv", ps[:, 0:KEYS], P, EPS, P, 0, KEYS)
                tt(kvl[:, :], kvl[:, :], rs[:, :], ALU.mult, S("lat_t"))
                dve.wait_ge(S("lat_hi"), 3)
                sub(kvlo[:, :], kvl[:, :], kvhi[:, :], S("kvn_lo"))
            if on("gates"):
                dve.wait_ge(S("rope_loaded"), 32)
                with dve.Fori(0, 4) as i:
                    for u in range(4):
                        w = (T, KEYS)[u % 2]
                        r = slice(64, QK)
                        n = 4 * i + u
                        dve.wait_ge(S("prep_a"), n + 1)
                        nc.vector.memset(stat[:, 15:16], 0.0).then_inc(S("prep_go"), 1)
                        nc.vector.stream_shuffle(tmp[1][r, 0:w], tmp[0][r, 0:w], SHUFFLE).then_inc(S("prep_swap"), 1)
                        dve.wait_ge(S("prep_swap"), n + 1)
                        tt(tmp[1][r, 0:w], tmp[1][r, 0:w], sinT[r, 0:w], ALU.mult, S("prep_sin"))
                        dve.wait_ge(S("prep_ss"), n + 1)
                        nc.vector.tensor_scalar(rs[0:QK, 0:w], ps[0:QK, 4 * HALF:4 * HALF + w], 1.0 / QK, EPS, ALU.mult,
                                                ALU.add).then_inc(S("prep_ms"), 1)
                        dve.wait_ge(S("prep_root"), n + 1)
                        nc.vector.reciprocal(rs[0:QK, 0:w], rs[0:QK, 0:w]).then_inc(S("prep_rs"), 1)
                        dve.wait_ge(S("prep_rs"), n + 1)
                        dve.wait_ge(S("prep_rot"), n + 1)
                        tt(tmp[0][0:QK, 0:w], tmp[0][0:QK, 0:w], rs[0:QK, 0:w], ALU.mult, S("prep_full"))
                        dve.wait_ge(S("prep_hi"), n + 1)
                        sub(phd[1][0:QK, 0:w], tmp[0][0:QK, 0:w], phd[0][0:QK, 0:w], S("prep_lo"))
            if on("v"):
                dve.wait_ge(S("prep_lo"), 16)
                dve.wait_ge(S("prep_stored"), 512)
                for n in range(2):
                    dve.wait_ge(S(f"gate_stored{n}"), 128)
                for tt_ in range(10):
                    dve.wait_ge(S("v_hi"), tt_ + 1)
                    sub(Vlo[:, tt_, :], ps[:, (tt_ % 8) * HALF:(tt_ % 8 + 1) * HALF], Vhi[:, tt_, :], S("v_lo"))
            if on("dft"):
                with dve.Fori(0, 2) as h:
                    for part in range(2):
                        for g in range(NG):
                            dve.wait_ge(S("ab_hi"), 8 * h + 4 * part + g + 1)
                            sub(ABlo[:, g, part, :], ps[:, (4 * part + g) * HALF:(4 * part + g + 1) * HALF], ABhi[:, g, part, :], S("ab_lo"))
                    for g in range(NG):
                        dve.wait_ge(S("fm_hi"), 4 * h + g + 1)
                        sub(fms[1][:, g, :], ps[:, g * HALF:(g + 1) * HALF], fms[0][:, g, :], S("fm_lo"))
            if on("mla"):
                dve.wait_ge(S("consts"), 48)
                with dve.Fori(0, 4) as i:
                    def evict(j, phase):
                        if phase == 1:
                            r = slice(64 * j, 64 * j + 64)
                            dve.wait_ge(S("mla_ohi"), 2 * i + j + 1)
                            sub(ats[1][r, :], ps[r, 6 * HALF:8 * HALF], ats[0][r, :], S("att_out"))
                    att_dve(dve, mla, i, evict)
            if on("merge"):
                dve.wait_ge(S("att_pv"), 32)
                with dve.Fori(0, 4) as i:
                    for j in range(2):
                        panels_done(dve, "merge", 2, i, j)
                        dve.wait_ge(S(f"sg_loaded{j}"), 32 * i + 32)
                        dve.wait_ge(S("y_lo"), 2 * i + j)
                        for n, o in enumerate((mm1, mm2)):
                            g, free = pair_of("merge", 2 * j + n)
                            tt(o[:, :], g, sg[j][n][:, :], ALU.mult, free)
                        for n in range(2):
                            evicted(dve, "merge", 4, i, 2 * j + n)
                        tt(mm1[:, :], mm1[:, :], mm2[:, :], ALU.add, S("y_full"))
                        dve.wait_ge(S("y_hi"), 2 * i + j + 1)
                        sub(Ylo[:, 2 * i + j, :], mm1[:, :], Yhi[:, 2 * i + j, :], S("y_lo"))
            if on("wout"):
                dve.wait_ge(S("x_loaded"), 32)
                nc.vector.memset(acc[:, :], 0.0).then_inc(S("zeroed"), 1)
                dve.wait_ge(S("zeroed"), 1)
                with dve.Fori(0, 4) as i:
                    for j in range(2):
                        panels_done(dve, "wout", 2, i, j)
                        g, free = pair_of("wout", j)
                        x_ = X1[:, 2 * i + j, :]
                        nc.vector.scalar_tensor_tensor(x_, g, modx[:, bass.ds(2 * i + (16 + j), 1)], x_, ALU.mult, ALU.add).then_inc(free, 1)
                        dve.wait_ge(S("n2_sq"), 2 * i + j + 1)
                        dve.wait_ge(S("n2_acc"), 2 * i + j)
                        tt(acc[:, 0:T], acc[:, 0:T], tmp[j][:, 0:T], ALU.add, S("n2_acc"))
                dve.wait_ge(S("norm_sum"), 4)
                mean_square(dve, "n2", ps[:, 4 * HALF:6 * HALF], D, EPS, P, 0, T)
                apply_dve(dve, "n2", KT, lambda k: X1[:, k, :], T, lambda k: Hb[1][:, k, :], lambda k: Hb[0][:, k, :])
            if on("mlp"):
                with dve.Fori(0, 4) as i:
                    def usq(t):
                        evicted(dve, "mlp", 16, i, t)
                        tt(tmp[t % 2][:, 0:T], tmp[t % 2][:, 0:T], tmp[t % 2][:, 0:T], ALU.mult, S("u_sq"))
                        dve.wait_ge(S("u_hi"), 8 * i + t + 1)
                        sub(Ulo[:, t, :], tmp[t % 2][:, 0:T], Uhi[:, t, :], S("u_lo"))
                    for t in range(8):
                        usq(t)
                    for k in range(8):
                        panels_done(dve, "mlp", 16, i, 8 + k)
                        g, free = pair_of("mlp", 8 + k)
                        nc.vector.scalar_tensor_tensor(X1[:, k, :], g, modx[:, 40 + k:41 + k], X1[:, k, :], ALU.mult, ALU.add).then_inc(free, 1)
                for k in range(KT):
                    dve.wait_ge(S("x2_hi"), k + 1)
                    sub(Hb[1][:, k, :], X1[:, k, :], Hb[0][:, k, :], S("x2_lo"))
            if on("pool"):
                dve.wait_ge(S("x2_hi"), 8)
                for b in (*pu, *pa):
                    nc.vector.memset(b[:, 0:16], 0.0).then_inc(S("zeroed"), 1)
                dve.wait_ge(S("zeroed"), 5)
                for g4 in range(4):
                    for t in range(2):
                        evicted(dve, "pool", 6, g4, t)
                        dve.wait_ge(S("pm_lo"), 2 * g4 + t)
                        src = pu[t]
                        for s_ in range(g4 + 1):
                            sh = 1 << s_
                            dst = pa[(s_ + g4) % 2]
                            tt(dst[:, 16:], src[:, 16:], src[:, 16 - sh:16 - sh + T], ALU.add, S("pool_sum"))
                            dve.wait_ge(S("pool_sum"), pool_count(g4, t, s_))
                            src = dst
                        o = pm_buf(g4, t)
                        tt(stat_pool[:, :], src[:, 16:32], poolc[:, g4, :], ALU.mult, S("pool_few"))
                        nc.vector.scalar_tensor_tensor(o[:, 32:], src[:, 32:], 1.0 / (2 << g4), pu[t][:, 32:], ALU.mult,
                                                       ALU.subtract).then_inc(S("pool_most"), 1)
                        dve.wait_ge(S("pool_few"), 2 * g4 + t + 1)
                        tt(o[:, 16:32], stat_pool[:, :], pu[t][:, 16:32], ALU.subtract, S("pm_full"))
                        dve.wait_ge(S("pool_most"), 2 * g4 + t + 1)
                        dve.wait_ge(S("pm_full"), 2 * g4 + t + 1)
                        dve.wait_ge(S("pool_sig"), 2 * g4 + t + 1)
                        g, free = pair_of("pool", 2 + t)
                        tt(sil[t][:, :], g, sgm[:, :], ALU.mult, free)
                        dve.wait_ge(S("pm_hi"), 2 * g4 + t + 1)
                        sub(PMlo[:, t, :], o[:, 16:], PMhi[:, t, :], S("pm_lo"))
                    for t in range(2):
                        panels_done(dve, "pool", 5, g4, 4)
                        g, free = pair_of("pool", 4 + t)
                        dve.wait_ge(S("pool_ylo"), 2 * g4 + t)
                        evicted(dve, "pool", 6, g4, 2 + t)
                        nc.vector.scalar_tensor_tensor(yf[:, :], g, col("pscale", 2 * g4 + t), sil[t][:, :], ALU.mult, ALU.mult).then_inc(free, 1)
                        dve.wait_ge(S("pool_yhi"), 2 * g4 + t + 1)
                        sub(ys[t][1][:, :], yf[:, :], ys[t][0][:, :], S("pool_ylo"))

            def mem_heads(l):
                a, st = mem[l], f"mem{l + 1}"
                if l == 1:
                    dve.wait_ge(S("fox_stored"), 256)
                with dve.Fori(0, MH) as i:
                    dve.wait_ge(S("mem_qhi"), 4 * l + i + 1)
                    g, free = pair_of(st, 0)
                    sub(Qm[1][:, :], g, Qm[0][:, :], free)
                    dve.wait_ge(S("mem_sig"), 4 * l + i + 1)
                    g, free = pair_of(st, 1)
                    tt(sil[0][:, :], g, sgm[:, :], ALU.mult, free)

                    def evict(j, phase):
                        if phase == 0:
                            dve.wait_ge(S("att_pv"), a.ub // 2 + 4 * i + 4)
                            evicted(dve, st, 2, i, 1)
                            dve.wait_ge(S("mem_ylo"), 4 * l + i)
                            tt(yf[:, :], ps[:, 6 * HALF:8 * HALF], sil[0][:, :], ALU.mult, S("att_out"))
                        else:
                            dve.wait_ge(S("mem_yhi"), 4 * l + i + 1)
                            sub(ys[1][1][:, :], yf[:, :], ys[1][0][:, :], S("mem_ylo"))
                    att_dve(dve, a, i, evict)

            def out_proj(l):
                st = f"out{l + 1}"
                nc.vector.memset(acc[:, :], 0.0).then_inc(S("zeroed"), 1)
                dve.wait_ge(S("zeroed"), 6 + l)
                with dve.Fori(0, 2) as i:
                    for t in range(4):
                        n = 4 * i + t
                        if t % 2 == 0:
                            dve.wait_ge(S("out_mid"), 4 * l + 2 * i + t // 2 + 1)
                        else:
                            panels_done(dve, st, 6, i, 3 * (t // 2) + 2)
                        g, free = pair_of(st, t)
                        b = tmp[t % 2][:, 0:T]
                        dve.wait_ge(S("ln_acc"), 8 * l + n)
                        nc.vector.scalar_tensor_tensor(b, f32(Hb[0][:, n, :]), ALPHA, g, ALU.mult, ALU.add).then_inc(free, 1)
                        evicted(dve, st, 4, i, t)
                        nc.vector.scalar_tensor_tensor(Z[:, n, :], f32(Hb[1][:, n, :]), ALPHA, b, ALU.mult, ALU.add).then_inc(S("ln_z"), 1)
                        dve.wait_ge(S("ln_z"), 8 * l + n + 1)
                        tt(acc[:, 0:T], acc[:, 0:T], Z[:, n, :], ALU.add, S("ln_acc"))
                dve.wait_ge(S("norm_sum"), 2 * l + 5)
                nc.vector.tensor_scalar(rs[:, 0:T], ps[:, 4 * HALF:6 * HALF], 1.0 / D, None, ALU.mult).then_inc(S("ln_mu"), 1)
                dve.wait_ge(S("ln_mu"), l + 1)
                for k in range(KT + 1):
                    if k < KT:
                        tt(Z[:, k, :], Z[:, k, :], rs[:, 0:T], ALU.subtract, S("ln_zc"))
                    if k >= 1:
                        dve.wait_ge(S("ln_sq"), 8 * l + k)
                        if k == 1:
                            nc.vector.tensor_copy(acc[:, 0:T], tmp[0][:, 0:T]).then_inc(S("ln_vacc"), 1)
                        else:
                            dve.wait_ge(S("ln_vacc"), 8 * l + k - 1)
                            tt(acc[:, 0:T], acc[:, 0:T], tmp[(k - 1) % 2][:, 0:T], ALU.add, S("ln_vacc"))
                dve.wait_ge(S("norm_sum"), 2 * l + 6)
                mean_square(dve, f"ln{l}", ps[:, 4 * HALF:6 * HALF], D, LN_EPS, P, 0, T)
                if l == 0:
                    apply_dve(dve, "ln0", KT, lambda k: Z[:, k, :], T, lambda k: Hb[1][:, k, :], lambda k: Hb[0][:, k, :])
                else:
                    for k in range(KT):
                        if k >= 2:
                            dve.wait_ge(S(f"out_stored{k % 2}"), 16 * (k // 2))
                        tt(tmp[k % 2][:, 0:T], Z[:, k, :], rs[:, 0:T], ALU.mult, S("ap_t"))

            if on("mem1"):
                mem_heads(0)
            if on("out1"):
                out_proj(0)
            if on("forget"):
                r = slice(0, FOX)
                panels_done(dve, "forget", 1, 0, 0)
                dve.wait_ge(S("ap_lo"), 32)
                nc.vector.tensor_scalar(tmp[0][r, 0:T], ps[r, 4 * HALF:6 * HALF], cols[r, COLS["bf"]:COLS["bf"] + 1], None,
                                        ALU.add).then_inc(S("logits_read"), 1)
                nc.vector.memset(rs[r, 0:T], 1.0).then_inc(S("gate_log"), 1)
                for x_ in (Kf, Qf):
                    for j in range(2):
                        for n in range(2):
                            nc.vector.memset(f32(x_[j][n][64:66, :]), 1.0 - n).then_inc(S("aug"), 1)
                dve.wait_ge(S("fg"), 3)
                nc.vector.tensor_scalar(tmp[0][r, 0:T], tmp[0][r, 0:T], 0.0, None, ALU.min).then_inc(S("gate_log"), 1)
                dve.wait_ge(S("gate_log"), 2)
                tt(acc[r, 0:T], tmp[1][r, 0:T], tmp[0][r, 0:T], ALU.subtract, S("gate_log"))
                dve.wait_ge(S("gate_log"), 3)
                nc.vector.tensor_tensor_scan(ncum[r, :], rs[r, 0:T], acc[r, 0:T], 0.0, ALU.mult, ALU.add).then_inc(S("cum"), 1)
                dve.wait_ge(S("fg"), 4)
                sub(nch[1][r, :], ncum[r, :], nch[0][r, :], S("cum"))
                dve.wait_ge(S("cum"), 2)
                for n in range(2):
                    nc.vector.tensor_scalar(mch[n][r, :], f32(nch[n][r, :]), -1.0, None, ALU.mult).then_inc(S("cum"), 1)
            if on("fox"):
                with dve.Fori(0, 8) as i:
                    g, free = pair_of("fox", 0)
                    for j in range(2):
                        dve.wait_ge(S("fox_hi"), 4 * i + j + 1)
                        sub(Kf[j][1][0:64, :], g[64 * j:64 * j + 64, :], Kf[j][0][0:64, :], free if j else S("fox_low"))
                    g, free = pair_of("fox", 2)
                    for j in range(2):
                        dve.wait_ge(S("fox_hi"), 4 * i + j + 3)
                        nc.vector.scalar_tensor_tensor(Qf[j][1][0:64, :], g[64 * j:64 * j + 64, :], 64 ** -0.5,
                                                       f32(Qf[j][0][0:64, :]), ALU.mult, ALU.subtract).then_inc(free if j else S("fox_low"), 1)
                    dve.wait_ge(S("fox_vhi"), i + 1)
                    sub(Vf[1][:, :, :], ps[:, 4 * HALF:6 * HALF].rearrange("p (k d) -> p k d", d=P), Vf[0][:, :, :], S("fox_vlo"))
                    dve.wait_ge(S("fox_sig"), i + 1)
                    g, free = pair_of("fox", 3)
                    tt(acc[:, 0:T], g, rs[:, 0:T], ALU.mult, free)

                    def evict(j, phase):
                        r = slice(64 * j, 64 * j + 64)
                        if phase == 0:
                            dve.wait_ge(S("att_pv"), fox.ub // 2 + 8 * i + 4 * j + 4)
                            evicted(dve, "fox", 4, i, 3)
                            dve.wait_ge(S("fox_ylo"), 2 * i + j)
                            tt(yff[r, :], ps[r, 6 * HALF:8 * HALF], acc[r, 0:T], ALU.mult, S("att_out"))
                        else:
                            dve.wait_ge(S("fox_yhi"), 2 * i + j + 1)
                            sub(ysf[1][r, :], yff[r, :], ysf[0][r, :], S("fox_ylo"))
                    att_dve(dve, fox, i, evict)
            if on("mem2"):
                mem_heads(1)
            if on("out2"):
                out_proj(1)

        @block.sync
        def _(sp):
            sp_program(sp)

        @block.gpsimd
        def _(gp):
            pool_program(gp)

        @block.tensor
        def _(pe):
            pe_program(pe)

        @block.scalar
        def _(act):
            act_program(act)

        @block.vector
        def _(dve):
            dve_program(dve)


def _tiles(w):
    k, n = w.shape
    return w.reshape(k // P, P, n // P, P).transpose(2, 1, 0, 3).reshape(n // P, P, k)


def _moving(w):
    k, n = w.shape
    return w.reshape(k // 256, 2, P, n).transpose(0, 2, 1, 3).reshape(k // 256, P, 2 * n)


def _padded(a):
    return np.pad(a, ((0, 0), (0, 0), (0, PW - a.shape[2])))


def _feature_major(x):
    n = x.shape[0]
    return np.ascontiguousarray(x.T.reshape(KT, P, n).transpose(1, 0, 2))


def _stream(i):
    w_in, w_in2, w_kv2, kvb, qb = i["w_in"][0], i["w_in_2"], i["w_kv_shared_2"], i["w_kvb"][0], i["w_qb"][0]
    gates = _tiles(w_in[:, 928:])
    parts = []
    for layer in range(2):
        parts += [_tiles(i["w_mem_kv_2"][layer][:, :512]), _moving(i["w_mem_kv_2"][layer][:, 512:])]
    parts += [_tiles(w_in[:, 512:896]), _tiles(w_in[:, 832:960]), _moving(w_in[:, :512])]
    for h in range(NH):
        q = qb[:, QK * h:QK * h + QK].reshape(2, P, QK).transpose(1, 0, 2).reshape(1, P, 2 * QK)
        parts += [_padded(q), gates[2 * h:2 * h + 1], _padded(kvb[None, :, P * h:P * h + P]), gates[2 * h + 1:2 * h + 2]]
    parts.append(_padded(kvb.reshape(P, NH, P)[:, :, NOPE:].reshape(1, P, FW)))
    ang = 2 * np.pi * (np.outer(np.arange(T), np.arange(T)) % T) / T
    cos, sin = np.cos(ang).astype(np.float32), np.sin(ang).astype(np.float32)
    ch = 2 * np.pi * (np.outer(np.arange(P), np.arange(P)) % P) / P
    norm = 1 / math.sqrt(T * P)
    chc, chs = (np.cos(ch) * norm).astype(np.float32), (-np.sin(ch) * norm).astype(np.float32)
    for h in range(2):
        parts += [_moving(cos[:, HALF * h:HALF * h + HALF]), _moving(sin[:, HALF * h:HALF * h + HALF]), _padded(chc[None]), _padded(chs[None])]
    f, a = _tiles(i["w_fourier"][0]), _tiles(i["w_mla_o"][0])
    parts += [np.concatenate([f, a], axis=2), _tiles(i["w_out"][0])]
    for c in range(4):
        parts += [_tiles(i["w_up"][0][:, D * c:D * c + D]), _tiles(i["w_down"][0][D * c:D * c + D])]
    u, u2 = _tiles(w_in2[0]), _tiles(w_in2[1])
    for g in range(4):
        mix = i["pool_w_2"][0, g].reshape(2, P, 2, P).transpose(1, 2, 0, 3).reshape(1, P, 512)
        parts += [u[2 * g:2 * g + 2], u[MT + 2 * g:MT + 2 * g + 2], _padded(mix)]

    def mem(t):
        return np.stack([t[8:12], t[MT + 8:MT + 12]], axis=1).reshape(8, P, PW)

    def proj(w):
        return _tiles(w).reshape(8, P, MT, P).transpose(0, 2, 1, 3).reshape(12, 8, P, P).transpose(0, 2, 1, 3).reshape(12, P, PW)

    parts += [mem(u), proj(i["w_out_2"][0])]
    fg = np.pad(w_kv2[:, 2 * D:], ((0, 0), (0, P - FOX)))
    k, v = _tiles(w_kv2[:, :D]), _tiles(w_kv2[:, D:2 * D])
    parts += [_tiles(fg), np.stack([k, v, u2[:8], u2[MT:MT + 8]], axis=1).reshape(32, P, PW), mem(u2), proj(i["w_out_2"][1])]
    parts.append(np.zeros((LEAD, P, PW), np.float32))
    w = np.concatenate(parts, axis=0)
    assert w.shape[0] == NP + LEAD, w.shape
    return w


def _columns(i):
    def c(a):
        a = a.reshape(-1)
        if a.shape[0] < P:
            a = np.pad(a, (0, P - a.shape[0]))
        return a.reshape(-1, P).T

    return np.ascontiguousarray(np.concatenate([c(i[n]) for n in (
        "c", "c_ctx", "ada_b", "norm1_g", "norm2_g", "b_gate", "q_norm_g", "kv_norm_g", "q_gain", "k_gain", "ln_g_2", "ln_b_2",
        "pool_scale_2", "b_forget_2")], axis=1))


def _rope():
    n = np.arange(T)
    freqs = (10000.0 ** (-np.arange(8, dtype=np.float32) / 8)).astype(np.float32)
    row, colu = (n // 64).astype(np.float32), (n % 64).astype(np.float32)
    ar, ac = row[:, None] * freqs, colu[:, None] * freqs
    ang = np.concatenate([ar, ar, ac, ac], axis=1).T.astype(np.float32)
    cos, sin = np.ones((QK, KEYS), np.float32), np.zeros((QK, KEYS), np.float32)
    cos[NOPE:, :T] = np.cos(ang)
    sign = np.array([-1.0] * 8 + [1.0] * 8 + [-1.0] * 8 + [1.0] * 8, np.float32)[:, None]
    sin[NOPE:, :T] = np.sin(ang) * sign
    return cos, sin


def kernel(**inputs):
    from concourse import bacc
    from concourse.bass_utils import run_bass_kernel_spmd

    i = {k: np.asarray(v) for k, v in inputs.items()}
    cos, sin = _rope()
    few = np.array([[1.0 / min(t + 1, 2 << g) for t in range(16)] for g in range(4)], np.float32)
    arrays = {
        "w": _stream(i),
        "ada": np.ascontiguousarray(i["ada_w"][0].reshape(KT, P, 24, 256).transpose(2, 1, 0, 3)),
        "cols": _columns(i),
        "x": _feature_major(i["x"][0]),
        "ctx": _feature_major(i["ctx"][0]),
        "mem": _feature_major(i["mem_2"][0]),
        "ident": np.eye(P, dtype=np.float32),
        "mask": np.where(np.arange(P)[None, :] <= np.arange(P)[:, None], 0.0, -1e30).astype(np.float32),
        "poolc": np.ascontiguousarray(np.broadcast_to(few, (P, 4, 16))),
        "cos": cos,
        "sin": sin,
    }
    nc = bacc.Bacc("TRN2", target_bir_lowering=False, num_devices=1)
    d = {n: nc.dram_tensor(f"in_{n}", a.shape, F, kind="ExternalInput").ap() for n, a in arrays.items()}
    out = nc.dram_tensor("out", (KT, P, T), F, kind="ExternalOutput").ap()
    build(nc, d, out)
    r = run_bass_kernel_spmd(nc, [{f"in_{n}": a for n, a in arrays.items()}], core_ids=[0])
    return np.ascontiguousarray(r.results[0]["out"].reshape(D, T).T).reshape(1, T, D)
```

```python
import math
from contextlib import ExitStack

import concourse.bass as bass
import numpy as np
from concourse import mybir

ALU = mybir.AluOpType
ACT = mybir.ActivationFunctionType
AXX = mybir.AxisListType.X
F = mybir.dt.float32
R = mybir.dt.float32r

P = 128
T = 1024
CTX = 256
KEYS = T + CTX
D = 1024
KT = D // P
HALF = 512
PW = 1024
NH, NOPE, ROPE, VD = 8, 64, 32, 64
QK = NOPE + ROPE
FW = 512
NG = 4
QL = 256
FF = 4 * D
FOX = 16
MH = 4
MIX = D + MH * P
MT = MIX // P
EPS, LN_EPS = 1e-6, 1e-5
ALPHA = 4 ** 0.25
LEAD = 4
SPLIT_LEAD = 2

COLS = {}
_n = 0
for _name, _w in (("c", 8), ("cc", 8), ("ada_b", 48), ("n1", 8), ("n2", 8), ("b_gate", 16), ("qng", 2),
                  ("kvng", 1), ("qg", 1), ("kg", 1), ("ln_g", 16), ("ln_b", 16), ("pscale", 8), ("bf", 1)):
    COLS[_name] = _n
    _n += _w
NCOLS = _n

PANELS = (("mem", 16), ("lat", 4), ("f", 4), ("gates", 32), ("v", 1), ("dft", 20), ("merge", 8), ("wout", 8),
          ("mlp", 64), ("pool", 20), ("mem1", 8), ("out1", 12), ("forget", 1), ("fox", 32), ("mem2", 8), ("out2", 12))
P0 = {}
_n = 0
for _name, _w in PANELS:
    P0[_name] = _n
    _n += _w
NP = _n
NPAN = dict(PANELS)

TILES = (("mem", 8), ("lat", 4), ("gates", 16), ("mla", 80), ("merge", 16), ("wout", 8), ("mlp", 64), ("pool", 24),
         ("mem1", 16), ("out1", 8), ("fox", 160), ("mem2", 16), ("out2", 8))
T0 = {}
_n = 0
for _name, _w in TILES:
    T0[_name] = _n
    _n += _w

SHUFFLE = [(i + 8) % 16 + 16 * (i // 16) for i in range(32)]


ORDER = ["mem", "lat", "f", "gates", "v", "dft", "mla", "merge", "wout", "mlp", "pool", "mem1", "out1", "forget", "fox", "mem2", "out2"]


def build(nc, d, out, upto=99, dbg=None):
    ctx = ExitStack()
    with ctx:
        def sb(name, shape, dt=F):
            return ctx.enter_context(nc.sbuf_tensor(name, shape, dt))

        raw = [sb(f"raw{i}", [P, PW]) for i in range(2)]
        whi = [sb(f"whi{i}", [P, PW], R) for i in range(2)]
        wlo = [sb(f"wlo{i}", [P, PW], R) for i in range(2)]
        onesf = sb("onesf", [P, P])
        onesr = sb("onesr", [P, P], R)
        ident = sb("ident", [P, P])
        cols = sb("cols", [P, NCOLS])
        modx, modc = sb("modx", [P, 48]), sb("modc", [P, 16])
        scx, scc, sc2 = sb("scx", [P, 8]), sb("scc", [P, 8]), sb("sc2", [P, 8])
        silc, sigc = sb("silc", [P, 16]), sb("sigc", [P, 16])
        stat = sb("stat", [P, 16])
        mx, mxf = sb("mx", [P, 24]), sb("mxf", [P, 16])
        identr = sb("identr", [P, P], R)
        stat_pool = sb("stat_pool", [P, 16])
        poolc = sb("poolc", [P, 4, 16])
        rs, acc = sb("rs", [P, KEYS]), sb("acc", [P, KEYS])
        tmp, mrow = [], []
        for i in range(2):
            tmp.append(sb(f"tmp{i}", [P, KEYS]))
            mrow.append(nc.alloc_sbuf_tensor_at(f"mrow{i}", [P, P], R, offset=nc.sbuf_base - 4 * CTX))
        ZONE = 160 * 1024
        zone = sb("zone", [P, ZONE // 4])
        zbase = nc.sbuf_base - ZONE

        def at(name, kb, shape, dt=F):
            n = 4
            for s in shape[1:]:
                n *= s
            assert kb * 1024 + n <= ZONE, (name, kb, n)
            return nc.alloc_sbuf_tensor_at(name, shape, dt, offset=zbase + int(kb * 1024))

        Hhi, Hlo = at("Hhi", 0, [P, KT, T], R), at("Hlo", 32, [P, KT, T], R)
        Mhi, Mlo = at("Mhi", 0, [P, KT, CTX], R), at("Mlo", 8, [P, KT, CTX], R)
        Mraw = at("Mraw", 16, [P, KT, CTX])
        accx, accc = at("accx", 24, [P, 2048]), at("accc", 32, [P, 2048])
        mks = [at("mks_hi", 40, [P, MH, CTX], R), at("mks_lo", 44, [P, MH, CTX], R)]
        mvs = [at("mvs_hi", 48, [P, 2, HALF], R), at("mvs_lo", 52, [P, 2, HALF], R)]
        XT = at("XT", 64, [P, KT, T])
        CT = at("CT", 96, [P, KT, CTX])
        HChi, HClo = at("HChi", 104, [P, KT, CTX], R), at("HClo", 112, [P, KT, CTX], R)
        adas = [at(f"adas{i}", 122 + 8 * i, [P, KT, 256]) for i in range(2)]
        acc2 = at("acc2", 138, [P, 4096])
        ql, kvl, kr = at("ql", 64, [P, 2, T]), at("kvl", 72, [P, KEYS]), at("kr", 77, [P, KEYS])
        Fhi, Flo = at("Fhi", 90, [P, KT, FW], R), at("Flo", 106, [P, KT, FW], R)
        qnhi, qnlo = at("qnhi", 122, [P, 2, T], R), at("qnlo", 130, [P, 2, T], R)
        kvhi, kvlo = at("kvhi", 138, [P, KEYS], R), at("kvlo", 143, [P, KEYS], R)
        cosT, sinT = at("cosT", 148, [P, KEYS]), at("sinT", 153, [P, KEYS])
        gst = [at(f"gst{i}", 82 + 4 * i, [P, T]) for i in range(2)]
        phd = [at("prep_hi", 64, [P, KEYS], R), at("prep_lo", 69, [P, KEYS], R)]
        ABhi, ABlo = at("ABhi", 0, [P, NG, 2, HALF], R), at("ABlo", 16, [P, NG, 2, HALF], R)
        fms = [at("fms_hi", 32, [P, NG, HALF], R), at("fms_lo", 40, [P, NG, HALF], R)]
        Vhi, Vlo = at("Vhi", 48, [P, 10, FW], R), at("Vlo", 69, [P, 10, FW], R)
        mla_heads = []
        for j, kb in enumerate((122, 0, 28, 56)):
            Q_, K_, V_ = ([at(f"{x}{j}{n}", kb + o + w * n, shape, R) for n in range(2)] for x, o, w, shape in (
                ("Qp", 0, 4, [P, T]), ("Kp", 8, 5, [P, KEYS]), ("Vp", 18, 5, [P, 10, P])))
            mla_heads.append((Q_, K_, V_, 64 * (j % 2)))
        Erh, Erl = ([at(f"E{x}{i}", o + 4 * i, [P, T], R) for i in range(2)] for x, o in (("hi", 84), ("lo", 92)))
        ats = [at("ats_hi", 100, [P, T], R), at("ats_lo", 104, [P, T], R)]
        o32 = at("o32", 108, [P, T])
        Fm = [at("Fm_hi", 64, [P, NG, T], R), at("Fm_lo", 80, [P, NG, T], R)]
        At = [at("At_hi", 96, [P, NG, T], R), at("At_lo", 112, [P, NG, T], R)]
        sg = [[at(f"sg{i}{j}", 128 + 8 * i + 4 * j, [P, T]) for j in range(2)] for i in range(2)]
        mm1, mm2 = at("mm1", 144, [P, T]), at("mm2", 148, [P, T])
        Yhi, Ylo = at("Yhi", 0, [P, KT, T], R), at("Ylo", 32, [P, KT, T], R)
        X1 = at("X1", 64, [P, KT, T])
        Hb = [at("Hb_hi", 96, [P, KT, T], R), at("Hb_lo", 128, [P, KT, T], R)]
        Uhi, Ulo = at("Uhi", 0, [P, KT, T], R), at("Ulo", 32, [P, KT, T], R)
        pu = [at(f"pu{i}", 0 + 4.25 * i, [P, T + 16]) for i in range(2)]
        pa = [at(f"pa{i}", 8.5 + 4.25 * i, [P, T + 16]) for i in range(2)]
        PMhi, PMlo = at("PMhi", 17, [P, 2, T], R), at("PMlo", 25, [P, 2, T], R)
        sil = [at(f"sil{i}", 33 + 4 * i, [P, T]) for i in range(2)]
        sgm = at("sgm", 41, [P, T])
        yf = at("yf", 45, [P, T])
        ys = [[at(f"ys{i}{n}", 49 + 4 * (2 * i + n), [P, T], R) for n in range(2)] for i in range(2)]
        Qm = [[at(f"Qm{j}{n}", 8 * j + 4 * n, [P, T], R) for n in range(2)] for j in range(2)]
        Km = [[at(f"Km{j}{n}", 16 + 2 * j + n, [P, CTX], R) for n in range(2)] for j in range(2)]
        Vm = [[at(f"Vm{j}{n}", 20 + 2 * j + n, [P, 2, P], R) for n in range(2)] for j in range(2)]
        Em = [[at(f"Em{j}{n}", 24 + 16 * n + 4 * j, [P, T], R) for n in range(2)] for j in range(4)]
        om = at("om", 56, [P, T])
        silm = [at(f"silm{j}", 60 + 4 * j, [P, T]) for j in range(2)]
        ym = [[at(f"ym{j}{n}", 68 + 8 * j + 4 * n, [P, T], R) for n in range(2)] for j in range(2)]
        mr = [at(f"mr{j}", 84 + 4 * j, [P, T], R) for j in range(2)]
        sgq = at("sgq", 92, [P, T])
        maskc, maskr = at("maskc", 92, [P, P]), at("maskr", 93, [P, P], R)
        fox_heads = []
        for j in range(2):
            Q_, K_, V_ = ([at(f"{x}{j}{n}", o + 8 * j + 4 * n, shape, R) for n in range(2)] for x, o, shape in (
                ("Qf", 0, [P, T]), ("Kf", 16, [P, T]), ("Vf", 32, [P, KT, P])))
            fox_heads.append((Q_, K_, V_, 64 * j))
        Qf, Kf, Vf = ([h[k] for h in fox_heads] for k in range(3))
        yff = at("yff", 48, [P, T])
        nch = [at("nch_hi", 52, [P, T], R), at("nch_lo", 56, [P, T], R)]
        mch = [at("mch_hi", 60, [P, T], R), at("mch_lo", 64, [P, T], R)]
        ysf = [at("ysf_hi", 68, [P, T], R), at("ysf_lo", 72, [P, T], R)]
        Efh, Efl = ([at(f"Ef{x}{i}", o + 4 * i, [P, T], R) for i in range(2)] for x, o in (("hi", 52), ("lo", 60)))
        vtf = at("vtf", 84, [P, T])
        ncum = at("ncum", 88, [P, T])
        Z = at("Z", 96, [P, KT, T])
        Yb = [at("Yb_hi", 0, [P, MT, T], R), at("Yb_lo", 48, [P, MT, T], R)]
        ps = ctx.enter_context(nc.psum_tensor("ps", [P, 8 * HALF], F))
        G = [ps[:, 0:1024], ps[:, 1024:2048]]

        def scratch(name, *shape):
            return nc.dram_tensor(name, shape, F, kind="Internal").ap()

        mk_d = scratch("mk_d", 2, 2, P, MH, CTX)
        mv_d = scratch("mv_d", 2, 2, P, 2, HALF)
        gate_d = scratch("gate_d", 16, P, T)
        q_d, k_d = scratch("q_d", NH, 2, QK, T), scratch("k_d", NH, 2, QK, KEYS)
        v_d = scratch("v_d", 2, 4, P, 10, P)
        fm_d, at_d = scratch("fm_d", 2, NG, P, T), scratch("at_d", 2, NG, P, T)
        y_d = [scratch(f"y_d{l}", MT, 2, P, T) for l in range(2)]
        cum_d = scratch("cum_d", FOX, 2, 2, T)

        sems = {}

        def S(name):
            if name not in sems:
                sems[name] = ctx.enter_context(nc.semaphore(name))
            return sems[name]

        g_free = [S("g_free0"), S("g_free1")]
        f32 = lambda ap: ap.bitcast(F)
        block = ctx.enter_context(nc.Block())
        SCALE = {"mla": QK ** -0.5, "fox": 1.0, "mem": P ** -0.5}

        def evicted(eng, stage, tiles, i, t):
            if isinstance(i, int):
                t, i = t + tiles * i, 0
            n = T0[stage] + t
            eng.wait_ge(g_free[n % 2], n // 2 + 1 + (tiles // 2) * i)

        def pair_of(stage, t):
            n = T0[stage] + t
            return G[n % 2], g_free[n % 2]

        def panels_done(eng, stage, per, i, j):
            eng.wait_ge(S("panel_done"), P0[stage] + per * i + j + 1)

        def pair(pe, stage, tiles, i, t):
            if isinstance(i, int):
                t, i = t + tiles * i, 0
            n = T0[stage] + t
            pe.wait_ge(g_free[n % 2], n // 2 + (tiles // 2) * i)
            return G[n % 2]

        def whi_of(w, k):
            return w[:, k * HALF:(k + 1) * HALF]

        def pm_buf(g, t):
            return pa[1]

        def pool_count(g, t, s):
            return g * (g + 1) + t * (g + 1) + s + 1


        class Att:

            def __init__(self, name, heads, rows, nkt, E, scale, before, fb, cb, kb, pb, per_step, causal=False):
                self.name, self.heads, self.rows, self.nkt, self.E, self.scale = name, heads, rows, nkt, E, scale
                self.H, self.before, self.fb, self.cb, self.kb, self.pb = len(heads), before, fb, cb, kb, pb
                self.per_step, self.causal = per_step, causal
                self.chunks = []
                for qt in range(8):
                    w = (qt + 1) * P if causal else nkt * P
                    self.chunks += [(qt, c, min(c + HALF, w), c // HALF) for c in range(0, w, HALF)]
                self.C, self.parts = len(self.chunks), (1 if nkt == 8 else 2) + 1
                self.steps = range(nkt)

            def of_step(self, s):
                return range(s * self.per_step, min((s + 1) * self.per_step, self.C))

            def queries(self, kt):
                return kt * P if self.causal else 0

            def head(self, i, j):
                return self.before + self.H * i + j

            def flip(self, i, j):
                return self.fb + self.H * i + j

            def used(self, i, j, kt):
                return self.pb + self.nkt * (self.H * i + j) + kt

            def unit(self, i, j, kt):
                return self.kb + self.nkt * (self.H * i + j) + kt

            def chunk(self, i, j, c):
                return self.cb + self.C * (self.H * i + j) + c

            def tile(self, i, j, kt):
                return (4 if self.causal else 0) + self.nkt * j + kt

            def span(self, kt):
                a = self.queries(kt)
                return ([(a, HALF)] if a < HALF else []) + [(max(a, HALF), T)]

        mla = Att("mla", mla_heads, QK, 10, (Erh, Erl), SCALE["mla"], 0, 0, 0, 0, 0, 4)
        fox = Att("fox", fox_heads, 66, 8, (Efh, Efl), SCALE["fox"], 8, 10, 200, 88, 80, 3, causal=True)
        mla.row0, fox.row0 = 0, 256 + 128
        mla.y, mla.o32, fox.y, fox.o32 = ats, o32, ysf, yff
        PRIMED = {"att_max": 2, "att_lo": 2, "att_pv": 2, "att_mlo": 1, "att_out": 1, "att_ylo": 1, "att_stored": 1, "mem_pv": 1, "mem_stored": 1}
        PV = ps[:, 4 * HALF:6 * HALF]

        def mm3(o, wh, wl, xh, xl, start, stop):
            nc.tensor.matmul(o, wh, xh, start=start, stop=False)
            nc.tensor.matmul(o, wh, xl, start=False, stop=False)
            return nc.tensor.matmul(o, wl, xh, start=False, stop=stop)

        def mem_c(l, i):
            return (192, 392)[l] + 4 * i + PRIMED["att_max"]

        def mem_f(l, i):
            return (8, 26)[l] + i

        def mem_r(l, i):
            return (256, 256 + 128 + 512)[l] + 64 * i

        def mem_u(l, i):
            return (80, 216)[l] + 4 * i

        sums_m = (rs, acc)

        def others(r0):
            return slice(64 - r0, 128 - r0)

        def att_pe(pe, a):
            tiles = a.nkt * a.H + (4 if a.causal else 0)

            def chunk(i, j, c):
                qt, c0, c1, _ = a.chunks[c]
                Q, K = a.heads[j][0], a.heads[j][1]
                pe.wait_ge(S("att_max"), a.chunk(i, j, c) - 1 + PRIMED["att_max"])
                if c == 0:
                    pe.wait_ge(S("att_mlo"), a.flip(i, j) + PRIMED["att_mlo"])
                    a.loaded(pe, i, j)
                b = (6 + c % 2) * HALF
                o = ps[:, b:b + c1 - c0]
                q = [x[0:a.rows, qt * P:qt * P + P] for x in Q]
                k = [x[0:a.rows, c0:c1] for x in K]
                diag = a.causal and c1 == (qt + 1) * P
                last = mm3(o, q[0], q[1], k[0], k[1], True, not diag)
                if diag:
                    last = nc.tensor.matmul(ps[:, b + c1 - c0 - P:b + c1 - c0], identr[:, :], maskr[:, :], start=False, stop=True)
                last.then_inc(S("att_s"), 1)

            def flip_max(i, j):
                pe.wait_ge(S("att_mx"), a.flip(i, j) + 1)
                nc.tensor.transpose(ps[0:8, 6 * HALF:6 * HALF + P], mxf[:, 0:8], ident[:, :]).then_inc(S("att_mt"), 1)

            def transposed(i, j, kt):
                Q, K = a.heads[j][0], a.heads[j][1]
                if kt == 0:
                    pe.wait_ge(S("att_row"), a.row0 + 32 * (a.H * i + j) + 32)
                o = pair(pe, a.name, tiles, i, a.tile(i, j, kt))
                k = [x[0:97, kt * P:kt * P + P] for x in K]
                for c0, c1 in a.span(kt):
                    diag = a.causal and c0 == a.queries(kt)
                    last = mm3(o[:, c0:c1], k[0], k[1], Q[0][0:97, c0:c1], Q[1][0:97, c0:c1], True, not diag)
                    if diag:
                        last = nc.tensor.matmul(o[:, c0:c0 + P], maskr[:, :], identr[:, :], start=False, stop=True)
                last.then_inc(S("att_st"), 1)

            def values(i, j, kt):
                V = a.heads[j][2]
                pe.wait_ge(S("att_lo"), a.unit(i, j, kt) + 1 + PRIMED["att_lo"])
                if kt == 0:
                    pe.wait_ge(S("att_out"), a.head(i, j) + PRIMED["att_out"])
                for c0, c1 in a.span(kt):
                    last = mm3(PV[:, c0:c1], V[0][:, kt, :], V[1][:, kt, :], a.E[0][kt % 2][:, c0:c1], a.E[1][kt % 2][:, c0:c1],
                               kt == 0, kt == a.nkt - 1 and not a.causal)
                if a.causal and kt == a.nkt - 1:
                    Q, K = a.heads[j][0], a.heads[j][1]
                    for c0 in (0, HALF):
                        last = nc.tensor.matmul(PV[:, c0:c0 + HALF], K[1][96:97, 0:P], Q[0][96:97, c0:c0 + HALF], start=False, stop=True)
                last.then_inc(S("att_pv"), 1)

            def scores(i, j):
                for c in range(a.C):
                    chunk(i, j, c)

            def body(i, j):
                for kt in a.steps:
                    transposed(i, j, kt)
                    if j + 1 < a.H:
                        for c in a.of_step(kt):
                            chunk(i, j + 1, c)
                        if kt == a.nkt - 2:
                            flip_max(i, j + 1)
                    if kt >= 1:
                        values(i, j, kt - 1)
                values(i, j, a.nkt - 1)

            return scores, flip_max, body

        def att_act(act, a):
            tiles = a.nkt * a.H + (4 if a.causal else 0)

            def rows_hi(i, j):
                act.wait_ge(S("att_mt"), a.flip(i, j) + 1)
                nc.scalar.activation(mrow[0][0:8, :], ps[0:8, 6 * HALF:6 * HALF + P], ACT.Copy, scale=-1.0).then_inc(S("att_mhi"), 1)

            def rows_send(i, j):
                act.wait_ge(S("att_mlo"), a.flip(i, j) + 1 + PRIMED["att_mlo"])
                for n in range(2):
                    nc.scalar.dma_start(f32(a.heads[j][0][n][96:97, :]), f32(mrow[n][0:8, :])).then_inc(S("att_row"), 16)

            def part_hi(i, j):
                r = slice(a.heads[j][3], a.heads[j][3] + 64)
                act.wait_ge(S("att_y"), a.head(i, j) + 1)
                if j % 2 == 0:
                    act.wait_ge(S("att_stored"), 32 * (a.before // 2 + a.H // 2 * i + j // 2) + PRIMED["att_stored"])
                nc.scalar.activation(a.y[0][r, :], a.o32[r, :], ACT.Copy).then_inc(S("att_yhi"), 1)

            def out(i, j):
                act.wait_ge(S("att_pv"), a.used(i, j, a.nkt - 1) + 1 + PRIMED["att_pv"])
                act.wait_ge(S("att_ylo"), a.head(i, j) + PRIMED["att_ylo"])
                nc.scalar.activation(a.o32[:, :], PV, ACT.Copy).then_inc(S("att_out"), 1)

            def body(i, j):
                for kt in a.steps:
                    n = a.unit(i, j, kt)
                    g, free = pair_of(a.name, a.tile(i, j, kt))
                    c = slice(a.queries(kt), T)
                    act.wait_ge(S("att_st"), n + 1)
                    act.wait_ge(S("att_lo"), n - 1 + PRIMED["att_lo"])
                    nc.scalar.activation(tmp[kt % 2][:, c], g[:, c], ACT.Exp, scale=a.scale).then_inc(free, 1)
                    evicted(act, a.name, tiles, i, a.tile(i, j, kt))
                    act.wait_ge(S("att_pv"), a.used(i, j, kt) - 1 + PRIMED["att_pv"])
                    nc.scalar.activation(a.E[0][kt % 2][:, c], tmp[kt % 2][:, c], ACT.Copy).then_inc(S("att_hi"), 1)
                    if j + 1 < a.H and kt == a.nkt - 2:
                        rows_hi(i, j + 1)
                    if j >= 1 and kt == a.nkt - 2:
                        part_hi(i, j - 1)
                    if j + 1 < a.H and kt == a.nkt - 2:
                        rows_send(i, j + 1)
                out(i, j)
                if j == a.H - 1:
                    part_hi(i, j)

            return rows_hi, rows_send, body

        def att_dve(dve, a):
            def chunk(i, j, c):
                qt, c0, c1, part = a.chunks[c]
                n = a.chunk(i, j, c)
                dve.wait_ge(S("att_s"), n + 1)
                b = (6 + c % 2) * HALF
                nc.vector.reduce_max(mx[:, part * 8 + qt:part * 8 + qt + 1], ps[:, b:b + c1 - c0], AXX).then_inc(S("att_max"), 1)

            def combine(i, j):
                dve.wait_ge(S("att_max"), a.chunk(i, j, a.C - 1) + 1 + PRIMED["att_max"])
                dve.wait_ge(S("att_mlo"), a.flip(i, j) + PRIMED["att_mlo"])
                nc.vector.reduce_max(mxf[:, 0:8], mx[:, 0:8 * a.parts].rearrange("p (c q) -> p q c", q=8), AXX).then_inc(S("att_mx"), 1)

            def rows_lo(i, j):
                dve.wait_ge(S("att_mhi"), a.flip(i, j) + 1)
                nc.vector.scalar_tensor_tensor(mrow[1][0:8, :], ps[0:8, 6 * HALF:6 * HALF + P], -1.0, f32(mrow[0][0:8, :]), ALU.mult,
                                               ALU.subtract).then_inc(S("att_mlo"), 1)

            def low(i, j, kt):
                c = slice(a.queries(kt), T)
                dve.wait_ge(S("att_hi"), a.unit(i, j, kt) + 1)
                nc.vector.tensor_tensor(a.E[1][kt % 2][:, c], tmp[kt % 2][:, c], f32(a.E[0][kt % 2][:, c]), ALU.subtract).then_inc(S("att_lo"), 1)

            def inverse(i, j, q):
                r0 = a.heads[j][3]
                dve.wait_ge(S("att_out"), a.head(i, j) + 1 + PRIMED["att_out"])
                nc.vector.reciprocal(rs[r0:r0 + 64, 256 * q:256 * q + 256], a.o32[others(r0), 256 * q:256 * q + 256]).then_inc(S("att_rec"), 1)

            def product(i, j):
                r = slice(a.heads[j][3], a.heads[j][3] + 64)
                dve.wait_ge(S("att_rec"), 4 * a.head(i, j) + 4)
                nc.vector.tensor_tensor(a.o32[r, :], a.o32[r, :], rs[r, 0:T], ALU.mult).then_inc(S("att_y" if not a.causal else "att_yraw"), 1)
                if a.causal:
                    dve.wait_ge(S("att_yraw"), 2 * i + j + 1)
                    evicted(dve, "fox", 20, i, 3)
                    nc.vector.tensor_tensor(a.o32[r, :], a.o32[r, :], acc[r, 0:T], ALU.mult).then_inc(S("att_y"), 1)

            def part_lo(i, j):
                r = slice(a.heads[j][3], a.heads[j][3] + 64)
                dve.wait_ge(S("att_yhi"), a.head(i, j) + 1)
                nc.vector.tensor_tensor(a.y[1][r, :], a.o32[r, :], f32(a.y[0][r, :]), ALU.subtract).then_inc(S("att_ylo"), 1)

            def body(i, j):
                for kt in a.steps:
                    if j + 1 < a.H:
                        for c in a.of_step(kt):
                            chunk(i, j + 1, c)
                        if a.of_step(kt) and a.of_step(kt)[-1] == a.C - 1:
                            combine(i, j + 1)
                    low(i, j, kt)
                    if j + 1 < a.H and kt == a.nkt - 2:
                        rows_lo(i, j + 1)
                    if j >= 1:
                        q = kt - (a.nkt - 6)
                        if 0 <= q < 4:
                            inverse(i, j - 1, q)
                        if q == 3:
                            product(i, j - 1)
                        if kt == a.nkt - 1:
                            part_lo(i, j - 1)
                if j == a.H - 1:
                    for q in range(4):
                        inverse(i, j, q)
                    product(i, j)
                    part_lo(i, j)

            def scores(i, j):
                for c in range(a.C):
                    chunk(i, j, c)
                combine(i, j)

            return scores, rows_lo, body

        def on(stage):
            return ORDER.index(stage) <= upto

        def sp_program(sp):
            def load_panel(stage, per, i, j):
                if isinstance(i, int):
                    j, i = j + per * i, 0
                n = P0[stage] + LEAD + j
                q = n + per * i
                sp.wait_ge(S("split"), q - 1)
                sp.dma_start(raw[n % 2][:, :], d["w"][q]).then_inc(S(f"loaded{n % 2}"), 16)

            def ada_chunk(c, slot):
                sp.dma_start(adas[slot][:, :, :], d["ada"][c]).then_inc(S(f"ada_loaded{slot}"), 16)

            sp.dma_start(cols[:, :], d["cols"]).then_inc(S("cols_loaded"), 16)
            sp.dma_start(Mraw[:, :, :], d["mem"]).then_inc(S("memt_loaded"), 16)
            for q in range(2):
                sp.dma_start(raw[q][:, :], d["w"][q]).then_inc(S(f"loaded{q}"), 16)
            ada_chunk(0, 0)
            ada_chunk(1, 1)
            sp.dma_start(XT[:, :, :], d["x"]).then_inc(S("x_loaded"), 16)
            sp.dma_start(CT[:, :, :], d["ctx"]).then_inc(S("ctx_loaded"), 16)
            for name, t in (("ident", ident),):
                sp.dma_start(t[:, :], d[name]).then_inc(S("consts"), 16)
            sp.dma_start(poolc[:, :, :], d["poolc"]).then_inc(S("consts"), 16)
            for q in range(2, LEAD):
                sp.wait_ge(S("split"), q - 1)
                sp.dma_start(raw[q % 2][:, :], d["w"][q]).then_inc(S(f"loaded{q % 2}"), 16)

            with sp.Fori(0, 2) as l:
                for j in range(4):
                    load_panel("mem", 8, l, j)
                    sp.wait_ge(S("ada_used"), 4 * l + j + 1)
                    ada_chunk(4 * l + j + 2, j % 2)
                for t in (2, 3):
                    evicted(sp, "mem", 4, l, t)
                for n in range(2):
                    sp.dma_start(mk_d[l, n], f32(mks[n][:, :, :])).then_inc(S("mk_stored"), 16)
                for j in range(4, 8):
                    load_panel("mem", 8, l, j)
                sp.wait_ge(S("mv_lo"), l + 1)
                for n in range(2):
                    sp.dma_start(mv_d[l, n], f32(mvs[n][:, :, :])).then_inc(S("mv_stored"), 16)
            c = 10
            for stage in ("lat", "f"):
                if on(stage):
                    for j in range(4):
                        load_panel(stage, 4, 0, j)
                        for _ in range(2):
                            if c < 24:
                                sp.wait_ge(S("ada_used"), c - 1)
                                ada_chunk(c, c % 2)
                                c += 1
            if on("gates"):
                sp.wait_ge(S("ada_cols"), 2)
                sp.dma_start(cosT[0:QK, :], d["cos"]).then_inc(S("rope_loaded"), 16)
                sp.dma_start(sinT[0:QK, :], d["sin"]).then_inc(S("rope_loaded"), 16)

                def store_unit(i, u):
                    sp.wait_ge(S("prep_lo"), 4 * i + u + 1)
                    dst = (q_d, k_d)[u % 2]
                    w = (T, KEYS)[u % 2]
                    for n in range(2):
                        sp.dma_start(dst[2 * i + u // 2, n], f32(phd[n][0:QK, 0:w])).then_inc(S("prep_stored"), 16)

                def store_gate(i, t):
                    evicted(sp, "gates", 4, i, t)
                    sp.dma_start(gate_d[4 * i + t], gst[t % 2][:, :]).then_inc(S(f"gate_stored{t % 2}"), 16)

                with sp.Fori(0, 4) as i:
                    for j in range(8):
                        load_panel("gates", 8, i, j)
                        if j == 2:
                            store_unit(i, 0)
                        if j == 3:
                            store_gate(i, 0)
                        if j == 5:
                            store_unit(i, 1)
                            store_gate(i, 1)
                        if j == 6:
                            store_unit(i, 2)
                        if j == 7:
                            store_gate(i, 2)
                    store_unit(i, 3)
                    store_gate(i, 3)
            if on("v"):
                load_panel("v", 1, 0, 0)
                sp.wait_ge(S("v_lo"), 10)
                for n, t in enumerate((Vhi, Vlo)):
                    for r in range(4):
                        sp.dma_start(v_d[n, r], f32(t[:, :, P * r:P * r + P])).then_inc(S("v_stored"), 16)
            if on("dft"):
                with sp.Fori(0, 2) as h:
                    for j in range(10):
                        load_panel("dft", 10, h, j)
                    sp.wait_ge(S("fm_lo"), 4 * h + 4)
                    for n in range(2):
                        sp.dma_start(fm_d[n].rearrange("g p f -> p g f")[:, :, bass.ds(h * HALF, HALF)],
                                     f32(fms[n][:, :, :])).then_inc(S("fm_stored"), 16)
            if on("mla"):
                def load_head(i, j):
                    Q, K, V, r0 = mla_heads[j]
                    for n in range(2):
                        sp.dma_start(f32(Q[n][0:QK, :]), q_d[4 * i + j, n]).then_inc(S(f"mla_loaded{j}"), 16)
                        sp.dma_start(f32(K[n][0:QK, :]), k_d[4 * i + j, n]).then_inc(S(f"mla_loaded{j}"), 16)
                        sp.dma_start(f32(V[n][:, :, r0:r0 + 64]), v_d[n, 2 * i + j // 2][:, :, r0:r0 + 64]).then_inc(S(f"mla_loaded{j}"), 16)

                sp.wait_ge(S("prep_stored"), 16 * 32)
                sp.wait_ge(S("v_stored"), 16 * 8)
                load_head(0, 0)
                sp.wait_ge(S("fm_stored"), 16 * 4)
                for j in range(1, 4):
                    load_head(0, j)
                for i in range(2):
                    for j in range(4):
                        if i == 0:
                            sp.wait_ge(S("att_pv"), mla.used(i, j, 9) + 1 + PRIMED["att_pv"])
                            load_head(1, j)
                        if j % 2 == 1:
                            sp.wait_ge(S("att_ylo"), mla.head(i, j) + 1 + PRIMED["att_ylo"])
                            for n in range(2):
                                sp.dma_start(at_d[n, 2 * i + j // 2], f32(ats[n][:, :])).then_inc(S("att_stored"), 16)
            if on("merge"):
                sp.wait_ge(S("att_stored"), 32 * 4 + PRIMED["att_stored"])
                for n in range(2):
                    sp.dma_start(f32(Fm[n][:, :, :]), fm_d[n].rearrange("g p t -> p g t")).then_inc(S("fa_loaded"), 16)
                    sp.dma_start(f32(At[n][:, :, :]), at_d[n].rearrange("g p t -> p g t")).then_inc(S("fa_loaded"), 16)
                sp.wait_ge(S("gate_stored0"), 16 * 8)
                sp.wait_ge(S("gate_stored1"), 16 * 8)
                with sp.Fori(0, 4) as i:
                    for j in range(2):
                        for q in range(2):
                            sp.wait_ge(g_free[q], T0["merge"] // 2 + 2 * i + j - 1)
                        for n in range(2):
                            sp.dma_start(sg[j][n][:, :], gate_d[2 * i + j + 8 * n]).then_inc(S(f"sg_loaded{j}"), 16)
                        load_panel("merge", 2, i, j)
            if on("wout"):
                sp.wait_ge(S("panel_done"), P0["merge"] + 8)
                sp.dma_start(X1[:, :, :], d["x"]).then_inc(S("x_loaded"), 16)
                with sp.Fori(0, 4) as i:
                    for j in range(2):
                        load_panel("wout", 2, i, j)
            if on("mlp"):
                with sp.Fori(0, 4) as i:
                    for j in range(16):
                        load_panel("mlp", 16, i, j)

            def store_y(l, f, slot, sem):
                for n in range(2):
                    sp.dma_start(y_d[l][f, n], f32(slot[n][:, :])).then_inc(S(sem), 16)

            def mem_heads(l):
                st = f"mem{l + 1}"
                sp.wait_ge(S("mk_stored"), 64)
                sp.wait_ge(S("mv_stored"), 64)
                if l == 0:
                    sp.wait_ge(S("pool_ylo"), 8)
                    sp.wait_ge(S("pool_stored0"), 16 * 8)
                    sp.wait_ge(S("pool_stored1"), 16 * 8)
                else:
                    sp.wait_ge(S("att_stored"), 32 * 12 + PRIMED["att_stored"])
                with sp.Fori(0, 2) as i:
                    sp.wait_ge(S("mem_pv"), 4 * l + 2 * i + PRIMED["mem_pv"])
                    for j in range(2):
                        for n in range(2):
                            sp.dma_start(f32(Km[j][n][:, :]), mk_d[l, n][:, 2 * i + j, :]).then_inc(S("mem_kv"), 16)
                            sp.dma_start(f32(Vm[j][n][:, :, :]), mv_d[l, n][:, :, bass.ds(i * 256 + j * P, P)]).then_inc(S("mem_kv"), 16)
                    for j in range(4):
                        load_panel(st, 4, i, j)
                    for j in range(2):
                        sp.wait_ge(S("mem_ylo"), 4 * l + 2 * i + j + 1)
                        for n in range(2):
                            sp.dma_start(y_d[l][8 + j + 2 * i, n], f32(ym[j][n][:, :])).then_inc(S("mem_stored"), 16)

            def out_proj(l):
                st = f"out{l + 1}"
                sp.wait_ge(S("mem_stored"), 128 * (l + 1) + PRIMED["mem_stored"])
                for n in range(2):
                    sp.dma_start(f32(Yb[n][:, :, :]), y_d[l][:, n].rearrange("f p t -> p f t")).then_inc(S("yb"), 16)
                with sp.Fori(0, 2) as i:
                    for j in range(6):
                        load_panel(st, 6, i, j)

            if on("pool"):
                for g in range(4):
                    for j in range(5):
                        load_panel("pool", 5, g, j)
                    for t in range(2):
                        sp.wait_ge(S("pool_ylo"), 2 * g + t + 1)
                        store_y(0, 2 * g + t, ys[t], f"pool_stored{t}")
            if on("mem1"):
                mem_heads(0)
            if on("out1"):
                out_proj(0)
            if on("forget"):
                sp.dma_start(maskc[:, :], d["mask"]).then_inc(S("consts"), 16)
                load_panel("forget", 1, 0, 0)
                sp.wait_ge(S("cum"), 4)
                for s_, t in enumerate((nch, mch)):
                    for n in range(2):
                        sp.dma_start(cum_d[:, s_, n], f32(t[n][0:FOX, :])).then_inc(S("cum_stored"), 16)
                sp.wait_ge(S("cum_stored"), 64)
                sp.wait_ge(S("aug"), 20)
            if on("fox"):
                with sp.Fori(0, 8) as i:
                    sp.wait_ge(S("att_pv"), fox.used(i, 0, 0) + PRIMED["att_pv"])
                    for j in range(2):
                        for n in range(2):
                            sp.dma_start(f32(Kf[j][n][64:65, :]), cum_d[bass.ds(2 * i + j, 1), 0, n]).then_inc(S("fox_cum"), 16)
                            sp.dma_start(f32(Qf[j][n][65:66, :]), cum_d[bass.ds(2 * i + j, 1), 1, n]).then_inc(S("fox_cum"), 16)
                    for j in range(4):
                        load_panel("fox", 4, i, j)
                    sp.wait_ge(S("att_ylo"), fox.head(i, 2) + PRIMED["att_ylo"])
                    for n in range(2):
                        sp.dma_start(y_d[1][i, n], f32(ysf[n][:, :])).then_inc(S("att_stored"), 16)
            if on("mem2"):
                mem_heads(1)
            if on("out2"):
                out_proj(1)
                with sp.Fori(0, 4) as i:
                    for j in range(2):
                        sp.wait_ge(S("ln2_out"), 2 * i + j + 1)
                        sp.dma_start(out[2 * i + j], tmp[j][:, 0:T]).then_inc(S(f"out_stored{j}"), 16)
                for j in range(2):
                    sp.wait_ge(S(f"out_stored{j}"), 64)
            if dbg is not None:
                dbg(sp, S, at)

        def pool_program(gp):
            def split(n, i=0, per=0, after=None):
                q = n + per * i
                b = n % 2
                gp.wait_ge(S(f"loaded{b}"), 16 * (n // 2 + 1 + (per // 2) * i))
                if n >= 2:
                    gp.wait_ge(S("panel_done"), q - 1)
                if after is not None:
                    gp.wait_ge(*after)
                nc.gpsimd.tensor_tensor(whi[b][:, :], raw[b][:, :], onesf[:, 0:1].to_broadcast([P, PW]), ALU.mult).then_inc(S("split_hi"), 1)
                gp.wait_ge(S("split_hi"), q + 1)
                nc.gpsimd.tensor_tensor(wlo[b][:, :], raw[b][:, :], f32(whi[b][:, :]), ALU.subtract).then_inc(S("split"), 1)

            def splits(stage, per, count, i=0, first=0, after=None):
                for j in range(first, first + count):
                    split(P0[stage] + SPLIT_LEAD + j, i, per, after if j == first else None)

            gp.wait_ge(S("ones"), 1)
            for n in range(SPLIT_LEAD):
                split(n)
            with gp.Fori(0, 2) as l:
                splits("mem", 8, 8, l)
            for stage in ("lat", "f"):
                if on(stage):
                    splits(stage, 0, 4)
            if on("gates"):
                gp.wait_ge(S("rope_loaded"), 32)

                def rope_unit(i, u):
                    w = (T, KEYS)[u % 2]
                    a, b = tmp[0], tmp[1]
                    r = slice(64, 96)
                    gp.wait_ge(S("split"), 8 * i + (P0["gates"] + SPLIT_LEAD + 2 * u))
                    gp.wait_ge(S("prep_swap"), 4 * i + u + 1)
                    nc.gpsimd.tensor_tensor(a[r, 0:w], a[r, 0:w], cosT[r, 0:w], ALU.mult).then_inc(S("prep_cos"), 1)
                    gp.wait_ge(S("prep_cos"), 4 * i + u + 1)
                    gp.wait_ge(S("prep_sin"), 4 * i + u + 1)
                    nc.gpsimd.tensor_tensor(a[r, 0:w], a[r, 0:w], b[r, 0:w], ALU.add).then_inc(S("prep_rot"), 1)

                with gp.Fori(0, 4) as i:
                    for u in range(4):
                        rope_unit(i, u)
                        splits("gates", 8, 2, i, 2 * u, after=(S("prep_rot"), 4 * i + u + 1))
            if on("v"):
                splits("v", 0, 1)
            if on("dft"):
                with gp.Fori(0, 2) as i:
                    splits("dft", 10, 10, i)
            for stage, per, n in (("merge", 2, 4), ("wout", 2, 4), ("mlp", 16, 4)):
                if on(stage):
                    with gp.Fori(0, n) as i:
                        splits(stage, per, per, i)
            if on("pool"):
                splits("pool", 0, 20)
            for stage, per, n in (("mem1", 4, 2), ("out1", 6, 2), ("forget", 1, 1), ("fox", 4, 8), ("mem2", 4, 2),
                                  ("out2", 6, 2)):
                if on(stage):
                    if n == 1:
                        splits(stage, 0, 1)
                    else:
                        with gp.Fori(0, n) as i:
                            splits(stage, per, per, i)

        def pe_program(pe):
            def panel(stage, per, i, j):
                if isinstance(i, int):
                    j, i = j + per * i, 0
                n = P0[stage] + j
                pe.wait_ge(S("split"), n + per * i + 1)
                return whi[n % 2], wlo[n % 2]

            def done(last):
                last.then_inc(S("panel_done"), 1)

            def blocks(o, wh, wl, xh, xl, ks, first, last, k0=0, w=T, off=0, ready=None):
                for n, b in enumerate(ks):
                    c = off + P * b
                    if ready is not None:
                        ready(k0 + n)
                    for h in range(0, w, HALF):
                        e = min(h + HALF, w)
                        st, sp_ = first and n == 0, last and n == len(ks) - 1
                        ins = mm3(o[:, h:e], wh[:, c:c + P], wl[:, c:c + P], xh[:, k0 + n, h:e], xl[:, k0 + n, h:e], st, sp_)
                return ins

            def tile(stage, per, i, j, tiles, t, xh, xl, ready=None):
                wh, wl = panel(stage, per, i, j)
                o = pair(pe, stage, tiles, i, t)
                done(blocks(o, wh, wl, xh, xl, range(KT), True, True, ready=ready))

            pe.wait_ge(S("memt_lo"), 1)
            with pe.Fori(0, 2) as l:
                for hd in range(MH):
                    wh, wl = panel("mem", 8, l, hd)
                    o = pair(pe, "mem", 4, l, hd)
                    done(blocks(o, wh, wl, Mhi, Mlo, range(KT), True, True, w=CTX))
                for n in range(4):
                    wh, wl = panel("mem", 8, l, 4 + n)
                    if n == 0:
                        pe.wait_ge(S("mv_lo"), l)
                    for tt in range(2):
                        for k in range(2):
                            kt = 2 * n + k
                            last = mm3(ps[:, (4 + tt) * HALF:(5 + tt) * HALF], Mhi[:, kt, tt * P:tt * P + P],
                                       Mlo[:, kt, tt * P:tt * P + P], whi_of(wh, k), whi_of(wl, k), kt == 0, kt == 7)
                    done(last)
            pe.wait_ge(S("ones"), 1)
            pe.wait_ge(S("ada_used"), 8)
            pe.wait_ge(S("ada_c"), 8)
            for n in range(16):
                nc.tensor.matmul(ps[:, 6 * HALF + n:6 * HALF + n + 1], accx[:, P * n:P * n + P], onesf[:, 0:1], start=True, stop=True)
            for n in range(16):
                last = nc.tensor.matmul(ps[:, 6 * HALF + 48 + n:6 * HALF + 49 + n], accc[:, P * n:P * n + P], onesf[:, 0:1], start=True, stop=True)
            last.then_inc(S("ada_cols"), 1)
            pe.wait_ge(S("mv_lo"), 2)
            pe.wait_ge(S("sq_acc"), 8)
            for h in range(2):
                nc.tensor.matmul(ps[:, (4 + h) * HALF:(5 + h) * HALF], onesf[:, :], acc[:, h * HALF:(h + 1) * HALF], start=True, stop=True)
            pe.wait_ge(S("sq_acc"), 16)
            nc.tensor.matmul(ps[:, 7 * HALF:7 * HALF + CTX], onesf[:, :], acc[:, T:KEYS], start=True, stop=True).then_inc(S("norm_sum"), 1)
            if on("lat"):
                for t in range(4):
                    if t < 2:
                        tile("lat", 4, 0, t, 4, t, Hhi, Hlo, ready=(lambda k: pe.wait_ge(S("ap_lo"), k + 1)) if t == 0 else None)
                    else:
                        wh, wl = panel("lat", 4, 0, t)
                        o = pair(pe, "lat", 4, 0, t)
                        blocks(o, wh, wl, Hhi, Hlo, range(KT), True, True)
                        pe.wait_ge(S("ap_lo"), 16)
                        o = ps[:, (2 + t) * HALF:(2 + t) * HALF + CTX]
                        done(blocks(o, wh, wl, HChi, HClo, range(KT), True, True, w=CTX))
            if on("f"):
                for n in range(4):
                    wh, wl = panel("f", 4, 0, n)
                    for tt in range(KT):
                        if n == 0:
                            if tt in (0, 2):
                                pe.wait_ge(g_free[tt // 2], (T0["lat"] + 4) // 2)
                            if tt == 4:
                                pe.wait_ge(S("lat_ctx"), 2)
                        for k in range(2):
                            kt = 2 * n + k
                            last = mm3(ps[:, tt * HALF:(tt + 1) * HALF], Hhi[:, kt, tt * P:tt * P + P], Hlo[:, kt, tt * P:tt * P + P],
                                       whi_of(wh, k), whi_of(wl, k), kt == 0, kt == 7)
                        if n == 3 and tt < 7:
                            last.then_inc(S("rows_full"), 1)
                    done(last)
                pe.wait_ge(S("f_lo"), 8)
                pe.wait_ge(S("ada_used"), 24)
                for n in range(32):
                    last = nc.tensor.matmul(ps[:, 6 * HALF + 16 + n:6 * HALF + 17 + n], acc2[:, P * n:P * n + P], onesf[:, 0:1], start=True, stop=True)
                last.then_inc(S("ada_cols"), 1)
                pe.wait_ge(S("lat_sq"), 1)
                for h in range(2):
                    last = nc.tensor.matmul(ps[:, (4 + h) * HALF:(5 + h) * HALF], onesf[:, :], acc[:, h * HALF:(h + 1) * HALF], start=True, stop=True)
                last.then_inc(S("norm_sum"), 1)
                pe.wait_ge(S("lat_kvsq"), 1)
                for h in range(0, KEYS, HALF):
                    e = min(h + HALF, KEYS)
                    last = nc.tensor.matmul(ps[:, h:e], onesf[:, :], tmp[1][:, h:e], start=True, stop=True)
                last.then_inc(S("norm_sum"), 1)
            if on("gates"):
                pe.wait_ge(S("norm_ms"), 4)
                with pe.Fori(0, 4) as i:
                    for hd in range(2):
                        for u in range(2):
                            n = 2 * hd + u
                            w = (T, KEYS)[u]
                            wh, wl = panel("gates", 8, i, 4 * hd + 2 * u)
                            if hd == 0 and u == 0:
                                pe.wait_ge(S("qn_lo"), 1)
                                pe.wait_ge(S("kvn_lo"), 1)
                            pe.wait_ge(S("prep_ms"), 4 * i + n)
                            for c in range(0, w, HALF):
                                e = min(c + HALF, w)
                                if u == 0:
                                    for k in range(2):
                                        last = mm3(ps[0:QK, 4 * HALF + c:4 * HALF + e], wh[:, QK * k:QK * k + QK], wl[:, QK * k:QK * k + QK],
                                                   qnhi[:, k, c:e], qnlo[:, k, c:e], k == 0, k == 1)
                                else:
                                    last = mm3(ps[:, 4 * HALF + c:4 * HALF + e], wh[:, 0:P], wl[:, 0:P], kvhi[:, c:e], kvlo[:, c:e], True, True)
                            done(last)
                            tile("gates", 8, i, 4 * hd + 2 * u + 1, 4, n, Hhi, Hlo)
                            pe.wait_ge(S("prep_sq"), 4 * i + n + 1)
                            for c in range(0, w, HALF):
                                e = min(c + HALF, w)
                                last = nc.tensor.matmul(ps[0:QK, 4 * HALF + c:4 * HALF + e], onesf[0:QK, 0:QK], acc[0:QK, c:e], start=True, stop=True)
                            last.then_inc(S("prep_ss"), 1)
            if on("v"):
                wh, wl = panel("v", 1, 0, 0)
                for tt in range(10):
                    if tt == 0:
                        for q in range(2):
                            pe.wait_ge(g_free[q], (T0["gates"] + 16) // 2)
                    if tt == 4:
                        pe.wait_ge(S("prep_ms"), 16)
                    if tt >= 8:
                        pe.wait_ge(S("v_lo"), tt - 7)
                    last = mm3(ps[:, (tt % 8) * HALF:(tt % 8 + 1) * HALF], kvhi[:, tt * P:tt * P + P], kvlo[:, tt * P:tt * P + P],
                               wh[:, 0:HALF], wl[:, 0:HALF], True, True)
                    if tt < 9:
                        last.then_inc(S("rows_full"), 1)
                done(last)
            if on("dft"):
                pe.wait_ge(S("v_lo"), 10)
                with pe.Fori(0, 2) as h:
                    for part in range(2):
                        for n in range(4):
                            wh, wl = panel("dft", 10, h, 4 * part + n)
                            if n == 0:
                                pe.wait_ge(S("fm_lo"), 4 * h)
                                pe.wait_ge(S("ab_lo"), 8 * h)
                            for g in range(NG):
                                for k in range(2):
                                    kt = 2 * n + k
                                    last = mm3(ps[:, (4 * part + g) * HALF:(4 * part + g + 1) * HALF], Fhi[:, kt, P * g:P * g + P],
                                               Flo[:, kt, P * g:P * g + P], whi_of(wh, k), whi_of(wl, k), kt == 0, kt == 7)
                            done(last)
                    for part in range(2):
                        wh, wl = panel("dft", 10, h, 8 + part)
                        for g in range(NG):
                            pe.wait_ge(S("ab_lo"), 8 * h + (4 if part == 0 else 5 + g))
                            last = mm3(ps[:, g * HALF:(g + 1) * HALF], wh[:, 0:P], wl[:, 0:P], ABhi[:, g, part, :], ABlo[:, g, part, :],
                                       part == 0, part == 1)
                        done(last)
            if on("mla"):
                pe.wait_ge(S("fm_lo"), 8)
                pe.wait_ge(S("consts"), 32)
                mla.loaded = lambda e, i, j: e.wait_ge(S(f"mla_loaded{j}"), 96 * i + 96)
                scores, flip_max, body = att_pe(pe, mla)
                with pe.Fori(0, 2) as i:
                    scores(i, 0)
                    flip_max(i, 0)
                    for j in range(4):
                        body(i, j)
            if on("merge"):
                pe.wait_ge(S("fa_loaded"), 64)
                with pe.Fori(0, 4) as i:
                    for j in range(2):
                        wh, wl = panel("merge", 2, i, j)
                        for n, X in enumerate((Fm, At)):
                            o = pair(pe, "merge", 4, i, 2 * j + n)
                            last = blocks(o, wh, wl, X[0], X[1], range(4 * n, 4 * n + 4), True, True)
                        done(last)
            if on("wout"):
                with pe.Fori(0, 4) as i:
                    for j in range(2):
                        if j == 0:
                            pe.wait_ge(S("y_lo"), 8)
                        tile("wout", 2, i, j, 2, j, Yhi, Ylo)
                pe.wait_ge(S("n2_acc"), 8)
                for h in range(2):
                    last = nc.tensor.matmul(ps[:, (4 + h) * HALF:(5 + h) * HALF], onesf[:, :], acc[:, h * HALF:(h + 1) * HALF], start=True, stop=True)
                last.then_inc(S("norm_sum"), 1)
            if on("mlp"):
                with pe.Fori(0, 4) as i:
                    for t in range(8):
                        tile("mlp", 16, i, t, 16, t, Hb[0], Hb[1], ready=(lambda k: pe.wait_ge(S("ap_lo"), 16 + k + 1)) if t == 0 else None)
                    for t in range(8):
                        tile("mlp", 16, i, 8 + t, 16, 8 + t, Uhi, Ulo,
                             ready=(lambda k: pe.wait_ge(S("u_lo"), 8 * i + k + 1)) if t == 0 else None)
            if on("pool"):
                for g in range(4):
                    for t in range(4):
                        tile("pool", 5, g, t, 6, t, Hb[0], Hb[1], ready=(lambda k: pe.wait_ge(S("x2_lo"), k + 1)) if g == 0 and t == 0 else None)
                    wh, wl = panel("pool", 5, g, 4)
                    for t in range(2):
                        o = pair(pe, "pool", 6, g, 4 + t)
                        pe.wait_ge(S("pm_lo"), 2 * g + 2)
                        last = blocks(o, wh, wl, PMhi, PMlo, (2 * t, 2 * t + 1), True, True)
                    done(last)

            def mem_heads(l):
                st = f"mem{l + 1}"
                pe.wait_ge(S("identr"), 2)
                with pe.Fori(0, 2) as i:
                    for j in range(2):
                        tile(st, 4, i, j, 8, j, Hb[0], Hb[1])
                    for j in range(2):
                        evicted(pe, st, 8, i, j)
                        if j == 0:
                            pe.wait_ge(S("mem_kv"), 256 * l + 128 * i + 128)
                        for h in range(2):
                            o = 4 + 2 * h
                            if j == 1:
                                pe.wait_ge(S("att_max"), mem_c(l, i) + h + 1)
                            for q in range(4):
                                qc = slice((4 * h + q) * P, (4 * h + q + 1) * P)
                                last = mm3(ps[:, o * HALF + 256 * q:o * HALF + 256 * q + 256], Qm[j][0][:, qc], Qm[j][1][:, qc],
                                           Km[j][0][:, :], Km[j][1][:, :], True, True)
                            last.then_inc(S("att_s"), 1)
                    tile(st, 4, i, 2, 8, 2, Hb[0], Hb[1])
                    pe.wait_ge(S("att_mx"), mem_f(l, i) + 1)
                    nc.tensor.transpose(ps[0:16, 4 * HALF:4 * HALF + P], mxf[:, 0:16], ident[:, :]).then_inc(S("att_mt"), 1)
                    tile(st, 4, i, 3, 8, 3, Hb[0], Hb[1])
                    for j in range(2):
                        for kt in range(2):
                            n = mem_u(l, i) + 2 * j + kt
                            o = 4 + 2 * kt
                            if j == 0:
                                pe.wait_ge(S("att_row"), mem_r(l, i) + 64)
                            else:
                                pe.wait_ge(S("mem_exp"), 8 * l + 4 * i + kt + 1)
                            for c in range(2):
                                cs = slice(c * HALF, (c + 1) * HALF)
                                b = ps[:, (o + c) * HALF:(o + c + 1) * HALF]
                                mm3(b, Km[j][0][:, kt * P:kt * P + P], Km[j][1][:, kt * P:kt * P + P], Qm[j][0][:, cs], Qm[j][1][:, cs], True, False)
                                last = nc.tensor.matmul(b, onesr[0:2, :], mr[j][0:2, cs], start=False, stop=True)
                            last.then_inc(S("att_st"), 1)
                    for j in range(2):
                        pe.wait_ge(S("att_lo"), mem_u(l, i) + 2 * j + 2 + PRIMED["att_lo"])
                        o, sums = pair(pe, st, 8, i, 4 + 2 * j), pair(pe, st, 8, i, 5 + 2 * j)
                        for c in range(2):
                            cs = slice(c * HALF, (c + 1) * HALF)
                            for kt in range(2):
                                E = Em[2 * j + kt]
                                mm3(o[:, cs], Vm[j][0][:, kt, :], Vm[j][1][:, kt, :], E[0][:, cs], E[1][:, cs], kt == 0, kt == 1)
                                for n in range(2):
                                    last = nc.tensor.matmul(sums[:, cs], onesr[:, :], E[n][:, cs], start=kt == 0 and n == 0, stop=kt == 1 and n == 1)
                        last.then_inc(S("mem_pv"), 1)

            def out_proj(l):
                st = f"out{l + 1}"
                with pe.Fori(0, 2) as i:
                    pe.wait_ge(S("yb"), 32 * (l + 1))
                    have = -1
                    for t in range(4):
                        o = pair(pe, st, 4, i, t)
                        b = 12 * t
                        while b < 12 * t + 12:
                            j = b // 8
                            if j != have:
                                wh, wl = panel(st, 6, i, j)
                                have = j
                            e = min(8 * j + 8, 12 * t + 12)
                            last = blocks(o, wh, wl, Yb[0], Yb[1], range(b - 8 * j, e - 8 * j), b == 12 * t, e == 12 * t + 12, k0=b - 12 * t)
                            if e == 8 * j + 8:
                                done(last)
                            else:
                                last.then_inc(S("out_mid"), 1)
                            b = e
                for n, what in enumerate(("ln_acc", "ln_vacc")):
                    pe.wait_ge(S(what), 8 * (l + 1))
                    for h in range(2):
                        last = nc.tensor.matmul(ps[:, (4 + h) * HALF:(5 + h) * HALF], onesf[:, :], acc[:, h * HALF:(h + 1) * HALF], start=True, stop=True)
                    last.then_inc(S("norm_sum"), 1)

            if on("mem1"):
                mem_heads(0)
            if on("out1"):
                out_proj(0)
            if on("forget"):
                wh, wl = panel("forget", 1, 0, 0)
                pe.wait_ge(S("norm_ms"), 6)
                done(blocks(ps[:, 4 * HALF:6 * HALF], wh, wl, Hb[0], Hb[1], range(KT), True, True,
                            ready=lambda k: pe.wait_ge(S("ap_lo"), 24 + k + 1)))
            if on("fox"):
                fox.loaded = lambda e, i, j: e.wait_ge(S("fox_cum"), 128 * i + 128)
                pe.wait_ge(S("logits_read"), 1)
                pe.wait_ge(S("aug"), 20)
                pe.wait_ge(S("identr"), 3)
                scores, flip_max, body = att_pe(pe, fox)
                with pe.Fori(0, 8) as i:
                    for j in range(3):
                        tile("fox", 4, i, j, 20, j, Hb[0], Hb[1])
                    evicted(pe, "fox", 20, i, 0)
                    evicted(pe, "fox", 20, i, 1)
                    scores(i, 0)
                    evicted(pe, "fox", 20, i, 2)
                    pe.wait_ge(S("att_out"), fox.head(i, 0) + PRIMED["att_out"])
                    for k in range(KT):
                        last = nc.tensor.transpose(ps[:, 4 * HALF + P * k:4 * HALF + P * k + P], vtf[:, P * k:P * k + P], ident[:, :])
                    last.then_inc(S("fox_vflip"), 1)
                    flip_max(i, 0)
                    tile("fox", 4, i, 3, 20, 3, Hb[0], Hb[1])
                    pe.wait_ge(S("fox_vlo"), 2 * i + 2)
                    for j in range(2):
                        body(i, j)
            if on("mem2"):
                mem_heads(1)
            if on("out2"):
                out_proj(1)

        def col(name, k=0):
            return cols[:, COLS[name] + k:COLS[name] + k + 1]

        NORM = {"n1": 0, "n1c": 1, "latq": 2, "latkv": 3, "n2": 4, "ln0": 5, "ln1": 6}
        APPLY = {"n1": 0, "n1c": 8, "n2": 16, "ln0": 24, "ln1": 32}

        def apply_dve(dve, s, n, src, w, lo, hi=None, c0=0):
            def scaled(k):
                if k >= 2:
                    dve.wait_ge(S("ap_lo"), APPLY[s] + k - 1)
                nc.vector.tensor_tensor(tmp[k % 2][:, c0:c0 + w], src(k), rs[:, c0:c0 + w], ALU.mult).then_inc(S("ap_t"), 1)

            def low(k):
                dve.wait_ge(S("ap_hi"), APPLY[s] + k + 1)
                nc.vector.tensor_tensor(lo(k), tmp[k % 2][:, c0:c0 + w], f32(hi(k)), ALU.subtract).then_inc(S("ap_lo"), 1)

            for k in range(n):
                scaled(k)
                if k >= 1:
                    low(k - 1)
            low(n - 1)

        def apply_act(act, s, n, w, hi, scale, shift, c0=0):
            for k in range(n):
                b = tmp[k % 2][:, c0:c0 + w]
                act.wait_ge(S("ap_t"), APPLY[s] + k + 1)
                nc.scalar.activation(b, b, ACT.Identity, scale=scale(k), bias=shift(k)).then_inc(S("ap_full"), 1)
                act.wait_ge(S("ap_full"), APPLY[s] + k + 1)
                nc.scalar.activation(hi(k), b, ACT.Copy).then_inc(S("ap_hi"), 1)

        def root(act, s, rows, a, b):
            act.wait_ge(S("norm_ms"), NORM[s] + 1)
            nc.scalar.activation(rs[0:rows, a:b], rs[0:rows, a:b], ACT.Sqrt).then_inc(S("norm_root"), 1)

        def mean_square(dve, s, src, count, eps, rows, a, b):
            nc.vector.tensor_scalar(rs[0:rows, a:b], src, 1.0 / count, eps, ALU.mult, ALU.add).then_inc(S("norm_ms"), 1)
            dve.wait_ge(S("norm_root"), NORM[s] + 1)
            nc.vector.reciprocal(rs[0:rows, a:b], rs[0:rows, a:b]).then_inc(S("norm_rs"), 1)
            dve.wait_ge(S("norm_rs"), NORM[s] + 1)

        def act_program(act):
            def copy(dst, src, sem, func=ACT.Copy, **kw):
                nc.scalar.activation(dst, src, func, **kw).then_inc(sem, 1)

            act.wait_ge(S("memt_loaded"), 16)
            copy(Mhi[:, :, :], Mraw[:, :, :], S("memt_hi"))
            act.wait_ge(S("cols_loaded"), 16)
            copy(sigc[:, :], cols[:, 0:16], S("sigc"), ACT.Sigmoid)
            act.wait_ge(S("x_loaded"), 16)
            for k in range(KT):
                if k >= 2:
                    act.wait_ge(S("sq_acc"), k - 1)
                copy(tmp[k % 2][:, 0:T], XT[:, k, :], S("sq"), ACT.Square)
            act.wait_ge(S("ctx_loaded"), 16)
            for k in range(KT):
                if k >= 2:
                    act.wait_ge(S("sq_acc"), 8 + k - 1)
                copy(tmp[k % 2][:, T:KEYS], CT[:, k, :], S("sq"), ACT.Square)
            with act.Fori(0, 2) as l:
                act.wait_ge(S("mk_stored"), 32 * l)
                for hd in range(MH):
                    panels_done(act, "mem", 8, l, hd)
                    copy(mks[0][:, hd, :], pair_of("mem", hd)[0][:, 0:CTX], S("mk_hi"))
                panels_done(act, "mem", 8, l, 7)
                act.wait_ge(S("mv_stored"), 32 * l)
                copy(mvs[0][:, :, :], ps[:, 4 * HALF:6 * HALF].rearrange("p (a b) -> p a b", a=2), S("mv_hi"))
            root(act, "n1", P, 0, T)
            root(act, "n1c", P, T, KEYS)
            act.wait_ge(S("mods"), 4)
            act.wait_ge(S("mk_stored"), 64)
            act.wait_ge(S("mv_stored"), 64)
            apply_act(act, "n1", KT, T, lambda k: Hhi[:, k, :], lambda k: scx[:, k:k + 1], lambda k: modx[:, k:k + 1])
            apply_act(act, "n1c", KT, CTX, lambda k: HChi[:, k, :], lambda k: scc[:, k:k + 1], lambda k: modc[:, k:k + 1], c0=T)
            if on("lat"):
                for t in range(4):
                    panels_done(act, "lat", 4, 0, t)
                    g, free = pair_of("lat", t)
                    if t < 2:
                        copy(ql[:, t, :], g, free)
                    else:
                        r, dst = ((slice(0, P), kvl), (slice(64, QK), kr))[t - 2]
                        copy(dst[r, 0:T], g[r, :], free)
                        copy(dst[r, T:KEYS], ps[r, (2 + t) * HALF:(2 + t) * HALF + CTX], S("lat_ctx"))
            if on("f"):
                for tt in range(KT):
                    if tt < 7:
                        act.wait_ge(S("rows_full"), tt + 1)
                    else:
                        panels_done(act, "f", 4, 0, 3)
                    copy(Fhi[:, tt, :], ps[:, tt * HALF:(tt + 1) * HALF], S("rows_hi"))
                evicted(act, "lat", 4, 0, 0)
                evicted(act, "lat", 4, 0, 1)
                act.wait_ge(S("ap_lo"), 16)
                for k in range(2):
                    copy(tmp[k][:, 0:T], ql[:, k, :], S("lat_s"), ACT.Square)
                evicted(act, "lat", 4, 0, 2)
                act.wait_ge(S("lat_ctx"), 2)
                act.wait_ge(S("lat_sq"), 1)
                copy(tmp[1][:, :], kvl[:, :], S("lat_kvsq"), ACT.Square)
                root(act, "latq", P, 0, T)
                for k in range(2):
                    act.wait_ge(S("lat_t"), k + 1)
                    copy(ql[:, k, :], ql[:, k, :], S("lat_full"), scale=col("qng", k))
                    act.wait_ge(S("lat_full"), k + 1)
                    copy(qnhi[:, k, :], ql[:, k, :], S("lat_hi"))
                root(act, "latkv", P, 0, KEYS)
                act.wait_ge(S("lat_t"), 3)
                copy(kvl[:, :], kvl[:, :], S("lat_full"), scale=col("kvng"))
                act.wait_ge(S("lat_full"), 3)
                copy(kvhi[:, :], kvl[:, :], S("lat_hi"))
            if on("gates"):
                evicted(act, "lat", 4, 0, 3)
                with act.Fori(0, 4) as i:
                    for u in range(4):
                        w = (T, KEYS)[u % 2]
                        panels_done(act, "gates", 8, i, 2 * u)
                        act.wait_ge(S("prep_lo"), 4 * i + u)
                        raw_ = ps[:, 4 * HALF:4 * HALF + w]
                        if u % 2 == 0:
                            copy(tmp[0][0:QK, 0:w], raw_[0:QK, :], S("prep_a"), scale=cols[0:QK, COLS["qg"]:COLS["qg"] + 1])
                            copy(acc[0:QK, 0:w], raw_[0:QK, :], S("prep_sq"), ACT.Square)
                        else:
                            lo_, up = slice(0, NOPE), slice(NOPE, QK)
                            kg = COLS["kg"]
                            copy(tmp[0][lo_, 0:w], raw_[lo_, :], S("prep_x"), scale=cols[lo_, kg:kg + 1])
                            copy(tmp[0][up, 0:w], kr[up, :], S("prep_a"), scale=cols[up, kg:kg + 1])
                            copy(acc[up, 0:w], kr[up, :], S("prep_x"), ACT.Square)
                            copy(acc[lo_, 0:w], raw_[lo_, :], S("prep_sq"), ACT.Square)
                        panels_done(act, "gates", 8, i, 2 * u + 1)
                        g, free = pair_of("gates", u)
                        act.wait_ge(S(f"gate_stored{u % 2}"), 32 * i + 16 * (u // 2))
                        copy(gst[u % 2][:, :], g, free, ACT.Sigmoid, bias=cols[:, bass.ds(4 * i + (COLS["b_gate"] + u), 1)])
                        act.wait_ge(S("prep_ms"), 4 * i + u + 1)
                        copy(rs[0:QK, 0:w], rs[0:QK, 0:w], S("prep_root"), ACT.Sqrt)
                        act.wait_ge(S("prep_full"), 4 * i + u + 1)
                        act.wait_ge(S("prep_stored"), 128 * i + 32 * u)
                        copy(phd[0][0:QK, 0:w], tmp[0][0:QK, 0:w], S("prep_hi"))
            if on("v"):
                act.wait_ge(S("prep_stored"), 512)
                for n in range(2):
                    act.wait_ge(S(f"gate_stored{n}"), 128)
                for tt in range(10):
                    if tt < 9:
                        act.wait_ge(S("rows_full"), 7 + tt + 1)
                    else:
                        panels_done(act, "v", 1, 0, 0)
                    copy(Vhi[:, tt, :], ps[:, (tt % 8) * HALF:(tt % 8 + 1) * HALF], S("rows_hi"))
            if on("dft"):
                with act.Fori(0, 2) as h:
                    for part in range(2):
                        panels_done(act, "dft", 10, h, 4 * part + 3)
                        for g in range(NG):
                            copy(ABhi[:, g, part, :], ps[:, (4 * part + g) * HALF:(4 * part + g + 1) * HALF], S("dft_hi"))
                    panels_done(act, "dft", 10, h, 9)
                    act.wait_ge(S("fm_stored"), 32 * h)
                    for g in range(NG):
                        copy(fms[0][:, g, :], ps[:, g * HALF:(g + 1) * HALF], S("dft_hi"))
            if on("mla"):
                act.wait_ge(S("fm_lo"), 8)
                act.wait_ge(S("consts"), 32)
                copy(identr[:, :], ident[:, :], S("identr"))
                copy(onesr[:, :], onesf[:, :], S("identr"))
                rows_hi, rows_send, body = att_act(act, mla)
                with act.Fori(0, 2) as i:
                    rows_hi(i, 0)
                    rows_send(i, 0)
                    for j in range(4):
                        body(i, j)
            if on("merge"):
                act.wait_ge(S("att_pv"), 80 + PRIMED["att_pv"])
                with act.Fori(0, 4) as i:
                    for j in range(2):
                        act.wait_ge(S("y_full"), 2 * i + j + 1)
                        copy(Yhi[:, 2 * i + j, :], mm1[:, :], S("y_hi"))
            if on("wout"):
                with act.Fori(0, 4) as i:
                    for j in range(2):
                        evicted(act, "wout", 2, i, j)
                        copy(tmp[j][:, 0:T], X1[:, 2 * i + j, :], S("n2_sq"), ACT.Square)
                root(act, "n2", P, 0, T)
                act.wait_ge(S("mods"), 6)
                apply_act(act, "n2", KT, T, lambda k: Hb[0][:, k, :], lambda k: sc2[:, k:k + 1], lambda k: modx[:, 24 + k:25 + k])
            if on("mlp"):
                with act.Fori(0, 4) as i:
                    for t in range(8):
                        panels_done(act, "mlp", 16, i, t)
                        g, free = pair_of("mlp", t)
                        if t >= 2:
                            act.wait_ge(S("u_lo"), 8 * i + t - 1)
                        copy(tmp[t % 2][:, 0:T], g, free, ACT.Relu)
                        act.wait_ge(S("u_sq"), 8 * i + t + 1)
                        copy(Uhi[:, t, :], tmp[t % 2][:, 0:T], S("u_hi"))
                panels_done(act, "mlp", 64, 0, 63)
                for k in range(KT):
                    evicted(act, "mlp", 16, 3, 8 + k)
                    copy(Hb[0][:, k, :], X1[:, k, :], S("x2_hi"))
            if on("pool"):
                for g4 in range(4):
                    for t in range(2):
                        panels_done(act, "pool", 5, g4, t)
                        g, free = pair_of("pool", t)
                        act.wait_ge(S("pm_lo"), 2 * g4)
                        copy(pu[t][:, 16:], g, free)
                    for t in range(2):
                        panels_done(act, "pool", 5, g4, 2 + t)
                        g, free = pair_of("pool", 2 + t)
                        if t == 1:
                            evicted(act, "pool", 6, g4, 2)
                        copy(sgm[:, :], g, S("pool_sig"), ACT.Sigmoid)
                        act.wait_ge(S("pm_full"), 2 * g4 + t + 1)
                        copy(PMhi[:, t, :], pm_buf(g4, t)[:, 16:], S("pm_hi"))
                    for t in range(2):
                        evicted(act, "pool", 6, g4, 4 + t)
                        act.wait_ge(S(f"pool_stored{t}"), 32 * g4)
                        copy(ys[t][0][:, :], yf[:, :], S("pool_yhi"))

            def mem_heads(l):
                st = f"mem{l + 1}"
                if l == 0:
                    act.wait_ge(S("pool_stored0"), 128)
                    act.wait_ge(S("pool_stored1"), 128)
                else:
                    act.wait_ge(S("att_stored"), 384 + PRIMED["att_stored"])
                with act.Fori(0, 2) as i:
                    for j in range(2):
                        panels_done(act, st, 4, i, j)
                        g, free = pair_of(st, j)
                        copy(Qm[j][0][:, :], g, S("mem_qhi"))
                    panels_done(act, st, 4, i, 2)
                    g, free = pair_of(st, 2)
                    copy(sgq[:, :], g, S("mem_sig"), ACT.Sigmoid)
                    act.wait_ge(S("att_mt"), mem_f(l, i) + 1)
                    copy(mrow[0][0:16, :], ps[0:16, 4 * HALF:4 * HALF + P], S("att_mhi"), scale=-1.0)
                    act.wait_ge(S("att_mlo"), mem_f(l, i) + 1 + PRIMED["att_mlo"])
                    for j in range(2):
                        for n in range(2):
                            nc.scalar.dma_start(f32(mr[j][n:n + 1, :]), f32(mrow[n][8 * j:8 * j + 8, :])).then_inc(S("att_row"), 16)
                    panels_done(act, st, 4, i, 3)
                    g, free = pair_of(st, 3)
                    evicted(act, st, 8, i, 2)
                    copy(sgq[:, :], g, S("mem_sig"), ACT.Sigmoid)
                    for u in range(4):
                        n = mem_u(l, i) + u
                        kt = u % 2
                        act.wait_ge(S("att_st"), n + 1)
                        act.wait_ge(S("att_lo"), n - 1 + PRIMED["att_lo"])
                        copy(tmp[kt][:, 0:T], ps[:, (4 + 2 * kt) * HALF:(6 + 2 * kt) * HALF], S("mem_exp"), ACT.Exp, scale=SCALE["mem"])
                        act.wait_ge(S("mem_exp"), 8 * l + 4 * i + u + 1)
                        copy(Em[u][0][:, :], tmp[kt][:, 0:T], S("att_hi"))
                    for j in range(2):
                        act.wait_ge(S("mem_pv"), 4 * l + 2 * i + j + 1 + PRIMED["mem_pv"])
                        if j == 1:
                            act.wait_ge(S("mem_ylo"), 4 * l + 2 * i + 1)
                        for k in range(2):
                            g, free = pair_of(st, 4 + 2 * j + k)
                            copy((om[:, :], sums_m[j][:, 0:T])[k], g, free)
                        act.wait_ge(S("mem_y"), 3 * (4 * l + 2 * i + j) + 3)
                        act.wait_ge(S("mem_stored"), 128 * l + 64 * i + PRIMED["mem_stored"])
                        copy(ym[j][0][:, :], om[:, :], S("mem_yhi"))

            def out_proj(l):
                act.wait_ge(S("ln_acc"), 8 * (l + 1))
                for k in range(KT):
                    act.wait_ge(S("ln_zc"), 8 * l + k + 1)
                    if k >= 2:
                        act.wait_ge(S("ln_vacc"), 8 * l + k - 1)
                    copy(tmp[k % 2][:, 0:T], Z[:, k, :], S("ln_sq"), ACT.Square)
                root(act, f"ln{l}", P, 0, T)
                gcol, bcol = (lambda k: col("ln_g", 8 * l + k)), (lambda k: col("ln_b", 8 * l + k))
                if l == 0:
                    apply_act(act, "ln0", KT, T, lambda k: Hb[0][:, k, :], gcol, bcol)
                else:
                    for k in range(KT):
                        b = tmp[k % 2][:, 0:T]
                        act.wait_ge(S("ap_t"), APPLY["ln1"] + k + 1)
                        copy(b, b, S("ln2_out"), ACT.Identity, scale=gcol(k), bias=bcol(k))

            if on("mem1"):
                mem_heads(0)
            if on("out1"):
                out_proj(0)
            if on("forget"):
                r = slice(0, FOX)
                act.wait_ge(S("logits_read"), 1)
                copy(tmp[1][r, 0:T], tmp[0][r, 0:T], S("fg"), ACT.Abs)
                act.wait_ge(S("fg"), 1)
                copy(tmp[1][r, 0:T], tmp[1][r, 0:T], S("fg"), ACT.Exp, scale=-1.0)
                act.wait_ge(S("fg"), 2)
                copy(tmp[1][r, 0:T], tmp[1][r, 0:T], S("fg"), ACT.Ln, bias=1.0)
                act.wait_ge(S("cum"), 1)
                copy(nch[0][r, :], ncum[r, :], S("fg"))
            if on("fox"):
                act.wait_ge(S("cum_stored"), 64)
                act.wait_ge(S("consts"), 48)
                copy(maskr[:, :], maskc[:, :], S("identr"))
                rows_hi, rows_send, body = att_act(act, fox)
                with act.Fori(0, 8) as i:
                    for t in range(2):
                        panels_done(act, "fox", 4, i, t)
                        g, free = pair_of("fox", t)
                        for j in range(2):
                            copy((Kf, Qf)[t][j][0][0:64, :], g[64 * j:64 * j + 64, :], S("fox_hi"), scale=(1.0, 64 ** -0.5)[t])
                    panels_done(act, "fox", 4, i, 2)
                    g, free = pair_of("fox", 2)
                    copy(vtf[:, :], g, free)
                    act.wait_ge(S("fox_vflip"), i + 1)
                    for j in range(2):
                        c = slice(64 * j, 64 * j + 64)
                        copy(Vf[j][0][:, :, c], PV.rearrange("p (k d) -> p k d", d=P)[:, :, c], S("fox_vhi"))
                    rows_hi(i, 0)
                    rows_send(i, 0)
                    panels_done(act, "fox", 4, i, 3)
                    g, free = pair_of("fox", 3)
                    act.wait_ge(S("att_ylo"), fox.head(i, 0) + PRIMED["att_ylo"])
                    copy(rs[:, 0:T], g, S("fox_sig"), ACT.Sigmoid)
                    for j in range(2):
                        body(i, j)
            if on("mem2"):
                mem_heads(1)
            if on("out2"):
                out_proj(1)

        def dve_program(dve):
            def sub(lo, x, hi, sem):
                nc.vector.tensor_tensor(lo, x, f32(hi), ALU.subtract).then_inc(sem, 1)

            def tt(o, a, b, op, sem):
                nc.vector.tensor_tensor(o, a, b, op).then_inc(sem, 1)

            nc.vector.memset(onesf[:, :], 1.0).then_inc(S("ones"), 1)
            c = 0
            for name, places in PRIMED.items():
                for _ in range(places):
                    nc.vector.memset(stat[:, c:c + 1], 0.0).then_inc(S(name), 1)
                    c += 1
            dve.wait_ge(S("memt_hi"), 1)
            sub(Mlo[:, :, :], Mraw[:, :, :], Mhi[:, :, :], S("memt_lo"))
            dve.wait_ge(S("sigc"), 1)
            tt(silc[:, :], cols[:, 0:16], sigc[:, :], ALU.mult, S("silc"))
            dve.wait_ge(S("silc"), 1)

            def ada(c, dst, sil0, sem, wait_self):
                for k in range(KT):
                    o = dst
                    w_ = adas[c % 2][:, k, :]
                    s_ = silc[:, sil0 + k:sil0 + k + 1]
                    if k == 0:
                        ins = nc.vector.tensor_scalar(o, w_, s_, None, ALU.mult)
                    else:
                        dve.wait_ge(S("ada_link"), wait_self(k))
                        ins = nc.vector.scalar_tensor_tensor(o, w_, s_, o, ALU.mult, ALU.add)
                    ins.then_inc(S("ada_link") if k < KT - 1 else S(sem), 1)

            dve.wait_ge(S("x_loaded"), 16)
            for k in range(KT):
                dve.wait_ge(S("sq"), k + 1)
                if k == 0:
                    nc.vector.tensor_copy(acc[:, 0:T], tmp[0][:, 0:T]).then_inc(S("sq_acc"), 1)
                else:
                    dve.wait_ge(S("sq_acc"), k)
                    tt(acc[:, 0:T], acc[:, 0:T], tmp[k % 2][:, 0:T], ALU.add, S("sq_acc"))
            for k in range(KT):
                dve.wait_ge(S("sq"), 8 + k + 1)
                if k == 0:
                    nc.vector.tensor_copy(acc[:, T:KEYS], tmp[0][:, T:KEYS]).then_inc(S("sq_acc"), 1)
                else:
                    dve.wait_ge(S("sq_acc"), 8 + k)
                    tt(acc[:, T:KEYS], acc[:, T:KEYS], tmp[k % 2][:, T:KEYS], ALU.add, S("sq_acc"))
            with dve.Fori(0, 2) as l:
                for hd in range(MH):
                    dve.wait_ge(S(f"ada_loaded{hd % 2}"), 32 * l + 16 * (hd // 2 + 1))
                    c = 4 * l + hd
                    ada(hd, accc[:, bass.ds(256 * c, 256)], 8, "ada_c", lambda k: 14 * (4 * l + hd) + k)
                    ada(hd, accx[:, bass.ds(256 * c, 256)], 0, "ada_used", lambda k: 14 * (4 * l + hd) + 7 + k)
                    dve.wait_ge(S("mk_hi"), 4 * l + hd + 1)
                    g, free = pair_of("mem", hd)
                    sub(mks[1][:, hd, :], g[:, 0:CTX], mks[0][:, hd, :], free)
                dve.wait_ge(S("mv_hi"), l + 1)
                sub(mvs[1][:, :, :], ps[:, 4 * HALF:6 * HALF].rearrange("p (a b) -> p a b", a=2), mvs[0][:, :, :], S("mv_lo"))
            dve.wait_ge(S("ada_cols"), 1)
            m6 = 6 * HALF
            ab = COLS["ada_b"]
            tt(modx[:, 0:16], ps[:, m6:m6 + 16], cols[:, ab:ab + 16], ALU.add, S("mods"))
            tt(modc[:, 0:16], ps[:, m6 + 48:m6 + 64], cols[:, ab:ab + 16], ALU.add, S("mods"))
            dve.wait_ge(S("mods"), 2)
            n1 = cols[:, COLS["n1"]:COLS["n1"] + 8]
            nc.vector.scalar_tensor_tensor(scx[:, :], modx[:, 8:16], 1.0, n1, ALU.add, ALU.mult).then_inc(S("mods"), 1)
            nc.vector.scalar_tensor_tensor(scc[:, :], modc[:, 8:16], 1.0, n1, ALU.add, ALU.mult).then_inc(S("mods"), 1)
            dve.wait_ge(S("norm_sum"), 1)
            mean_square(dve, "n1", ps[:, 4 * HALF:6 * HALF], D, EPS, P, 0, T)
            mean_square(dve, "n1c", ps[:, 7 * HALF:7 * HALF + CTX], D, EPS, P, T, KEYS)
            apply_dve(dve, "n1", KT, lambda k: XT[:, k, :], T, lambda k: Hlo[:, k, :], lambda k: Hhi[:, k, :])
            apply_dve(dve, "n1c", KT, lambda k: CT[:, k, :], CTX, lambda k: HClo[:, k, :], lambda k: HChi[:, k, :], c0=T)
            if on("f"):
                for c in range(8, 24):
                    dve.wait_ge(S(f"ada_loaded{c % 2}"), 16 * (c // 2 + 1))
                    ada(c, acc2[:, 256 * (c - 8):256 * (c - 7)], 0, "ada_used", lambda k: 112 + 7 * (c - 8) + k)
                for tt_ in range(KT):
                    dve.wait_ge(S("rows_hi"), tt_ + 1)
                    sub(Flo[:, tt_, :], ps[:, tt_ * HALF:(tt_ + 1) * HALF], Fhi[:, tt_, :], S("f_lo"))
                dve.wait_ge(S("lat_s"), 2)
                tt(acc[:, 0:T], tmp[0][:, 0:T], tmp[1][:, 0:T], ALU.add, S("lat_sq"))
                dve.wait_ge(S("ada_cols"), 2)
                tt(modx[:, 16:48], ps[:, m6 + 16:m6 + 48], cols[:, ab + 16:ab + 48], ALU.add, S("mods"))
                dve.wait_ge(S("mods"), 5)
                n2 = cols[:, COLS["n2"]:COLS["n2"] + 8]
                nc.vector.scalar_tensor_tensor(sc2[:, :], modx[:, 32:40], 1.0, n2, ALU.add, ALU.mult).then_inc(S("mods"), 1)
                dve.wait_ge(S("norm_sum"), 2)
                mean_square(dve, "latq", ps[:, 4 * HALF:6 * HALF], QL, EPS, P, 0, T)
                for k in range(2):
                    tt(ql[:, k, :], ql[:, k, :], rs[:, 0:T], ALU.mult, S("lat_t"))
                for k in range(2):
                    dve.wait_ge(S("lat_hi"), k + 1)
                    sub(qnlo[:, k, :], ql[:, k, :], qnhi[:, k, :], S("qn_lo"))
                dve.wait_ge(S("norm_sum"), 3)
                mean_square(dve, "latkv", ps[:, 0:KEYS], P, EPS, P, 0, KEYS)
                tt(kvl[:, :], kvl[:, :], rs[:, :], ALU.mult, S("lat_t"))
                dve.wait_ge(S("lat_hi"), 3)
                sub(kvlo[:, :], kvl[:, :], kvhi[:, :], S("kvn_lo"))
            if on("gates"):
                dve.wait_ge(S("rope_loaded"), 32)
                with dve.Fori(0, 4) as i:
                    for u in range(4):
                        w = (T, KEYS)[u % 2]
                        r = slice(64, QK)
                        n = 4 * i + u
                        dve.wait_ge(S("prep_a"), n + 1)
                        nc.vector.memset(stat[:, 15:16], 0.0).then_inc(S("prep_go"), 1)
                        nc.vector.stream_shuffle(tmp[1][r, 0:w], tmp[0][r, 0:w], SHUFFLE).then_inc(S("prep_swap"), 1)
                        dve.wait_ge(S("prep_swap"), n + 1)
                        tt(tmp[1][r, 0:w], tmp[1][r, 0:w], sinT[r, 0:w], ALU.mult, S("prep_sin"))
                        dve.wait_ge(S("prep_ss"), n + 1)
                        nc.vector.tensor_scalar(rs[0:QK, 0:w], ps[0:QK, 4 * HALF:4 * HALF + w], 1.0 / QK, EPS, ALU.mult,
                                                ALU.add).then_inc(S("prep_ms"), 1)
                        dve.wait_ge(S("prep_root"), n + 1)
                        nc.vector.reciprocal(rs[0:QK, 0:w], rs[0:QK, 0:w]).then_inc(S("prep_rs"), 1)
                        dve.wait_ge(S("prep_rs"), n + 1)
                        dve.wait_ge(S("prep_rot"), n + 1)
                        tt(tmp[0][0:QK, 0:w], tmp[0][0:QK, 0:w], rs[0:QK, 0:w], ALU.mult, S("prep_full"))
                        dve.wait_ge(S("prep_hi"), n + 1)
                        sub(phd[1][0:QK, 0:w], tmp[0][0:QK, 0:w], phd[0][0:QK, 0:w], S("prep_lo"))
            if on("v"):
                dve.wait_ge(S("prep_lo"), 16)
                dve.wait_ge(S("prep_stored"), 512)
                for n in range(2):
                    dve.wait_ge(S(f"gate_stored{n}"), 128)
                for tt_ in range(10):
                    dve.wait_ge(S("rows_hi"), 8 + tt_ + 1)
                    sub(Vlo[:, tt_, :], ps[:, (tt_ % 8) * HALF:(tt_ % 8 + 1) * HALF], Vhi[:, tt_, :], S("v_lo"))
            if on("dft"):
                with dve.Fori(0, 2) as h:
                    for part in range(2):
                        for g in range(NG):
                            dve.wait_ge(S("dft_hi"), 12 * h + 4 * part + g + 1)
                            sub(ABlo[:, g, part, :], ps[:, (4 * part + g) * HALF:(4 * part + g + 1) * HALF], ABhi[:, g, part, :], S("ab_lo"))
                    for g in range(NG):
                        dve.wait_ge(S("dft_hi"), 12 * h + 8 + g + 1)
                        sub(fms[1][:, g, :], ps[:, g * HALF:(g + 1) * HALF], fms[0][:, g, :], S("fm_lo"))
            def ones_beside(Vs, r0):
                for n in range(2):
                    nc.vector.memset(f32(Vs[n][:, :, others(r0)]), 1.0 - n).then_inc(S("beside"), 1)

            if on("mla"):
                for j in range(4):
                    if j == 1:
                        dve.wait_ge(S("fm_lo"), 8)
                        dve.wait_ge(S("fm_stored"), 64)
                    Q, K, V, r0 = mla_heads[j]
                    ones_beside(V, r0)
                    for n in range(2):
                        nc.vector.memset(f32(K[n][96:97, :]), 1.0 - n).then_inc(S("beside"), 1)
                scores, rows_lo, body = att_dve(dve, mla)
                with dve.Fori(0, 2) as i:
                    scores(i, 0)
                    rows_lo(i, 0)
                    for j in range(4):
                        body(i, j)
            if on("merge"):
                dve.wait_ge(S("att_pv"), 80 + PRIMED["att_pv"])
                with dve.Fori(0, 4) as i:
                    for j in range(2):
                        panels_done(dve, "merge", 2, i, j)
                        dve.wait_ge(S(f"sg_loaded{j}"), 32 * i + 32)
                        dve.wait_ge(S("y_lo"), 2 * i + j)
                        for n, o in enumerate((mm1, mm2)):
                            g, free = pair_of("merge", 2 * j + n)
                            tt(o[:, :], g, sg[j][n][:, :], ALU.mult, free)
                        for n in range(2):
                            evicted(dve, "merge", 4, i, 2 * j + n)
                        tt(mm1[:, :], mm1[:, :], mm2[:, :], ALU.add, S("y_full"))
                        dve.wait_ge(S("y_hi"), 2 * i + j + 1)
                        sub(Ylo[:, 2 * i + j, :], mm1[:, :], Yhi[:, 2 * i + j, :], S("y_lo"))
            if on("wout"):
                dve.wait_ge(S("x_loaded"), 32)
                nc.vector.memset(acc[:, :], 0.0).then_inc(S("zeroed"), 1)
                dve.wait_ge(S("zeroed"), 1)
                with dve.Fori(0, 4) as i:
                    for j in range(2):
                        panels_done(dve, "wout", 2, i, j)
                        g, free = pair_of("wout", j)
                        x_ = X1[:, 2 * i + j, :]
                        nc.vector.scalar_tensor_tensor(x_, g, modx[:, bass.ds(2 * i + (16 + j), 1)], x_, ALU.mult, ALU.add).then_inc(free, 1)
                        dve.wait_ge(S("n2_sq"), 2 * i + j + 1)
                        dve.wait_ge(S("n2_acc"), 2 * i + j)
                        tt(acc[:, 0:T], acc[:, 0:T], tmp[j][:, 0:T], ALU.add, S("n2_acc"))
                dve.wait_ge(S("norm_sum"), 4)
                mean_square(dve, "n2", ps[:, 4 * HALF:6 * HALF], D, EPS, P, 0, T)
                apply_dve(dve, "n2", KT, lambda k: X1[:, k, :], T, lambda k: Hb[1][:, k, :], lambda k: Hb[0][:, k, :])
            if on("mlp"):
                with dve.Fori(0, 4) as i:
                    def usq(t):
                        evicted(dve, "mlp", 16, i, t)
                        tt(tmp[t % 2][:, 0:T], tmp[t % 2][:, 0:T], tmp[t % 2][:, 0:T], ALU.mult, S("u_sq"))
                        dve.wait_ge(S("u_hi"), 8 * i + t + 1)
                        sub(Ulo[:, t, :], tmp[t % 2][:, 0:T], Uhi[:, t, :], S("u_lo"))
                    for t in range(8):
                        usq(t)
                    for k in range(8):
                        panels_done(dve, "mlp", 16, i, 8 + k)
                        g, free = pair_of("mlp", 8 + k)
                        nc.vector.scalar_tensor_tensor(X1[:, k, :], g, modx[:, 40 + k:41 + k], X1[:, k, :], ALU.mult, ALU.add).then_inc(free, 1)
                for k in range(KT):
                    dve.wait_ge(S("x2_hi"), k + 1)
                    sub(Hb[1][:, k, :], X1[:, k, :], Hb[0][:, k, :], S("x2_lo"))
            if on("pool"):
                dve.wait_ge(S("x2_hi"), 8)
                for b in (*pu, *pa):
                    nc.vector.memset(b[:, 0:16], 0.0).then_inc(S("zeroed"), 1)
                dve.wait_ge(S("zeroed"), 5)
                for g4 in range(4):
                    for t in range(2):
                        evicted(dve, "pool", 6, g4, t)
                        dve.wait_ge(S("pm_lo"), 2 * g4 + t)
                        src = pu[t]
                        for s_ in range(g4 + 1):
                            sh = 1 << s_
                            dst = pa[(s_ + g4) % 2]
                            tt(dst[:, 16:], src[:, 16:], src[:, 16 - sh:16 - sh + T], ALU.add, S("pool_sum"))
                            dve.wait_ge(S("pool_sum"), pool_count(g4, t, s_))
                            src = dst
                        o = pm_buf(g4, t)
                        tt(stat_pool[:, :], src[:, 16:32], poolc[:, g4, :], ALU.mult, S("pool_mean"))
                        nc.vector.scalar_tensor_tensor(o[:, 32:], src[:, 32:], 1.0 / (2 << g4), pu[t][:, 32:], ALU.mult,
                                                       ALU.subtract).then_inc(S("pool_mean"), 1)
                        dve.wait_ge(S("pool_mean"), 2 * (2 * g4 + t) + 1)
                        tt(o[:, 16:32], stat_pool[:, :], pu[t][:, 16:32], ALU.subtract, S("pm_full"))
                        dve.wait_ge(S("pool_mean"), 2 * (2 * g4 + t) + 2)
                        dve.wait_ge(S("pm_full"), 2 * g4 + t + 1)
                        dve.wait_ge(S("pool_sig"), 2 * g4 + t + 1)
                        g, free = pair_of("pool", 2 + t)
                        tt(sil[t][:, :], g, sgm[:, :], ALU.mult, free)
                        dve.wait_ge(S("pm_hi"), 2 * g4 + t + 1)
                        sub(PMlo[:, t, :], o[:, 16:], PMhi[:, t, :], S("pm_lo"))
                    for t in range(2):
                        panels_done(dve, "pool", 5, g4, 4)
                        g, free = pair_of("pool", 4 + t)
                        dve.wait_ge(S("pool_ylo"), 2 * g4 + t)
                        evicted(dve, "pool", 6, g4, 2 + t)
                        nc.vector.scalar_tensor_tensor(yf[:, :], g, col("pscale", 2 * g4 + t), sil[t][:, :], ALU.mult, ALU.mult).then_inc(free, 1)
                        dve.wait_ge(S("pool_yhi"), 2 * g4 + t + 1)
                        sub(ys[t][1][:, :], yf[:, :], ys[t][0][:, :], S("pool_ylo"))

            def mem_heads(l):
                st = f"mem{l + 1}"
                if l == 0:
                    dve.wait_ge(S("pool_stored0"), 128)
                    dve.wait_ge(S("pool_stored1"), 128)
                else:
                    dve.wait_ge(S("att_stored"), 384 + PRIMED["att_stored"])
                with dve.Fori(0, 2) as i:
                    for j in range(2):
                        dve.wait_ge(S("mem_qhi"), 4 * l + 2 * i + j + 1)
                        g, free = pair_of(st, j)
                        sub(Qm[j][1][:, :], g, Qm[j][0][:, :], free)
                    dve.wait_ge(S("att_mlo"), mem_f(l, i) + PRIMED["att_mlo"])
                    for u in range(4):
                        j, h = u // 2, u % 2
                        dve.wait_ge(S("att_s"), mem_c(l, i) - 2 + u + 1)
                        nc.vector.reduce_max(mxf[:, 8 * j + 4 * h:8 * j + 4 * h + 4], ps[:, (4 + 2 * h) * HALF:(6 + 2 * h) * HALF].rearrange(
                            "p (q k) -> p q k", k=256), AXX).then_inc(S("att_max") if u < 3 else S("att_mx"), 1)
                    nc.vector.memset(stat[:, 14:15], 0.0).then_inc(S("att_max"), 1)
                    dve.wait_ge(S("mem_sig"), 4 * l + 2 * i + 1)
                    g, free = pair_of(st, 2)
                    tt(silm[0][:, :], g, sgq[:, :], ALU.mult, free)
                    dve.wait_ge(S("att_mhi"), mem_f(l, i) + 1)
                    nc.vector.scalar_tensor_tensor(mrow[1][0:16, :], ps[0:16, 4 * HALF:4 * HALF + P], -1.0, f32(mrow[0][0:16, :]), ALU.mult,
                                                   ALU.subtract).then_inc(S("att_mlo"), 1)
                    dve.wait_ge(S("mem_sig"), 4 * l + 2 * i + 2)
                    g, free = pair_of(st, 3)
                    tt(silm[1][:, :], g, sgq[:, :], ALU.mult, free)
                    for u in range(4):
                        dve.wait_ge(S("att_hi"), mem_u(l, i) + u + 1)
                        sub(Em[u][1][:, :], tmp[u % 2][:, 0:T], Em[u][0][:, :], S("att_lo"))
                    for j in range(2):
                        h = 4 * l + 2 * i + j
                        evicted(dve, st, 8, i, 5 + 2 * j)
                        evicted(dve, st, 8, i, 4 + 2 * j)
                        nc.vector.reciprocal(sums_m[j][:, 0:T], sums_m[j][:, 0:T]).then_inc(S("mem_y"), 1)
                        tt(om[:, :], om[:, :], silm[j][:, :], ALU.mult, S("mem_y"))
                        dve.wait_ge(S("mem_y"), 3 * h + 2)
                        tt(om[:, :], om[:, :], sums_m[j][:, 0:T], ALU.mult, S("mem_y"))
                        dve.wait_ge(S("mem_yhi"), h + 1)
                        sub(ym[j][1][:, :], om[:, :], ym[j][0][:, :], S("mem_ylo"))

            def out_proj(l):
                st = f"out{l + 1}"
                nc.vector.memset(acc[:, :], 0.0).then_inc(S("zeroed"), 1)
                dve.wait_ge(S("zeroed"), 6 + l)
                with dve.Fori(0, 2) as i:
                    for t in range(4):
                        n = 4 * i + t
                        if t % 2 == 0:
                            dve.wait_ge(S("out_mid"), 4 * l + 2 * i + t // 2 + 1)
                        else:
                            panels_done(dve, st, 6, i, 3 * (t // 2) + 2)
                        g, free = pair_of(st, t)
                        b = tmp[t % 2][:, 0:T]
                        dve.wait_ge(S("ln_acc"), 8 * l + n)
                        nc.vector.scalar_tensor_tensor(b, f32(Hb[0][:, n, :]), ALPHA, g, ALU.mult, ALU.add).then_inc(free, 1)
                        evicted(dve, st, 4, i, t)
                        nc.vector.scalar_tensor_tensor(Z[:, n, :], f32(Hb[1][:, n, :]), ALPHA, b, ALU.mult, ALU.add).then_inc(S("ln_z"), 1)
                        dve.wait_ge(S("ln_z"), 8 * l + n + 1)
                        tt(acc[:, 0:T], acc[:, 0:T], Z[:, n, :], ALU.add, S("ln_acc"))
                dve.wait_ge(S("norm_sum"), 2 * l + 5)
                nc.vector.tensor_scalar(rs[:, 0:T], ps[:, 4 * HALF:6 * HALF], 1.0 / D, None, ALU.mult).then_inc(S("ln_mu"), 1)
                dve.wait_ge(S("ln_mu"), l + 1)
                for k in range(KT + 1):
                    if k < KT:
                        tt(Z[:, k, :], Z[:, k, :], rs[:, 0:T], ALU.subtract, S("ln_zc"))
                    if k >= 1:
                        dve.wait_ge(S("ln_sq"), 8 * l + k)
                        if k == 1:
                            nc.vector.tensor_copy(acc[:, 0:T], tmp[0][:, 0:T]).then_inc(S("ln_vacc"), 1)
                        else:
                            dve.wait_ge(S("ln_vacc"), 8 * l + k - 1)
                            tt(acc[:, 0:T], acc[:, 0:T], tmp[(k - 1) % 2][:, 0:T], ALU.add, S("ln_vacc"))
                dve.wait_ge(S("norm_sum"), 2 * l + 6)
                mean_square(dve, f"ln{l}", ps[:, 4 * HALF:6 * HALF], D, LN_EPS, P, 0, T)
                if l == 0:
                    apply_dve(dve, "ln0", KT, lambda k: Z[:, k, :], T, lambda k: Hb[1][:, k, :], lambda k: Hb[0][:, k, :])
                else:
                    for k in range(KT):
                        if k >= 2:
                            dve.wait_ge(S(f"out_stored{k % 2}"), 16 * (k // 2))
                        tt(tmp[k % 2][:, 0:T], Z[:, k, :], rs[:, 0:T], ALU.mult, S("ap_t"))

            if on("mem1"):
                mem_heads(0)
            if on("out1"):
                out_proj(0)
            if on("forget"):
                r = slice(0, FOX)
                panels_done(dve, "forget", 1, 0, 0)
                dve.wait_ge(S("ap_lo"), 32)
                nc.vector.tensor_scalar(tmp[0][r, 0:T], ps[r, 4 * HALF:6 * HALF], cols[r, COLS["bf"]:COLS["bf"] + 1], None,
                                        ALU.add).then_inc(S("logits_read"), 1)
                nc.vector.memset(rs[r, 0:T], 1.0).then_inc(S("gate_log"), 1)
                for x_ in (Kf, Qf):
                    for j in range(2):
                        for n in range(2):
                            nc.vector.memset(f32(x_[j][n][64:96, :]), 0.0).then_inc(S("aug"), 1)
                dve.wait_ge(S("aug"), 8)
                for x_ in (Kf, Qf):
                    for j in range(2):
                        for n in range(2):
                            nc.vector.memset(f32(x_[j][n][64:66, :]), 1.0 - n).then_inc(S("aug"), 1)
                for j in range(2):
                    for n in range(2):
                        nc.vector.memset(f32(Kf[j][n][96:97, :]), 1.0 - n).then_inc(S("aug"), 1)
                dve.wait_ge(S("fg"), 3)
                nc.vector.tensor_scalar(tmp[0][r, 0:T], tmp[0][r, 0:T], 0.0, None, ALU.min).then_inc(S("gate_log"), 1)
                dve.wait_ge(S("gate_log"), 2)
                tt(acc[r, 0:T], tmp[1][r, 0:T], tmp[0][r, 0:T], ALU.subtract, S("gate_log"))
                dve.wait_ge(S("gate_log"), 3)
                nc.vector.tensor_tensor_scan(ncum[r, :], rs[r, 0:T], acc[r, 0:T], 0.0, ALU.mult, ALU.add).then_inc(S("cum"), 1)
                dve.wait_ge(S("fg"), 4)
                sub(nch[1][r, :], ncum[r, :], nch[0][r, :], S("cum"))
                dve.wait_ge(S("cum"), 2)
                for n in range(2):
                    nc.vector.tensor_scalar(mch[n][r, :], f32(nch[n][r, :]), -1.0, None, ALU.mult).then_inc(S("cum"), 1)
            if on("fox"):
                dve.wait_ge(S("cum_stored"), 64)
                nc.vector.memset(mx[:, 8:12], -3e38).then_inc(S("beside"), 1)
                for j in range(2):
                    ones_beside(Vf[j], 64 * j)
                scores, rows_lo, body = att_dve(dve, fox)
                with dve.Fori(0, 8) as i:
                    for t in range(2):
                        g, free = pair_of("fox", t)
                        for j in range(2):
                            dve.wait_ge(S("fox_hi"), 4 * i + 2 * t + j + 1)
                            nc.vector.scalar_tensor_tensor((Kf, Qf)[t][j][1][0:64, :], g[64 * j:64 * j + 64, :], (1.0, 64 ** -0.5)[t],
                                                           f32((Kf, Qf)[t][j][0][0:64, :]), ALU.mult, ALU.subtract).then_inc(free if j else S("fox_low"), 1)
                    scores(i, 0)
                    for j in range(2):
                        c = slice(64 * j, 64 * j + 64)
                        dve.wait_ge(S("fox_vhi"), 2 * i + 2)
                        sub(Vf[j][1][:, :, c], PV.rearrange("p (k d) -> p k d", d=P)[:, :, c], Vf[j][0][:, :, c], S("fox_vlo"))
                    rows_lo(i, 0)
                    dve.wait_ge(S("fox_sig"), i + 1)
                    g, free = pair_of("fox", 3)
                    tt(acc[:, 0:T], g, rs[:, 0:T], ALU.mult, free)
                    for j in range(2):
                        body(i, j)
            if on("mem2"):
                mem_heads(1)
            if on("out2"):
                out_proj(1)

        @block.sync
        def _(sp):
            sp_program(sp)

        @block.gpsimd
        def _(gp):
            pool_program(gp)

        @block.tensor
        def _(pe):
            pe_program(pe)

        @block.scalar
        def _(act):
            act_program(act)

        @block.vector
        def _(dve):
            dve_program(dve)


def _tiles(w):
    k, n = w.shape
    return w.reshape(k // P, P, n // P, P).transpose(2, 1, 0, 3).reshape(n // P, P, k)


def _moving(w):
    k, n = w.shape
    return w.reshape(k // 256, 2, P, n).transpose(0, 2, 1, 3).reshape(k // 256, P, 2 * n)


def _padded(a):
    return np.pad(a, ((0, 0), (0, 0), (0, PW - a.shape[2])))


def _feature_major(x):
    n = x.shape[0]
    return np.ascontiguousarray(x.T.reshape(KT, P, n).transpose(1, 0, 2))


def _stream(i):
    w_in, w_in2, w_kv2, kvb, qb = i["w_in"][0], i["w_in_2"], i["w_kv_shared_2"], i["w_kvb"][0], i["w_qb"][0]
    gates = _tiles(w_in[:, 928:])
    parts = []
    for layer in range(2):
        parts += [_tiles(i["w_mem_kv_2"][layer][:, :512]), _moving(i["w_mem_kv_2"][layer][:, 512:])]
    parts += [_tiles(w_in[:, 512:896]), _tiles(w_in[:, 832:960]), _moving(w_in[:, :512])]
    for h in range(NH):
        q = qb[:, QK * h:QK * h + QK].reshape(2, P, QK).transpose(1, 0, 2).reshape(1, P, 2 * QK)
        parts += [_padded(q), gates[2 * h:2 * h + 1], _padded(kvb[None, :, P * h:P * h + P]), gates[2 * h + 1:2 * h + 2]]
    parts.append(_padded(kvb.reshape(P, NH, P)[:, :, NOPE:].reshape(1, P, FW)))
    ang = 2 * np.pi * (np.outer(np.arange(T), np.arange(T)) % T) / T
    cos, sin = np.cos(ang).astype(np.float32), np.sin(ang).astype(np.float32)
    ch = 2 * np.pi * (np.outer(np.arange(P), np.arange(P)) % P) / P
    norm = 1 / math.sqrt(T * P)
    chc, chs = (np.cos(ch) * norm).astype(np.float32), (-np.sin(ch) * norm).astype(np.float32)
    for h in range(2):
        parts += [_moving(cos[:, HALF * h:HALF * h + HALF]), _moving(sin[:, HALF * h:HALF * h + HALF]), _padded(chc[None]), _padded(chs[None])]
    f, a = _tiles(i["w_fourier"][0]), _tiles(i["w_mla_o"][0])
    parts += [np.concatenate([f, a], axis=2), _tiles(i["w_out"][0])]
    for c in range(4):
        parts += [_tiles(i["w_up"][0][:, D * c:D * c + D]), _tiles(i["w_down"][0][D * c:D * c + D])]
    u, u2 = _tiles(w_in2[0]), _tiles(w_in2[1])
    for g in range(4):
        mix = i["pool_w_2"][0, g].reshape(2, P, 2, P).transpose(1, 2, 0, 3).reshape(1, P, 512)
        parts += [u[2 * g:2 * g + 2], u[MT + 2 * g:MT + 2 * g + 2], _padded(mix)]

    def mem(t):
        return np.concatenate([t[8:10], t[MT + 8:MT + 10], t[10:12], t[MT + 10:MT + 12]], axis=0)

    def proj(w):
        return _tiles(w).reshape(8, P, MT, P).transpose(0, 2, 1, 3).reshape(12, 8, P, P).transpose(0, 2, 1, 3).reshape(12, P, PW)

    parts += [mem(u), proj(i["w_out_2"][0])]
    fg = np.pad(w_kv2[:, 2 * D:], ((0, 0), (0, P - FOX)))
    k, v = _tiles(w_kv2[:, :D]), _tiles(w_kv2[:, D:2 * D])
    parts += [_tiles(fg), np.stack([k, u2[:8], v, u2[MT:MT + 8]], axis=1).reshape(32, P, PW), mem(u2), proj(i["w_out_2"][1])]
    parts.append(np.zeros((LEAD, P, PW), np.float32))
    w = np.concatenate(parts, axis=0)
    assert w.shape[0] == NP + LEAD, w.shape
    return w


def _columns(i):
    def c(a):
        a = a.reshape(-1)
        if a.shape[0] < P:
            a = np.pad(a, (0, P - a.shape[0]))
        return a.reshape(-1, P).T

    return np.ascontiguousarray(np.concatenate([c(i[n]) for n in (
        "c", "c_ctx", "ada_b", "norm1_g", "norm2_g", "b_gate", "q_norm_g", "kv_norm_g", "q_gain", "k_gain", "ln_g_2", "ln_b_2",
        "pool_scale_2", "b_forget_2")], axis=1))


def _rope():
    n = np.arange(T)
    freqs = (10000.0 ** (-np.arange(8, dtype=np.float32) / 8)).astype(np.float32)
    row, colu = (n // 64).astype(np.float32), (n % 64).astype(np.float32)
    ar, ac = row[:, None] * freqs, colu[:, None] * freqs
    ang = np.concatenate([ar, ar, ac, ac], axis=1).T.astype(np.float32)
    cos, sin = np.ones((QK, KEYS), np.float32), np.zeros((QK, KEYS), np.float32)
    cos[NOPE:, :T] = np.cos(ang)
    sign = np.array([-1.0] * 8 + [1.0] * 8 + [-1.0] * 8 + [1.0] * 8, np.float32)[:, None]
    sin[NOPE:, :T] = np.sin(ang) * sign
    return cos, sin


def kernel(**inputs):
    from concourse import bacc
    from concourse.bass_utils import run_bass_kernel_spmd

    i = {k: np.asarray(v) for k, v in inputs.items()}
    cos, sin = _rope()
    few = np.array([[1.0 / min(t + 1, 2 << g) for t in range(16)] for g in range(4)], np.float32)
    arrays = {
        "w": _stream(i),
        "ada": np.ascontiguousarray(i["ada_w"][0].reshape(KT, P, 24, 256).transpose(2, 1, 0, 3)),
        "cols": _columns(i),
        "x": _feature_major(i["x"][0]),
        "ctx": _feature_major(i["ctx"][0]),
        "mem": _feature_major(i["mem_2"][0]),
        "ident": np.eye(P, dtype=np.float32),
        "mask": np.where(np.arange(P)[None, :] <= np.arange(P)[:, None], 0.0, -1e30).astype(np.float32),
        "poolc": np.ascontiguousarray(np.broadcast_to(few, (P, 4, 16))),
        "cos": cos,
        "sin": sin,
    }
    nc = bacc.Bacc("TRN2", target_bir_lowering=False, num_devices=1)
    d = {n: nc.dram_tensor(f"in_{n}", a.shape, F, kind="ExternalInput").ap() for n, a in arrays.items()}
    out = nc.dram_tensor("out", (KT, P, T), F, kind="ExternalOutput").ap()
    build(nc, d, out)
    r = run_bass_kernel_spmd(nc, [{f"in_{n}": a for n, a in arrays.items()}], core_ids=[0])
    return np.ascontiguousarray(r.results[0]["out"].reshape(D, T).T).reshape(1, T, D)
```

```python
import math
from contextlib import ExitStack

import concourse.bass as bass
import numpy as np
from concourse import mybir

ALU = mybir.AluOpType
ACT = mybir.ActivationFunctionType
AXX = mybir.AxisListType.X
F = mybir.dt.float32
R = mybir.dt.float32r

P = 128
T = 1024
CTX = 256
KEYS = T + CTX
D = 1024
KT = D // P
HALF = 512
PW = 1024
NH, NOPE, ROPE, VD = 8, 64, 32, 64
QK = NOPE + ROPE
FW = 512
NG = 4
QL = 256
FF = 4 * D
FOX = 16
MH = 4
MIX = D + MH * P
MT = MIX // P
EPS, LN_EPS = 1e-6, 1e-5
ALPHA = 4 ** 0.25
LEAD = 4
SPLIT_LEAD = 2

COLS = {}
_n = 0
for _name, _w in (("c", 8), ("cc", 8), ("ada_b", 48), ("n1", 8), ("n2", 8), ("b_gate", 16), ("qng", 2),
                  ("kvng", 1), ("qg", 1), ("kg", 1), ("ln_g", 16), ("ln_b", 16), ("pscale", 8), ("bf", 1)):
    COLS[_name] = _n
    _n += _w
NCOLS = _n

PANELS = (("mem", 16), ("lat", 4), ("f", 4), ("gates", 32), ("v", 1), ("dft", 20), ("merge", 8), ("wout", 8),
          ("mlp", 64), ("pool", 20), ("mem1", 8), ("out1", 12), ("forget", 1), ("fox", 32), ("mem2", 8), ("out2", 12))
P0 = {}
_n = 0
for _name, _w in PANELS:
    P0[_name] = _n
    _n += _w
NP = _n
NPAN = dict(PANELS)

TILES = (("mem", 8), ("lat", 4), ("gates", 16), ("mla", 80), ("merge", 16), ("wout", 8), ("mlp", 64), ("pool", 24),
         ("mem1", 16), ("out1", 8), ("fox", 160), ("mem2", 16), ("out2", 8))
T0 = {}
_n = 0
for _name, _w in TILES:
    T0[_name] = _n
    _n += _w

SHUFFLE = [(i + 8) % 16 + 16 * (i // 16) for i in range(32)]


ORDER = ["mem", "lat", "f", "gates", "v", "dft", "mla", "merge", "wout", "mlp", "pool", "mem1", "out1", "forget", "fox", "mem2", "out2"]


def build(nc, d, out, upto=99, dbg=None):
    ctx = ExitStack()
    with ctx:
        def sb(name, shape, dt=F):
            return ctx.enter_context(nc.sbuf_tensor(name, shape, dt))

        raw = [sb(f"raw{i}", [P, PW]) for i in range(2)]
        whi = [sb(f"whi{i}", [P, PW], R) for i in range(2)]
        wlo = [sb(f"wlo{i}", [P, PW], R) for i in range(2)]
        onesf = sb("onesf", [P, P])
        onesr = sb("onesr", [P, P], R)
        ident = sb("ident", [P, P])
        cols = sb("cols", [P, NCOLS])
        modx, modc = sb("modx", [P, 48]), sb("modc", [P, 16])
        scx, scc, sc2 = sb("scx", [P, 8]), sb("scc", [P, 8]), sb("sc2", [P, 8])
        silc, sigc = sb("silc", [P, 16]), sb("sigc", [P, 16])
        stat = sb("stat", [P, 16])
        mx, mxf = sb("mx", [P, 24]), sb("mxf", [P, 16])
        identr = sb("identr", [P, P], R)
        primes, rcol = sb("primes", [P, 28]), sb("rcol", [P, 10])
        rlat = [primes[:, 0:10], primes[:, 10:20]]
        stat_pool = sb("stat_pool", [P, 16])
        poolc = sb("poolc", [P, 4, 16])
        rs, acc = sb("rs", [P, KEYS]), sb("acc", [P, KEYS])
        accr = nc.alloc_sbuf_tensor_at("accr", [P, T], R, offset=nc.sbuf_base - 4 * KEYS)
        tmp, mrow, tmpr = [], [], []
        for i in range(2):
            tmp.append(sb(f"tmp{i}", [P, KEYS]))
            tmpr.append(nc.alloc_sbuf_tensor_at(f"tmpr{i}", [P, T], R, offset=nc.sbuf_base - 4 * KEYS))
            mrow.append(nc.alloc_sbuf_tensor_at(f"mrow{i}", [P, P], R, offset=nc.sbuf_base - 4 * CTX))
        ZONE = 160 * 1024
        zone = sb("zone", [P, ZONE // 4])
        zbase = nc.sbuf_base - ZONE

        def at(name, kb, shape, dt=F):
            n = 4
            for s in shape[1:]:
                n *= s
            assert kb * 1024 + n <= ZONE, (name, kb, n)
            return nc.alloc_sbuf_tensor_at(name, shape, dt, offset=zbase + int(kb * 1024))

        Hhi, Hlo = at("Hhi", 0, [P, KT, T], R), at("Hlo", 32, [P, KT, T], R)
        Mhi, Mlo = at("Mhi", 0, [P, KT, CTX], R), at("Mlo", 8, [P, KT, CTX], R)
        Mraw = at("Mraw", 16, [P, KT, CTX])
        accx, accc = at("accx", 24, [P, 2048]), at("accc", 32, [P, 2048])
        mks = [at("mks_hi", 40, [P, MH, CTX], R), at("mks_lo", 44, [P, MH, CTX], R)]
        mvs = [at("mvs_hi", 48, [P, 2, HALF], R), at("mvs_lo", 52, [P, 2, HALF], R)]
        XT = at("XT", 64, [P, KT, T])
        CT = at("CT", 96, [P, KT, CTX])
        HChi, HClo = at("HChi", 104, [P, KT, CTX], R), at("HClo", 112, [P, KT, CTX], R)
        adas = [at(f"adas{i}", 122 + 8 * i, [P, KT, 256]) for i in range(2)]
        acc2 = at("acc2", 138, [P, 4096])
        ql, kvl, kr = at("ql", 64, [P, 2, T]), at("kvl", 72, [P, KEYS]), at("kr", 77, [P, KEYS])
        Fhi, Flo = at("Fhi", 90, [P, KT, FW], R), at("Flo", 106, [P, KT, FW], R)
        qnhi, qnlo = at("qnhi", 122, [P, 2, T], R), at("qnlo", 130, [P, 2, T], R)
        kvhi, kvlo = at("kvhi", 138, [P, KEYS], R), at("kvlo", 143, [P, KEYS], R)
        cosT, sinT = at("cosT", 148, [P, KEYS]), at("sinT", 153, [P, KEYS])
        gst = [at(f"gst{i}", 82 + 4 * i, [P, T]) for i in range(2)]
        phd = [at("prep_hi", 64, [P, KEYS], R), at("prep_lo", 69, [P, KEYS], R)]
        ABhi, ABlo = at("ABhi", 0, [P, NG, 2, HALF], R), at("ABlo", 16, [P, NG, 2, HALF], R)
        fms = [at("fms_hi", 32, [P, NG, HALF], R), at("fms_lo", 40, [P, NG, HALF], R)]
        Vhi, Vlo = at("Vhi", 48, [P, 10, FW], R), at("Vlo", 69, [P, 10, FW], R)
        mla_heads = []
        for j, kb in enumerate((122, 0, 48, 76)):
            Q_, K_, V_ = ([at(f"{x}{j}{n}", kb + o + w * n, shape, R) for n in range(2)] for x, o, w, shape in (
                ("Qp", 0, 4, [P, T]), ("Kp", 8, 5, [P, KEYS]), ("Vp", 18, 5, [P, 10, P])))
            mla_heads.append((Q_, K_, V_, 64 * (j % 2)))
        Erh, Erl = ([at(f"E{x}{i}", o + 4 * i, [P, T], R) for i in range(3)] for x, o in (("hi", 104), ("lo", 32)))
        ats = [at("ats_hi", 28, [P, T], R), at("ats_lo", 44, [P, T], R)]
        o32 = at("o32", 116, [P, T])
        Fm = [at("Fm_hi", 0, [P, NG, T], R), at("Fm_lo", 48, [P, NG, T], R)]
        At = [at("At_hi", 16, [P, NG, T], R), at("At_lo", 32, [P, NG, T], R)]
        sg = [[at(f"sg{i}{j}", 64 + 8 * i + 4 * j, [P, T]) for j in range(2)] for i in range(2)]
        mm1, mm2 = at("mm1", 80, [P, T]), at("mm2", 84, [P, T])
        Yhi, Ylo = at("Yhi", 96, [P, KT, T], R), at("Ylo", 128, [P, KT, T], R)
        X1 = at("X1", 64, [P, KT, T])
        Hb = [at("Hb_hi", 96, [P, KT, T], R), at("Hb_lo", 128, [P, KT, T], R)]
        Uhi, Ulo = at("Uhi", 0, [P, KT, T], R), at("Ulo", 32, [P, KT, T], R)
        pu = [at(f"pu{i}", 0 + 4.25 * i, [P, T + 16]) for i in range(2)]
        pa = [at(f"pa{i}", 8.5 + 4.25 * i, [P, T + 16]) for i in range(2)]
        PMhi, PMlo = at("PMhi", 17, [P, 2, T], R), at("PMlo", 25, [P, 2, T], R)
        sil = [at(f"sil{i}", 33 + 4 * i, [P, T]) for i in range(2)]
        sgm = at("sgm", 41, [P, T])
        Y32 = at("Y32", 48, [P, MT, T])
        Qm = [[at(f"Qm{j}{n}", 8 * j + 4 * n, [P, T], R) for n in range(2)] for j in range(2)]
        Km = [[at(f"Km{j}{n}", 16 + 2 * j + n, [P, CTX], R) for n in range(2)] for j in range(2)]
        Vm = [[at(f"Vm{j}{n}", 20 + 2 * j + n, [P, 2, P], R) for n in range(2)] for j in range(2)]
        Em = [[at(f"Em{j}{n}", 24 + 8 * n + 4 * j, [P, T], R) for n in range(2)] for j in range(2)]
        mr = at("mr", 40, [P, T], R)
        maskc, maskr = at("maskc", 92, [P, P]), at("maskr", 93, [P, P], R)
        fox_heads = []
        for j in range(2):
            Q_, K_, V_ = ([at(f"{x}{j}{n}", o + 8 * j + 4 * n, shape, R) for n in range(2)] for x, o, shape in (
                ("Qf", 0, [P, T]), ("Kf", 16, [P, T]), ("Vf", 32, [P, KT, P])))
            fox_heads.append((Q_, K_, V_, 64 * j))
        Qf, Kf, Vf = ([h[k] for h in fox_heads] for k in range(3))
        nch = [at("nch_hi", 52, [P, T], R), at("nch_lo", 56, [P, T], R)]
        mch = [at("mch_hi", 60, [P, T], R), at("mch_lo", 64, [P, T], R)]
        Efh = [at(f"Efhi{i}", 80 + 4 * i, [P, T], R) for i in range(3)]
        ncum = at("ncum", 88, [P, T])
        Z = at("Z", 96, [P, KT, T])
        Yb = [at("Yb_hi", 0, [P, MT, T], R), at("Yb_lo", 48, [P, MT, T], R)]
        ps = ctx.enter_context(nc.psum_tensor("ps", [P, 8 * HALF], F))
        G = [ps[:, 0:1024], ps[:, 1024:2048]]

        def scratch(name, *shape):
            return nc.dram_tensor(name, shape, F, kind="Internal").ap()

        mk_d = scratch("mk_d", 2, 2, P, MH, CTX)
        mv_d = scratch("mv_d", 2, 2, P, 2, HALF)
        gate_d = scratch("gate_d", 16, P, T)
        q_d, k_d = scratch("q_d", NH, 2, QK, T), scratch("k_d", NH, 2, QK, KEYS)
        v_d = scratch("v_d", 2, 4, P, 10, P)
        fm_d, at_d = scratch("fm_d", 2, NG, P, T), scratch("at_d", 2, NG, P, T)
        cum_d = scratch("cum_d", FOX, 2, 2, T)

        sems = {}

        def S(name):
            if name not in sems:
                sems[name] = ctx.enter_context(nc.semaphore(name))
            return sems[name]

        g_free = [S("g_free0"), S("g_free1")]
        f32 = lambda ap: ap.bitcast(F)
        block = ctx.enter_context(nc.Block())
        SCALE = {"mla": QK ** -0.5, "fox": 1.0, "mem": P ** -0.5}

        def evicted(eng, stage, tiles, i, t):
            if isinstance(i, int):
                t, i = t + tiles * i, 0
            n = T0[stage] + t
            eng.wait_ge(g_free[n % 2], n // 2 + 1 + (tiles // 2) * i + PRIMED["g_free"])

        def pair_of(stage, t):
            n = T0[stage] + t
            return G[n % 2], g_free[n % 2]

        def panels_done(eng, stage, per, i, j):
            eng.wait_ge(S("panel_done"), P0[stage] + per * i + j + 1)

        def pair(pe, stage, tiles, i, t):
            if isinstance(i, int):
                t, i = t + tiles * i, 0
            n = T0[stage] + t
            pe.wait_ge(g_free[n % 2], n // 2 + (tiles // 2) * i + PRIMED["g_free"])
            return G[n % 2]

        def whi_of(w, k):
            return w[:, k * HALF:(k + 1) * HALF]

        def pm_buf(g, t):
            return pa[1]

        def pool_count(g, t, s):
            return g * (g + 1) + t * (g + 1) + s + 1


        class Att:

            def __init__(self, name, heads, rows, nkt, E, scale, before, fb, cb, kb, pb, per_step, causal=False):
                self.name, self.heads, self.rows, self.nkt, self.E, self.scale = name, heads, rows, nkt, E, scale
                self.H, self.before, self.fb, self.cb, self.kb, self.pb = len(heads), before, fb, cb, kb, pb
                self.per_step, self.causal = per_step, causal
                self.chunks = []
                for qt in range(8):
                    w = (qt + 1) * P if causal else nkt * P
                    self.chunks += [(qt, c, min(c + HALF, w), c // HALF) for c in range(0, w, HALF)]
                self.C, self.parts = len(self.chunks), (1 if nkt == 8 else 2) + 1
                self.steps = range(nkt)
                self.pieces = nkt - 3

            def of_step(self, s):
                return range(s * self.per_step, min((s + 1) * self.per_step, self.C))

            def queries(self, kt):
                return kt * P if self.causal else 0

            def head(self, i, j):
                return self.before + self.H * i + j

            def before_in_buffer(self, kt):
                return kt - 3 if kt >= 3 else max(k for k in range(self.nkt) if k % 3 == kt) - self.nkt

            def flip(self, i, j):
                return self.fb + self.H * i + j

            def used(self, i, j, kt):
                return self.pb + self.nkt * (self.H * i + j) + kt

            def unit(self, i, j, kt):
                return self.kb + self.nkt * (self.H * i + j) + kt

            def chunk(self, i, j, c):
                return self.cb + self.C * (self.H * i + j) + c

            def tile(self, i, j, kt):
                return (4 if self.causal else 0) + self.nkt * j + kt

            def span(self, kt):
                a = self.queries(kt)
                return ([(a, HALF)] if a < HALF else []) + [(max(a, HALF), T)]

        mla = Att("mla", mla_heads, QK, 10, (Erh, Erl, tmp), SCALE["mla"], 0, 0, 0, 0, 0, 3)
        fox = Att("fox", fox_heads, 66, 8, (Efh, (*tmpr, accr), (*tmp, acc)), SCALE["fox"], 8, 10, 200, 88, 80, 3, causal=True)
        mla.rec0, fox.rec0 = 0, 8 * mla.pieces
        mla.row0, fox.row0 = 0, 256 + 128
        PRIMED = {"att_max": 2, "att_lo": 2, "att_pv": 2, "att_mlo": 1, "att_out": 1, "att_ylo": 1, "att_stored": 1, "mem_pv": 1, "mem_y": 1,
                  "mv_lo": 1, "mk_stored": 1, "mv_stored": 1, "prep_full": 1, "prep_lo": 1, "prep_stored": 1, "fm_lo": 1, "ab_lo": 1, "fm_stored": 1, "y_lo": 1, "n2_acc": 1, "ln_acc": 1, "gate_stored": 1, "g_free": 1}
        PV = ps[:, 4 * HALF:6 * HALF]

        def mm3(o, wh, wl, xh, xl, start, stop):
            nc.tensor.matmul(o, wh, xh, start=start, stop=False)
            nc.tensor.matmul(o, wh, xl, start=False, stop=False)
            return nc.tensor.matmul(o, wl, xh, start=False, stop=stop)

        def mem_c(l, i):
            return (192, 392)[l] + 4 * i + PRIMED["att_max"]

        def mem_f(l, i):
            return (8, 26)[l] + i

        def mem_r(l, i):
            return (256, 256 + 128 + 512)[l] + 64 * i

        def mem_u(l, i):
            return (80, 216)[l] + 4 * i

        sums_m = (rs, acc)

        def others(r0):
            return slice(64 - r0, 128 - r0)

        def att_pe(pe, a):
            tiles = a.nkt * a.H + (4 if a.causal else 0)

            def chunk(i, j, c):
                qt, c0, c1, _ = a.chunks[c]
                Q, K = a.heads[j][0], a.heads[j][1]
                pe.wait_ge(S("att_max"), a.chunk(i, j, c) - 1 + PRIMED["att_max"])
                if c == 0:
                    pe.wait_ge(S("att_mlo"), a.flip(i, j) + PRIMED["att_mlo"])
                    a.loaded(pe, i, j)
                b = (6 + c % 2) * HALF
                o = ps[:, b:b + c1 - c0]
                q = [x[0:a.rows, qt * P:qt * P + P] for x in Q]
                k = [x[0:a.rows, c0:c1] for x in K]
                diag = a.causal and c1 == (qt + 1) * P
                last = mm3(o, q[0], q[1], k[0], k[1], True, not diag)
                if diag:
                    last = nc.tensor.matmul(ps[:, b + c1 - c0 - P:b + c1 - c0], identr[:, :], maskr[:, :], start=False, stop=True)
                last.then_inc(S("att_s"), 1)

            def flip_max(i, j):
                pe.wait_ge(S("att_mx"), a.flip(i, j) + 1)
                nc.tensor.transpose(ps[0:8, 6 * HALF:6 * HALF + P], mxf[:, 0:8], ident[:, :]).then_inc(S("att_mt"), 1)

            def transposed(i, j, kt):
                Q, K = a.heads[j][0], a.heads[j][1]
                if kt == 0:
                    pe.wait_ge(S("att_row"), a.row0 + 32 * (a.H * i + j) + 32)
                o = pair(pe, a.name, tiles, i, a.tile(i, j, kt))
                k = [x[0:97, kt * P:kt * P + P] for x in K]
                for c0, c1 in a.span(kt):
                    diag = a.causal and c0 == a.queries(kt)
                    last = mm3(o[:, c0:c1], k[0], k[1], Q[0][0:97, c0:c1], Q[1][0:97, c0:c1], True, not diag)
                    if diag:
                        last = nc.tensor.matmul(o[:, c0:c0 + P], maskr[:, :], identr[:, :], start=False, stop=True)
                last.then_inc(S("att_st"), 1)

            def values(i, j, kt):
                V = a.heads[j][2]
                pe.wait_ge(S("att_lo"), a.unit(i, j, kt) + 1 + PRIMED["att_lo"])
                if kt == 0:
                    pe.wait_ge(S("att_out"), a.head(i, j) + PRIMED["att_out"])
                for c0, c1 in a.span(kt):
                    last = mm3(PV[:, c0:c1], V[0][:, kt, :], V[1][:, kt, :], a.E[0][kt % 3][:, c0:c1], a.E[1][kt % 3][:, c0:c1],
                               kt == 0, kt == a.nkt - 1 and not a.causal)
                if a.causal and kt == a.nkt - 1:
                    Q, K = a.heads[j][0], a.heads[j][1]
                    for c0 in (0, HALF):
                        last = nc.tensor.matmul(PV[:, c0:c0 + HALF], K[1][96:97, 0:P], Q[0][96:97, c0:c0 + HALF], start=False, stop=True)
                last.then_inc(S("att_pv"), 1)

            def scores(i, j):
                for c in range(a.C):
                    chunk(i, j, c)

            def body(i, j):
                for kt in a.steps:
                    transposed(i, j, kt)
                    if j + 1 < a.H:
                        for c in a.of_step(kt):
                            chunk(i, j + 1, c)
                        if kt == a.nkt - 2:
                            flip_max(i, j + 1)
                    if kt >= 2:
                        values(i, j, kt - 2)
                values(i, j, a.nkt - 2)
                values(i, j, a.nkt - 1)

            return scores, flip_max, body

        def att_act(act, a):
            tiles = a.nkt * a.H + (4 if a.causal else 0)

            def rows_hi(i, j):
                act.wait_ge(S("att_mt"), a.flip(i, j) + 1)
                nc.scalar.activation(mrow[0][0:8, :], ps[0:8, 6 * HALF:6 * HALF + P], ACT.Copy, scale=-1.0).then_inc(S("att_mhi"), 1)

            def rows_send(i, j):
                act.wait_ge(S("att_mlo"), a.flip(i, j) + 1 + PRIMED["att_mlo"])
                for n in range(2):
                    nc.scalar.dma_start(f32(a.heads[j][0][n][96:97, :]), f32(mrow[n][0:8, :])).then_inc(S("att_row"), 16)

            def part_hi(i, j):
                r = slice(a.heads[j][3], a.heads[j][3] + 64)
                act.wait_ge(S("att_y"), a.head(i, j) + 1)
                if j % 2 == 0:
                    act.wait_ge(S("att_stored"), 32 * (a.before // 2 + a.H // 2 * i + j // 2) + PRIMED["att_stored"])
                nc.scalar.activation(ats[0][r, :], o32[r, :], ACT.Copy).then_inc(S("att_yhi"), 1)

            def out(i, j):
                act.wait_ge(S("att_pv"), a.used(i, j, a.nkt - 1) + 1 + PRIMED["att_pv"])
                if a.causal:
                    o = others(a.heads[j][3])
                    act.wait_ge(S("att_y"), a.head(i, j))
                    if j == 0:
                        evicted(act, "fox", 20, i, 3)
                    nc.scalar.activation(rs[o, 0:T], PV[o, :], ACT.Copy).then_inc(S("att_sums"), 1)
                else:
                    act.wait_ge(S("att_ylo"), a.head(i, j) + PRIMED["att_ylo"])
                    nc.scalar.activation(o32[:, :], PV, ACT.Copy).then_inc(S("att_out"), 1)

            def body(i, j):
                for kt in a.steps:
                    n = a.unit(i, j, kt)
                    g, free = pair_of(a.name, a.tile(i, j, kt))
                    c = slice(a.queries(kt), T)
                    act.wait_ge(S("att_st"), n + 1)
                    e = a.E[2][kt % len(a.E[2])]
                    if not a.causal:
                        act.wait_ge(S("att_lo"), n - 1 + PRIMED["att_lo"])
                        nc.scalar.activation(e[:, c], g[:, c], ACT.Exp, scale=a.scale).then_inc(free, 1)
                        evicted(act, a.name, tiles, i, a.tile(i, j, kt))
                    act.wait_ge(S("att_pv"), a.used(i, j, a.before_in_buffer(kt)) + 1 + PRIMED["att_pv"])
                    if a.causal:
                        nc.scalar.activation(e[:, c], g[:, c], ACT.Exp, scale=a.scale).then_inc(free, 1)
                        evicted(act, a.name, tiles, i, a.tile(i, j, kt))
                    nc.scalar.activation(a.E[0][kt % 3][:, c], e[:, c], ACT.Copy).then_inc(S("att_hi"), 1)
                    if j + 1 < a.H and kt == a.nkt - 2:
                        rows_hi(i, j + 1)
                    if j >= 1 and kt == a.nkt - 2 and not a.causal:
                        part_hi(i, j - 1)
                    if j + 1 < a.H and kt == a.nkt - 2:
                        rows_send(i, j + 1)
                out(i, j)
                if j == a.H - 1 and not a.causal:
                    part_hi(i, j)

            return rows_hi, rows_send, body

        def att_dve(dve, a):
            def chunk(i, j, c):
                qt, c0, c1, part = a.chunks[c]
                n = a.chunk(i, j, c)
                dve.wait_ge(S("att_s"), n + 1)
                b = (6 + c % 2) * HALF
                nc.vector.reduce_max(mx[:, part * 8 + qt:part * 8 + qt + 1], ps[:, b:b + c1 - c0], AXX).then_inc(S("att_max"), 1)

            def combine(i, j):
                dve.wait_ge(S("att_max"), a.chunk(i, j, a.C - 1) + 1 + PRIMED["att_max"])
                dve.wait_ge(S("att_mlo"), a.flip(i, j) + PRIMED["att_mlo"])
                nc.vector.reduce_max(mxf[:, 0:8], mx[:, 0:8 * a.parts].rearrange("p (c q) -> p q c", q=8), AXX).then_inc(S("att_mx"), 1)

            def rows_lo(i, j):
                dve.wait_ge(S("att_mhi"), a.flip(i, j) + 1)
                nc.vector.scalar_tensor_tensor(mrow[1][0:8, :], ps[0:8, 6 * HALF:6 * HALF + P], -1.0, f32(mrow[0][0:8, :]), ALU.mult,
                                               ALU.subtract).then_inc(S("att_mlo"), 1)

            def low(i, j, kt):
                c = slice(a.queries(kt), T)
                dve.wait_ge(S("att_hi"), a.unit(i, j, kt) + 1)
                nc.vector.tensor_tensor(a.E[1][kt % 3][:, c], a.E[2][kt % len(a.E[2])][:, c], f32(a.E[0][kt % 3][:, c]), ALU.subtract).then_inc(S("att_lo"), 1)

            def inverse(i, j, q):
                c = slice(T * q // a.pieces, T * (q + 1) // a.pieces)
                r0 = a.heads[j][3]
                if not a.causal:
                    dve.wait_ge(S("att_out"), a.head(i, j) + 1 + PRIMED["att_out"])
                nc.vector.reciprocal(rs[r0:r0 + 64, c], (rs if a.causal else o32)[others(r0), c]).then_inc(S("att_rec"), 1)

            def product(i, j):
                r = slice(a.heads[j][3], a.heads[j][3] + 64)
                dve.wait_ge(S("att_rec"), a.rec0 + a.pieces * (a.H * i + j) + a.pieces)
                if a.causal:
                    dve.wait_ge(S("att_out"), a.head(i, j) + 1 + PRIMED["att_out"])
                y = Y32[:, i, :] if a.causal else o32
                nc.vector.tensor_tensor(y[r, :], y[r, :], rs[r, 0:T], ALU.mult).then_inc(S("att_y"), 1)

            def gated(i, j):
                r = slice(a.heads[j][3], a.heads[j][3] + 64)
                y = Y32[:, i, :]
                dve.wait_ge(S("att_sums"), 2 * i + j + 1)
                evicted(dve, "fox", 20, i, 3)
                nc.vector.tensor_tensor(y[r, :], PV[r, :], y[r, :], ALU.mult).then_inc(S("att_out"), 1)

            def part_lo(i, j):
                r = slice(a.heads[j][3], a.heads[j][3] + 64)
                dve.wait_ge(S("att_yhi"), a.head(i, j) + 1)
                nc.vector.tensor_tensor(ats[1][r, :], o32[r, :], f32(ats[0][r, :]), ALU.subtract).then_inc(S("att_ylo"), 1)

            def body(i, j):
                for kt in a.steps:
                    if j + 1 < a.H:
                        for c in a.of_step(kt):
                            chunk(i, j + 1, c)
                        if a.of_step(kt) and a.of_step(kt)[-1] == a.C - 1:
                            combine(i, j + 1)
                    low(i, j, kt)
                    if j + 1 < a.H and kt == a.nkt - 2:
                        rows_lo(i, j + 1)
                    if j >= 1:
                        if 1 <= kt < a.nkt - 2:
                            inverse(i, j - 1, kt - 1)
                        if kt == a.nkt - 2:
                            product(i, j - 1)
                        if kt == a.nkt - 1 and not a.causal:
                            part_lo(i, j - 1)
                if a.causal:
                    gated(i, j)
                if j == a.H - 1:
                    for q in range(a.pieces):
                        inverse(i, j, q)
                    product(i, j)
                    if not a.causal:
                        part_lo(i, j)

            def scores(i, j):
                for c in range(a.C):
                    chunk(i, j, c)
                combine(i, j)

            return scores, rows_lo, body

        def on(stage):
            return ORDER.index(stage) <= upto

        def sp_program(sp):
            def load_panel(stage, per, i, j):
                if isinstance(i, int):
                    j, i = j + per * i, 0
                n = P0[stage] + LEAD + j
                q = n + per * i
                sp.wait_ge(S("split"), q - 1)
                sp.dma_start(raw[n % 2][:, :], d["w"][q]).then_inc(S(f"loaded{n % 2}"), 16)

            def ada_chunk(c, slot):
                sp.dma_start(adas[slot][:, :, :], d["ada"][c]).then_inc(S(f"ada_loaded{slot}"), 16)

            sp.dma_start(cols[:, :], d["cols"]).then_inc(S("cols_loaded"), 16)
            sp.dma_start(Mraw[:, :, :], d["mem"]).then_inc(S("memt_loaded"), 16)
            for q in range(2):
                sp.dma_start(raw[q][:, :], d["w"][q]).then_inc(S(f"loaded{q}"), 16)
            ada_chunk(0, 0)
            ada_chunk(1, 1)
            sp.dma_start(XT[:, :, :], d["x"]).then_inc(S("x_loaded"), 16)
            sp.dma_start(CT[:, :, :], d["ctx"]).then_inc(S("ctx_loaded"), 16)
            for name, t in (("ident", ident),):
                sp.dma_start(t[:, :], d[name]).then_inc(S("consts"), 16)
            sp.dma_start(poolc[:, :, :], d["poolc"]).then_inc(S("consts"), 16)
            for q in range(2, LEAD):
                sp.wait_ge(S("split"), q - 1)
                sp.dma_start(raw[q % 2][:, :], d["w"][q]).then_inc(S(f"loaded{q % 2}"), 16)

            with sp.Fori(0, 2) as l:
                for j in range(4):
                    load_panel("mem", 8, l, j)
                    sp.wait_ge(S("ada_used"), 4 * l + j + 1)
                    ada_chunk(4 * l + j + 2, j % 2)
                for t in (2, 3):
                    evicted(sp, "mem", 4, l, t)
                for n in range(2):
                    sp.dma_start(mk_d[l, n], f32(mks[n][:, :, :])).then_inc(S("mk_stored"), 16)
                for j in range(4, 8):
                    load_panel("mem", 8, l, j)
                sp.wait_ge(S("mv_lo"), l + 1 + PRIMED["mv_lo"])
                for n in range(2):
                    sp.dma_start(mv_d[l, n], f32(mvs[n][:, :, :])).then_inc(S("mv_stored"), 16)
            c = 10
            for stage in ("lat", "f"):
                if on(stage):
                    for j in range(4):
                        load_panel(stage, 4, 0, j)
                        for _ in range(2):
                            if c < 24:
                                sp.wait_ge(S("ada_used"), c - 1)
                                ada_chunk(c, c % 2)
                                c += 1
            if on("gates"):
                sp.wait_ge(S("ada_cols"), 2)
                sp.dma_start(cosT[0:QK, :], d["cos"]).then_inc(S("rope_loaded"), 16)
                sp.dma_start(sinT[0:QK, :], d["sin"]).then_inc(S("rope_loaded"), 16)

                def store_unit(i, u):
                    sp.wait_ge(S("prep_lo"), 4 * i + u + 1 + PRIMED["prep_lo"])
                    dst = (q_d, k_d)[u % 2]
                    w = (T, KEYS)[u % 2]
                    for n in range(2):
                        sp.dma_start(dst[2 * i + u // 2, n], f32(phd[n][0:QK, 0:w])).then_inc(S("prep_stored"), 16)

                def store_gate(i, t):
                    evicted(sp, "gates", 4, i, t)
                    sp.dma_start(gate_d[4 * i + t], gst[t % 2][:, :]).then_inc(S(f"gate_stored{t % 2}"), 16)

                with sp.Fori(0, 4) as i:
                    for j in range(8):
                        load_panel("gates", 8, i, j)
                        if j in (1, 3, 5):
                            store_unit(i, j // 2)
                        if j in (2, 4, 6):
                            store_gate(i, j // 2 - 1)
                    store_unit(i, 3)
                    store_gate(i, 3)
            if on("v"):
                load_panel("v", 1, 0, 0)
                sp.wait_ge(S("v_lo"), 10)
                for n, t in enumerate((Vhi, Vlo)):
                    for r in range(4):
                        sp.dma_start(v_d[n, r], f32(t[:, :, P * r:P * r + P])).then_inc(S("v_stored"), 16)
            if on("mla"):
                def load_head(i, j):
                    Q, K, V, r0 = mla_heads[j]
                    for n in range(2):
                        sp.dma_start(f32(Q[n][0:QK, :]), q_d[4 * i + j, n]).then_inc(S(f"mla_loaded{j}"), 16)
                        sp.dma_start(f32(K[n][0:QK, :]), k_d[4 * i + j, n]).then_inc(S(f"mla_loaded{j}"), 16)
                        sp.dma_start(f32(V[n][:, :, r0:r0 + 64]), v_d[n, 2 * i + j // 2][:, :, r0:r0 + 64]).then_inc(S(f"mla_loaded{j}"), 16)

            if on("dft"):
                for h in range(2):
                    for j in range(10):
                        load_panel("dft", 10, h, j)
                    if h == 0 and on("mla"):
                        sp.wait_ge(S("prep_stored"), 16 * 32 + PRIMED["prep_stored"])
                        sp.wait_ge(S("v_stored"), 16 * 8)
                        load_head(0, 0)
                    if h == 0:
                        sp.wait_ge(S("fm_lo"), 4 + PRIMED["fm_lo"])
                    else:
                        sp.wait_ge(S("panel_done"), P0["dft"] + 20)
                        if on("mla"):
                            for j in range(1, 4):
                                load_head(0, j)
                        sp.wait_ge(S("fm_lo"), 8 + PRIMED["fm_lo"])
                    for n in range(2):
                        sp.dma_start(fm_d[n].rearrange("g p f -> p g f")[:, :, h * HALF:(h + 1) * HALF],
                                     f32(fms[n][:, :, :])).then_inc(S("fm_stored"), 16)
            if on("mla"):
                for i in range(2):
                    for j in range(4):
                        if i == 0:
                            sp.wait_ge(S("att_pv"), mla.used(i, j, 9) + 1 + PRIMED["att_pv"])
                            load_head(1, j)
                        if i == 1 and j == 2 and on("merge"):
                            sp.wait_ge(S("att_pv"), mla.used(i, j, 9) + 1 + PRIMED["att_pv"])
                            sp.wait_ge(S("fm_stored"), 16 * 4 + PRIMED["fm_stored"])
                            for n in range(2):
                                sp.dma_start(f32(Fm[n][:, :, :]), fm_d[n].rearrange("g p t -> p g t")).then_inc(S("f_loaded"), 16)
                            sp.wait_ge(S("att_stored"), 32 * 3 + PRIMED["att_stored"])
                            sp.dma_start(f32(At[0][:, 0:3, :]), at_d[0, 0:3].rearrange("g p t -> p g t")).then_inc(S("a_loaded"), 16)
                        if j % 2 == 1:
                            sp.wait_ge(S("att_ylo"), mla.head(i, j) + 1 + PRIMED["att_ylo"])
                            for n in range(2):
                                sp.dma_start(at_d[n, 2 * i + j // 2], f32(ats[n][:, :])).then_inc(S("att_stored"), 16)
            if on("merge"):
                sp.wait_ge(S("att_stored"), 32 * 4 + PRIMED["att_stored"])
                sp.dma_start(f32(At[0][:, 3:4, :]), at_d[0, 3:4].rearrange("g p t -> p g t")).then_inc(S("a_loaded"), 16)
                sp.dma_start(f32(At[1][:, :, :]), at_d[1].rearrange("g p t -> p g t")).then_inc(S("a_loaded"), 16)
                sp.wait_ge(S("gate_stored0"), 16 * 8 + PRIMED["gate_stored"])
                sp.wait_ge(S("gate_stored1"), 16 * 8 + PRIMED["gate_stored"])
                with sp.Fori(0, 4) as i:
                    for j in range(2):
                        for q in range(2):
                            sp.wait_ge(g_free[q], T0["merge"] // 2 + 2 * i + j - 1 + PRIMED["g_free"])
                        for n in range(2):
                            sp.dma_start(sg[j][n][:, :], gate_d[2 * i + j + 8 * n]).then_inc(S(f"sg_loaded{j}"), 16)
                        load_panel("merge", 2, i, j)
            if on("wout"):
                sp.wait_ge(S("y_lo"), 8 + PRIMED["y_lo"])
                sp.dma_start(X1[:, :, :], d["x"]).then_inc(S("x_loaded"), 16)
                with sp.Fori(0, 4) as i:
                    for j in range(2):
                        load_panel("wout", 2, i, j)
            if on("mlp"):
                with sp.Fori(0, 4) as i:
                    for j in range(16):
                        load_panel("mlp", 16, i, j)

            def mem_heads(l):
                st = f"mem{l + 1}"
                sp.wait_ge(S("mk_stored"), 64 + PRIMED["mk_stored"])
                sp.wait_ge(S("mv_stored"), 64 + PRIMED["mv_stored"])
                if l == 0:
                    sp.wait_ge(S("pm_lo"), 8)
                    sp.wait_ge(S("panel_done"), P0["pool"] + 20)
                else:
                    sp.wait_ge(S("att_out"), 24 + PRIMED["att_out"])
                with sp.Fori(0, 2) as i:
                    sp.wait_ge(S("mem_pv"), 4 * l + 2 * i + PRIMED["mem_pv"])
                    for j in range(2):
                        for n in range(2):
                            sp.dma_start(f32(Km[j][n][:, :]), mk_d[l, n][:, 2 * i + j, :]).then_inc(S("mem_kv"), 16)
                            sp.dma_start(f32(Vm[j][n][:, :, :]), mv_d[l, n][:, :, bass.ds(i * 256 + j * P, P)]).then_inc(S("mem_kv"), 16)
                    for j in range(4):
                        load_panel(st, 4, i, j)

            def out_proj(l):
                st = f"out{l + 1}"
                with sp.Fori(0, 2) as i:
                    for j in range(6):
                        load_panel(st, 6, i, j)

            if on("pool"):
                for g in range(4):
                    for j in range(5):
                        load_panel("pool", 5, g, j)
            if on("mem1"):
                mem_heads(0)
            if on("out1"):
                out_proj(0)
            if on("forget"):
                sp.dma_start(maskc[:, :], d["mask"]).then_inc(S("consts"), 16)
                load_panel("forget", 1, 0, 0)
                sp.wait_ge(S("cum"), 4)
                for s_, t in enumerate((nch, mch)):
                    for n in range(2):
                        sp.dma_start(cum_d[:, s_, n], f32(t[n][0:FOX, :])).then_inc(S("cum_stored"), 16)
                sp.wait_ge(S("cum_stored"), 64)
                sp.wait_ge(S("aug"), 20)
            if on("fox"):
                with sp.Fori(0, 8) as i:
                    sp.wait_ge(S("att_pv"), fox.used(i, 0, 0) + PRIMED["att_pv"])
                    for j in range(2):
                        for n in range(2):
                            sp.dma_start(f32(Kf[j][n][64:65, :]), cum_d[bass.ds(2 * i + j, 1), 0, n]).then_inc(S("fox_cum"), 16)
                            sp.dma_start(f32(Qf[j][n][65:66, :]), cum_d[bass.ds(2 * i + j, 1), 1, n]).then_inc(S("fox_cum"), 16)
                    for j in range(4):
                        load_panel("fox", 4, i, j)
            if on("mem2"):
                mem_heads(1)
            if on("out2"):
                out_proj(1)
                with sp.Fori(0, 4) as i:
                    for j in range(2):
                        sp.wait_ge(S("ln2_out"), 2 * i + j + 1)
                        sp.dma_start(out[2 * i + j], tmp[j][:, 0:T]).then_inc(S(f"out_stored{j}"), 16)
                for j in range(2):
                    sp.wait_ge(S(f"out_stored{j}"), 64)
            if dbg is not None:
                dbg(sp, S, at)

        def pool_program(gp):
            def split(n, i=0, per=0, w=PW):
                q = n + per * i
                b = n % 2
                gp.wait_ge(S(f"loaded{b}"), 16 * (n // 2 + 1 + (per // 2) * i))
                if n >= 2:
                    gp.wait_ge(S("panel_done"), q - 1)
                nc.gpsimd.tensor_tensor(whi[b][:, 0:w], raw[b][:, 0:w], onesf[:, 0:1].to_broadcast([P, w]), ALU.mult).then_inc(S("split_hi"), 1)
                gp.wait_ge(S("split_hi"), q + 1)
                nc.gpsimd.tensor_tensor(wlo[b][:, 0:w], raw[b][:, 0:w], f32(whi[b][:, 0:w]), ALU.subtract).then_inc(S("split"), 1)

            def splits(stage, per, count, i=0):
                for j in range(count):
                    split(P0[stage] + SPLIT_LEAD + j, i, per)

            gp.wait_ge(S("ones"), 1)
            for n in range(SPLIT_LEAD):
                split(n)
            with gp.Fori(0, 2) as l:
                splits("mem", 8, 8, l)
            for stage in ("lat", "f"):
                if on(stage):
                    splits(stage, 0, 4)
            if on("gates"):
                with gp.Fori(0, 4) as i:
                    for j in range(8):
                        split(P0["gates"] + SPLIT_LEAD + j, i, 8, w=(FW, PW, P, PW)[(SPLIT_LEAD + j) % 4])
            if on("v"):
                splits("v", 0, 1)
            if on("dft"):
                with gp.Fori(0, 2) as i:
                    splits("dft", 10, 10, i)
            for stage, per, n in (("merge", 2, 4), ("wout", 2, 4), ("mlp", 16, 4)):
                if on(stage):
                    with gp.Fori(0, n) as i:
                        splits(stage, per, per, i)
            if on("pool"):
                splits("pool", 0, 20)
            for stage, per, n in (("mem1", 4, 2), ("out1", 6, 2), ("forget", 1, 1), ("fox", 4, 8), ("mem2", 4, 2),
                                  ("out2", 6, 2)):
                if on(stage):
                    if n == 1:
                        splits(stage, 0, 1)
                    else:
                        with gp.Fori(0, n) as i:
                            splits(stage, per, per, i)

        def pe_program(pe):
            def panel(stage, per, i, j):
                if isinstance(i, int):
                    j, i = j + per * i, 0
                n = P0[stage] + j
                pe.wait_ge(S("split"), n + per * i + 1)
                return whi[n % 2], wlo[n % 2]

            def done(last):
                last.then_inc(S("panel_done"), 1)

            def blocks(o, wh, wl, xh, xl, ks, first, last, k0=0, w=T, off=0, ready=None):
                for n, b in enumerate(ks):
                    c = off + P * b
                    if ready is not None:
                        ready(k0 + n)
                    for h in range(0, w, HALF):
                        e = min(h + HALF, w)
                        st, sp_ = first and n == 0, last and n == len(ks) - 1
                        ins = mm3(o[:, h:e], wh[:, c:c + P], wl[:, c:c + P], xh[:, k0 + n, h:e], xl[:, k0 + n, h:e], st, sp_)
                return ins

            def tile(stage, per, i, j, tiles, t, xh, xl, ready=None):
                wh, wl = panel(stage, per, i, j)
                o = pair(pe, stage, tiles, i, t)
                done(blocks(o, wh, wl, xh, xl, range(KT), True, True, ready=ready))

            pe.wait_ge(S("memt_lo"), 1)
            with pe.Fori(0, 2) as l:
                for hd in range(MH):
                    wh, wl = panel("mem", 8, l, hd)
                    o = pair(pe, "mem", 4, l, hd)
                    done(blocks(o, wh, wl, Mhi, Mlo, range(KT), True, True, w=CTX))
                for n in range(4):
                    wh, wl = panel("mem", 8, l, 4 + n)
                    if n == 0:
                        pe.wait_ge(S("mv_lo"), l + PRIMED["mv_lo"])
                    for tt in range(2):
                        for k in range(2):
                            kt = 2 * n + k
                            last = mm3(ps[:, (4 + tt) * HALF:(5 + tt) * HALF], Mhi[:, kt, tt * P:tt * P + P],
                                       Mlo[:, kt, tt * P:tt * P + P], whi_of(wh, k), whi_of(wl, k), kt == 0, kt == 7)
                    done(last)
            pe.wait_ge(S("ones"), 1)
            pe.wait_ge(S("ada_used"), 8)
            pe.wait_ge(S("ada_c"), 8)
            for n in range(16):
                nc.tensor.matmul(ps[:, 6 * HALF + n:6 * HALF + n + 1], accx[:, P * n:P * n + P], onesf[:, 0:1], start=True, stop=True)
            for n in range(16):
                last = nc.tensor.matmul(ps[:, 6 * HALF + 48 + n:6 * HALF + 49 + n], accc[:, P * n:P * n + P], onesf[:, 0:1], start=True, stop=True)
            last.then_inc(S("ada_cols"), 1)
            pe.wait_ge(S("mv_lo"), 2 + PRIMED["mv_lo"])
            pe.wait_ge(S("sq_acc"), 8)
            for h in range(2):
                nc.tensor.matmul(ps[:, (4 + h) * HALF:(5 + h) * HALF], onesf[:, :], acc[:, h * HALF:(h + 1) * HALF], start=True, stop=True)
            pe.wait_ge(S("sq_acc"), 16)
            nc.tensor.matmul(ps[:, 7 * HALF:7 * HALF + CTX], onesf[:, :], acc[:, T:KEYS], start=True, stop=True).then_inc(S("norm_sum"), 1)
            if on("lat"):
                for t in range(4):
                    if t < 2:
                        tile("lat", 4, 0, t, 4, t, Hhi, Hlo, ready=(lambda k: pe.wait_ge(S("ap_lo"), k + 1)) if t == 0 else None)
                    else:
                        wh, wl = panel("lat", 4, 0, t)
                        o = pair(pe, "lat", 4, 0, t)
                        blocks(o, wh, wl, Hhi, Hlo, range(KT), True, True)
                        pe.wait_ge(S("ap_lo"), 16)
                        o = ps[:, (2 + t) * HALF:(2 + t) * HALF + CTX]
                        done(blocks(o, wh, wl, HChi, HClo, range(KT), True, True, w=CTX))
            if on("f"):
                for n in range(4):
                    wh, wl = panel("f", 4, 0, n)
                    for tt in range(KT):
                        if n == 0:
                            if tt in (0, 2):
                                pe.wait_ge(g_free[tt // 2], (T0["lat"] + 4) // 2 + PRIMED["g_free"])
                            if tt == 4:
                                pe.wait_ge(S("lat_ctx"), 2)
                        for k in range(2):
                            kt = 2 * n + k
                            last = mm3(ps[:, tt * HALF:(tt + 1) * HALF], Hhi[:, kt, tt * P:tt * P + P], Hlo[:, kt, tt * P:tt * P + P],
                                       whi_of(wh, k), whi_of(wl, k), kt == 0, kt == 7)
                        if n == 3 and tt < 7:
                            last.then_inc(S("rows_full"), 1)
                    done(last)
                pe.wait_ge(S("f_lo"), 8)
                pe.wait_ge(S("ada_used"), 24)
                for n in range(32):
                    last = nc.tensor.matmul(ps[:, 6 * HALF + 16 + n:6 * HALF + 17 + n], acc2[:, P * n:P * n + P], onesf[:, 0:1], start=True, stop=True)
                last.then_inc(S("ada_cols"), 1)
                pe.wait_ge(S("lat_sq"), 1)
                for t in range(KT):
                    last = nc.tensor.matmul(ps[:, 7 * HALF + t:7 * HALF + t + 1], acc[:, t * P:t * P + P], onesf[:, 0:1], start=True, stop=True)
                last.then_inc(S("norm_sum"), 1)
                pe.wait_ge(S("lat_kvsq"), 1)
                for t in range(KEYS // P):
                    last = nc.tensor.matmul(ps[:, 3 * HALF + t:3 * HALF + t + 1], tmp[1][:, t * P:t * P + P], onesf[:, 0:1], start=True, stop=True)
                last.then_inc(S("norm_sum"), 1)
                pe.wait_ge(S("consts"), 32)
                for n, (c0, r_, count) in enumerate(((4 * HALF, rlat[0], KT), (0, rlat[1], KEYS // P))):
                    pe.wait_ge(S("norm_rs"), NORM["latq"] + 1 + n)
                    for t in range(count):
                        last = nc.tensor.matmul(ps[:, c0 + t * P:c0 + t * P + P], r_[:, t:t + 1].to_broadcast([P, P]), ident[:, :], start=True, stop=True)
                    last.then_inc(S("lat_rows"), 1)
            if on("gates"):
                pe.wait_ge(S("lat_t"), 3)
                with pe.Fori(0, 4) as i:
                    for hd in range(2):
                        for u in range(2):
                            n = 2 * hd + u
                            w = (T, KEYS)[u]
                            wh, wl = panel("gates", 8, i, 4 * hd + 2 * u)
                            if hd == 0 and u == 0:
                                pe.wait_ge(S("qn_lo"), 1)
                                pe.wait_ge(S("kvn_lo"), 1)
                            pe.wait_ge(S("prep_full"), 4 * i + n + PRIMED["prep_full"])
                            for c in range(0, w, HALF):
                                e = min(c + HALF, w)
                                if u == 0:
                                    for k in range(2):
                                        last = mm3(ps[0:QK, 4 * HALF + c:4 * HALF + e], wh[:, QK * k:QK * k + QK], wl[:, QK * k:QK * k + QK],
                                                   qnhi[:, k, c:e], qnlo[:, k, c:e], k == 0, k == 1)
                                else:
                                    last = mm3(ps[:, 4 * HALF + c:4 * HALF + e], wh[:, 0:P], wl[:, 0:P], kvhi[:, c:e], kvlo[:, c:e], True, True)
                            done(last)
                            wh, wl = panel("gates", 8, i, 4 * hd + 2 * u + 1)
                            o = pair(pe, "gates", 4, i, n)
                            blocks(o, wh, wl, Hhi, Hlo, range(3), True, False)
                            pe.wait_ge(S("prep_sq"), 4 * i + n + 1)
                            for t in range(w // P):
                                last = nc.tensor.matmul(ps[:, 7 * HALF + t:7 * HALF + t + 1], acc[0:QK, t * P:t * P + P], onesf[0:QK, 0:1], start=True, stop=True)
                            last.then_inc(S("prep_ss"), 1)
                            blocks(o, wh, wl, Hhi, Hlo, range(3, 6), False, False, k0=3)
                            pe.wait_ge(S("prep_rs"), 4 * i + n + 1)
                            pe.wait_ge(S("prep_a"), 4 * i + n + 1)
                            for t in range(w // P):
                                last = nc.tensor.matmul(ps[0:QK, 4 * HALF + t * P:4 * HALF + t * P + P], rcol[:, t:t + 1].to_broadcast([P, QK]), ident[:, :],
                                                        start=True, stop=True)
                            last.then_inc(S("prep_rows"), 1)
                            done(blocks(o, wh, wl, Hhi, Hlo, range(6, 8), False, True, k0=6))
            if on("v"):
                wh, wl = panel("v", 1, 0, 0)
                for tt in range(10):
                    if tt == 0:
                        for q in range(2):
                            pe.wait_ge(g_free[q], (T0["gates"] + 16) // 2 + PRIMED["g_free"])
                    if tt == 4:
                        pe.wait_ge(S("prep_full"), 16 + PRIMED["prep_full"])
                    if tt >= 8:
                        pe.wait_ge(S("v_lo"), tt - 7)
                    last = mm3(ps[:, (tt % 8) * HALF:(tt % 8 + 1) * HALF], kvhi[:, tt * P:tt * P + P], kvlo[:, tt * P:tt * P + P],
                               wh[:, 0:HALF], wl[:, 0:HALF], True, True)
                    if tt < 9:
                        last.then_inc(S("rows_full"), 1)
                done(last)
            if on("dft"):
                pe.wait_ge(S("v_lo"), 10)
                with pe.Fori(0, 2) as h:
                    for part in range(2):
                        for n in range(4):
                            wh, wl = panel("dft", 10, h, 4 * part + n)
                            if n == 0:
                                pe.wait_ge(S("fm_lo"), 4 * h + PRIMED["fm_lo"])
                                pe.wait_ge(S("ab_lo"), 8 * h + PRIMED["ab_lo"])
                            for g in range(NG):
                                for k in range(2):
                                    kt = 2 * n + k
                                    last = mm3(ps[:, (4 * part + g) * HALF:(4 * part + g + 1) * HALF], Fhi[:, kt, P * g:P * g + P],
                                               Flo[:, kt, P * g:P * g + P], whi_of(wh, k), whi_of(wl, k), kt == 0, kt == 7)
                            done(last)
                    for part in range(2):
                        wh, wl = panel("dft", 10, h, 8 + part)
                        for g in range(NG):
                            pe.wait_ge(S("ab_lo"), 8 * h + (4 if part == 0 else 5 + g) + PRIMED["ab_lo"])
                            last = mm3(ps[:, g * HALF:(g + 1) * HALF], wh[:, 0:P], wl[:, 0:P], ABhi[:, g, part, :], ABlo[:, g, part, :],
                                       part == 0, part == 1)
                        done(last)
            if on("mla"):
                pe.wait_ge(S("fm_lo"), 8 + PRIMED["fm_lo"])
                pe.wait_ge(S("consts"), 32)
                mla.loaded = lambda e, i, j: e.wait_ge(S(f"mla_loaded{j}"), 96 * i + 96)
                scores, flip_max, body = att_pe(pe, mla)
                with pe.Fori(0, 2) as i:
                    scores(i, 0)
                    flip_max(i, 0)
                    for j in range(4):
                        body(i, j)
            if on("merge"):
                pe.wait_ge(S("f_loaded"), 32)
                with pe.Fori(0, 4) as i:
                    for j in range(2):
                        wh, wl = panel("merge", 2, i, j)
                        for n, X in enumerate((Fm, At)):
                            o = pair(pe, "merge", 4, i, 2 * j + n)
                            if j == 0 and n == 1:
                                pe.wait_ge(S("a_loaded"), 48)
                            last = blocks(o, wh, wl, X[0], X[1], range(4 * n, 4 * n + 4), True, True)
                        done(last)
            if on("wout"):
                with pe.Fori(0, 4) as i:
                    for j in range(2):
                        if j == 0:
                            pe.wait_ge(S("y_lo"), 8 + PRIMED["y_lo"])
                        tile("wout", 2, i, j, 2, j, Yhi, Ylo)
                pe.wait_ge(S("n2_acc"), 8 + PRIMED["n2_acc"])
                for h in range(2):
                    last = nc.tensor.matmul(ps[:, (4 + h) * HALF:(5 + h) * HALF], onesf[:, :], acc[:, h * HALF:(h + 1) * HALF], start=True, stop=True)
                last.then_inc(S("norm_sum"), 1)
            if on("mlp"):
                with pe.Fori(0, 4) as i:
                    for t in range(8):
                        tile("mlp", 16, i, t, 16, t, Hb[0], Hb[1], ready=(lambda k: pe.wait_ge(S("ap_lo"), 16 + k + 1)) if t == 0 else None)
                    for t in range(8):
                        tile("mlp", 16, i, 8 + t, 16, 8 + t, Uhi, Ulo,
                             ready=(lambda k: pe.wait_ge(S("u_lo"), 8 * i + k + 1)) if t == 0 else None)
            if on("pool"):
                for g in range(4):
                    for t in range(4):
                        tile("pool", 5, g, t, 6, t, Hb[0], Hb[1], ready=(lambda k: pe.wait_ge(S("x2_lo"), k + 1)) if g == 0 and t == 0 else None)
                    wh, wl = panel("pool", 5, g, 4)
                    for t in range(2):
                        o = pair(pe, "pool", 6, g, 4 + t)
                        pe.wait_ge(S("pm_lo"), 2 * g + 2)
                        last = blocks(o, wh, wl, PMhi, PMlo, (2 * t, 2 * t + 1), True, True)
                    done(last)

            def mem_heads(l):
                st = f"mem{l + 1}"
                pe.wait_ge(S("identr"), 2)
                with pe.Fori(0, 2) as i:
                    for j in range(2):
                        tile(st, 4, i, j, 8, j, Hb[0], Hb[1])
                    for j in range(2):
                        evicted(pe, st, 8, i, j)
                        if j == 0:
                            pe.wait_ge(S("mem_kv"), 256 * l + 128 * i + 128)
                        for h in range(2):
                            o = 4 + 2 * h
                            if j == 1:
                                pe.wait_ge(S("att_max"), mem_c(l, i) + h + 1)
                            for q in range(4):
                                qc = slice((4 * h + q) * P, (4 * h + q + 1) * P)
                                last = mm3(ps[:, o * HALF + 256 * q:o * HALF + 256 * q + 256], Qm[j][0][:, qc], Qm[j][1][:, qc],
                                           Km[j][0][:, :], Km[j][1][:, :], True, True)
                            last.then_inc(S("att_s"), 1)
                    tile(st, 4, i, 2, 8, 2, Hb[0], Hb[1])
                    pe.wait_ge(S("att_mx"), mem_f(l, i) + 1)
                    nc.tensor.transpose(ps[0:16, 4 * HALF:4 * HALF + P], mxf[:, 0:16], ident[:, :]).then_inc(S("att_mt"), 1)
                    tile(st, 4, i, 3, 8, 3, Hb[0], Hb[1])
                    for j in range(2):
                        for kt in range(2):
                            n = mem_u(l, i) + 2 * j + kt
                            o = 4 + 2 * kt
                            if j == 0:
                                pe.wait_ge(S("att_row"), mem_r(l, i) + 64)
                            else:
                                pe.wait_ge(S("mem_exp"), 8 * l + 4 * i + kt + 1)
                            for c in range(2):
                                cs = slice(c * HALF, (c + 1) * HALF)
                                b = ps[:, (o + c) * HALF:(o + c + 1) * HALF]
                                mm3(b, Km[j][0][:, kt * P:kt * P + P], Km[j][1][:, kt * P:kt * P + P], Qm[j][0][:, cs], Qm[j][1][:, cs], True, False)
                                last = nc.tensor.matmul(b, onesr[64 * j:64 * j + 2, :], mr[64 * j:64 * j + 2, cs], start=False, stop=True)
                            last.then_inc(S("att_st"), 1)
                    for j in range(2):
                        pe.wait_ge(S("att_lo"), mem_u(l, i) + 2 * j + 2 + PRIMED["att_lo"])
                        o, sums = pair(pe, st, 8, i, 4 + 2 * j), pair(pe, st, 8, i, 5 + 2 * j)
                        for c in range(2):
                            cs = slice(c * HALF, (c + 1) * HALF)
                            for kt in range(2):
                                E = Em[kt]
                                mm3(o[:, cs], Vm[j][0][:, kt, :], Vm[j][1][:, kt, :], E[0][:, cs], E[1][:, cs], kt == 0, kt == 1)
                                for n in range(2):
                                    last = nc.tensor.matmul(sums[:, cs], onesr[:, :], E[n][:, cs], start=kt == 0 and n == 0, stop=kt == 1 and n == 1)
                        last.then_inc(S("mem_pv"), 1)

            def out_proj(l):
                st = f"out{l + 1}"
                with pe.Fori(0, 2) as i:
                    have = -1
                    for t in range(4):
                        o = pair(pe, st, 4, i, t)
                        b = 12 * t
                        while b < 12 * t + 12:
                            j = b // 8
                            if j != have:
                                wh, wl = panel(st, 6, i, j)
                                have = j
                            e = min(8 * j + 8, 12 * t + 12)
                            last = blocks(o, wh, wl, Yb[0], Yb[1], range(b - 8 * j, e - 8 * j), b == 12 * t, e == 12 * t + 12, k0=b - 12 * t,
                                          ready=(lambda k: pe.wait_ge(S("yb_lo"), MT * l + k + 1)) if t == 0 else None)
                            if e == 8 * j + 8:
                                done(last)
                            else:
                                last.then_inc(S("out_mid"), 1)
                            b = e
                pe.wait_ge(S("ln_acc"), 8 * (l + 1) + PRIMED["ln_acc"])
                for h in range(2):
                    last = nc.tensor.matmul(ps[:, (4 + h) * HALF:(5 + h) * HALF], onesf[:, :], acc[:, h * HALF:(h + 1) * HALF], start=True, stop=True)
                last.then_inc(S("norm_sum"), 1)
                pe.wait_ge(S("ln_mu"), l + 1)
                for k in range(KT):
                    pe.wait_ge(S("ln_sq"), 8 * l + k + 1)
                    for h in range(2):
                        last = nc.tensor.matmul(ps[:, (4 + h) * HALF:(5 + h) * HALF], onesf[:, :], tmp[k % 2][:, h * HALF:(h + 1) * HALF],
                                                start=k == 0, stop=k == KT - 1)
                    last.then_inc(S("ln_sqsum"), 1)

            if on("mem1"):
                mem_heads(0)
            if on("out1"):
                out_proj(0)
            if on("forget"):
                wh, wl = panel("forget", 1, 0, 0)
                pe.wait_ge(S("norm_ms"), 6)
                done(blocks(ps[:, 4 * HALF:6 * HALF], wh, wl, Hb[0], Hb[1], range(KT), True, True,
                            ready=lambda k: pe.wait_ge(S("ap_lo"), 24 + k + 1)))
            if on("fox"):
                fox.loaded = lambda e, i, j: e.wait_ge(S("fox_cum"), 128 * i + 128)
                scores, flip_max, body = att_pe(pe, fox)
                with pe.Fori(0, 8) as i:
                    for j in range(3):
                        tile("fox", 4, i, j, 20, j, Hb[0], Hb[1])
                    evicted(pe, "fox", 20, i, 0)
                    evicted(pe, "fox", 20, i, 1)
                    pe.wait_ge(S("logits_read"), 1)
                    pe.wait_ge(S("aug"), 20)
                    pe.wait_ge(S("identr"), 3)
                    scores(i, 0)
                    evicted(pe, "fox", 20, i, 2)
                    pe.wait_ge(S("att_out"), fox.head(i, 0) + PRIMED["att_out"])
                    for k in range(KT):
                        last = nc.tensor.transpose(ps[:, 4 * HALF + P * k:4 * HALF + P * k + P], tmp[0][:, P * k:P * k + P], ident[:, :])
                    last.then_inc(S("fox_vflip"), 1)
                    flip_max(i, 0)
                    tile("fox", 4, i, 3, 20, 3, Hb[0], Hb[1])
                    pe.wait_ge(S("fox_vlo"), 2 * i + 2)
                    for j in range(2):
                        body(i, j)
            if on("mem2"):
                mem_heads(1)
            if on("out2"):
                out_proj(1)

        def col(name, k=0):
            return cols[:, COLS[name] + k:COLS[name] + k + 1]

        NORM = {"n1": 0, "n1c": 1, "latq": 2, "latkv": 3, "n2": 4, "ln0": 5, "ln1": 6}
        APPLY = {"n1": 0, "n1c": 8, "n2": 16, "ln0": 24, "ln1": 32}

        def apply_dve(dve, s, n, src, w, lo, hi=None, c0=0):
            def scaled(k):
                if k >= 2:
                    dve.wait_ge(S("ap_lo"), APPLY[s] + k - 1)
                nc.vector.tensor_tensor(tmp[k % 2][:, c0:c0 + w], src(k), rs[:, c0:c0 + w], ALU.mult).then_inc(S("ap_t"), 1)

            def low(k):
                dve.wait_ge(S("ap_hi"), APPLY[s] + k + 1)
                nc.vector.tensor_tensor(lo(k), tmp[k % 2][:, c0:c0 + w], f32(hi(k)), ALU.subtract).then_inc(S("ap_lo"), 1)

            for k in range(n):
                scaled(k)
                if k >= 1:
                    low(k - 1)
            low(n - 1)

        def apply_act(act, s, n, w, hi, scale, shift, c0=0):
            for k in range(n):
                b = tmp[k % 2][:, c0:c0 + w]
                act.wait_ge(S("ap_t"), APPLY[s] + k + 1)
                nc.scalar.activation(b, b, ACT.Identity, scale=scale(k), bias=shift(k)).then_inc(S("ap_full"), 1)
                act.wait_ge(S("ap_full"), APPLY[s] + k + 1)
                nc.scalar.activation(hi(k), b, ACT.Copy).then_inc(S("ap_hi"), 1)

        def root(act, s, rows, a, b):
            act.wait_ge(S("norm_ms"), NORM[s] + 1)
            nc.scalar.activation(rs[0:rows, a:b], rs[0:rows, a:b], ACT.Sqrt).then_inc(S("norm_root"), 1)

        def mean_square(dve, s, src, count, eps, rows, a, b):
            nc.vector.tensor_scalar(rs[0:rows, a:b], src, 1.0 / count, eps, ALU.mult, ALU.add).then_inc(S("norm_ms"), 1)
            dve.wait_ge(S("norm_root"), NORM[s] + 1)
            nc.vector.reciprocal(rs[0:rows, a:b], rs[0:rows, a:b]).then_inc(S("norm_rs"), 1)
            dve.wait_ge(S("norm_rs"), NORM[s] + 1)

        def act_program(act):
            def copy(dst, src, sem, func=ACT.Copy, **kw):
                nc.scalar.activation(dst, src, func, **kw).then_inc(sem, 1)

            act.wait_ge(S("memt_loaded"), 16)
            copy(Mhi[:, :, :], Mraw[:, :, :], S("memt_hi"))
            act.wait_ge(S("cols_loaded"), 16)
            copy(sigc[:, :], cols[:, 0:16], S("sigc"), ACT.Sigmoid)
            act.wait_ge(S("x_loaded"), 16)
            for k in range(KT):
                if k >= 2:
                    act.wait_ge(S("sq_acc"), k - 1)
                copy(tmp[k % 2][:, 0:T], XT[:, k, :], S("sq"), ACT.Square)
            act.wait_ge(S("ctx_loaded"), 16)
            for k in range(KT):
                if k >= 2:
                    act.wait_ge(S("sq_acc"), 8 + k - 1)
                copy(tmp[k % 2][:, T:KEYS], CT[:, k, :], S("sq"), ACT.Square)
            with act.Fori(0, 2) as l:
                act.wait_ge(S("mk_stored"), 32 * l + PRIMED["mk_stored"])
                for hd in range(MH):
                    panels_done(act, "mem", 8, l, hd)
                    copy(mks[0][:, hd, :], pair_of("mem", hd)[0][:, 0:CTX], S("mk_hi"))
                panels_done(act, "mem", 8, l, 7)
                act.wait_ge(S("mv_stored"), 32 * l + PRIMED["mv_stored"])
                copy(mvs[0][:, :, :], ps[:, 4 * HALF:6 * HALF].rearrange("p (a b) -> p a b", a=2), S("mv_hi"))
            root(act, "n1", P, 0, T)
            root(act, "n1c", P, T, KEYS)
            act.wait_ge(S("mods"), 4)
            act.wait_ge(S("mk_stored"), 64 + PRIMED["mk_stored"])
            act.wait_ge(S("mv_stored"), 64 + PRIMED["mv_stored"])
            apply_act(act, "n1", KT, T, lambda k: Hhi[:, k, :], lambda k: scx[:, k:k + 1], lambda k: modx[:, k:k + 1])
            apply_act(act, "n1c", KT, CTX, lambda k: HChi[:, k, :], lambda k: scc[:, k:k + 1], lambda k: modc[:, k:k + 1], c0=T)
            if on("lat"):
                for t in range(4):
                    panels_done(act, "lat", 4, 0, t)
                    g, free = pair_of("lat", t)
                    if t < 2:
                        copy(ql[:, t, :], g, free)
                    else:
                        r, dst = ((slice(0, P), kvl), (slice(64, QK), kr))[t - 2]
                        copy(dst[r, 0:T], g[r, :], free)
                        copy(dst[r, T:KEYS], ps[r, (2 + t) * HALF:(2 + t) * HALF + CTX], S("lat_ctx"))
            if on("f"):
                for tt in range(KT):
                    if tt < 7:
                        act.wait_ge(S("rows_full"), tt + 1)
                    else:
                        panels_done(act, "f", 4, 0, 3)
                    copy(Fhi[:, tt, :], ps[:, tt * HALF:(tt + 1) * HALF], S("rows_hi"))
                evicted(act, "lat", 4, 0, 0)
                evicted(act, "lat", 4, 0, 1)
                act.wait_ge(S("ap_lo"), 16)
                for k in range(2):
                    copy(tmp[k][:, 0:T], ql[:, k, :], S("lat_s"), ACT.Square)
                evicted(act, "lat", 4, 0, 2)
                act.wait_ge(S("lat_ctx"), 2)
                act.wait_ge(S("lat_sq"), 1)
                copy(tmp[1][:, :], kvl[:, :], S("lat_kvsq"), ACT.Square)
                for n in range(2):
                    act.wait_ge(S("norm_ms"), NORM["latq"] + 1 + n)
                    copy(rlat[n][:, 0:KT + 2 * n], rlat[n][:, 0:KT + 2 * n], S("norm_root"), ACT.Sqrt)
                for k in range(2):
                    act.wait_ge(S("lat_t"), k + 1)
                    copy(ql[:, k, :], ql[:, k, :], S("lat_full"), scale=col("qng", k))
                    act.wait_ge(S("lat_full"), k + 1)
                    copy(qnhi[:, k, :], ql[:, k, :], S("lat_hi"))
                act.wait_ge(S("lat_t"), 3)
                copy(kvl[:, :], kvl[:, :], S("lat_full"), scale=col("kvng"))
                act.wait_ge(S("lat_full"), 3)
                copy(kvhi[:, :], kvl[:, :], S("lat_hi"))
            if on("gates"):
                evicted(act, "lat", 4, 0, 3)
                with act.Fori(0, 4) as i:
                    for u in range(4):
                        w = (T, KEYS)[u % 2]
                        panels_done(act, "gates", 8, i, 2 * u)
                        raw_ = ps[:, 4 * HALF:4 * HALF + w]
                        lo_, up = slice(0, NOPE), slice(NOPE, QK)
                        kg = COLS["kg"]
                        if u % 2 == 0:
                            copy(acc[0:QK, 0:w], raw_[0:QK, :], S("prep_sq"), ACT.Square)
                        else:
                            copy(acc[up, 0:w], kr[up, :], S("prep_x"), ACT.Square)
                            copy(acc[lo_, 0:w], raw_[lo_, :], S("prep_sq"), ACT.Square)
                        act.wait_ge(S("prep_lo"), 4 * i + u + PRIMED["prep_lo"])
                        if u % 2 == 0:
                            copy(tmp[0][0:QK, 0:w], raw_[0:QK, :], S("prep_a"), scale=cols[0:QK, COLS["qg"]:COLS["qg"] + 1])
                        else:
                            copy(tmp[0][lo_, 0:w], raw_[lo_, :], S("prep_x"), scale=cols[lo_, kg:kg + 1])
                            copy(tmp[0][up, 0:w], kr[up, :], S("prep_a"), scale=cols[up, kg:kg + 1])
                        act.wait_ge(S("prep_ms"), 4 * i + u + 1)
                        copy(rcol[:, 0:w // P], rcol[:, 0:w // P], S("prep_root"), ACT.Sqrt)
                        act.wait_ge(S("prep_full"), 4 * i + u + 1 + PRIMED["prep_full"])
                        act.wait_ge(S("prep_stored"), 128 * i + 32 * u + PRIMED["prep_stored"])
                        copy(phd[0][0:QK, 0:w], tmp[0][0:QK, 0:w], S("prep_hi"))
                        panels_done(act, "gates", 8, i, 2 * u + 1)
                        g, free = pair_of("gates", u)
                        act.wait_ge(S(f"gate_stored{u % 2}"), 32 * i + 16 * (u // 2) + PRIMED["gate_stored"])
                        copy(gst[u % 2][:, :], g, free, ACT.Sigmoid, bias=cols[:, bass.ds(4 * i + (COLS["b_gate"] + u), 1)])
            if on("v"):
                act.wait_ge(S("prep_stored"), 512 + PRIMED["prep_stored"])
                for n in range(2):
                    act.wait_ge(S(f"gate_stored{n}"), 128 + PRIMED["gate_stored"])
                for tt in range(10):
                    if tt < 9:
                        act.wait_ge(S("rows_full"), 7 + tt + 1)
                    else:
                        panels_done(act, "v", 1, 0, 0)
                    copy(Vhi[:, tt, :], ps[:, (tt % 8) * HALF:(tt % 8 + 1) * HALF], S("rows_hi"))
            if on("dft"):
                with act.Fori(0, 2) as h:
                    for part in range(2):
                        panels_done(act, "dft", 10, h, 4 * part + 3)
                        for g in range(NG):
                            copy(ABhi[:, g, part, :], ps[:, (4 * part + g) * HALF:(4 * part + g + 1) * HALF], S("dft_hi"))
                    panels_done(act, "dft", 10, h, 9)
                    act.wait_ge(S("fm_stored"), 32 * h + PRIMED["fm_stored"])
                    for g in range(NG):
                        copy(fms[0][:, g, :], ps[:, g * HALF:(g + 1) * HALF], S("dft_hi"))
            if on("mla"):
                act.wait_ge(S("fm_lo"), 8 + PRIMED["fm_lo"])
                act.wait_ge(S("consts"), 32)
                copy(identr[:, :], ident[:, :], S("identr"))
                copy(onesr[:, :], onesf[:, :], S("identr"))
                rows_hi, rows_send, body = att_act(act, mla)
                with act.Fori(0, 2) as i:
                    rows_hi(i, 0)
                    rows_send(i, 0)
                    for j in range(4):
                        body(i, j)
            if on("merge"):
                act.wait_ge(S("att_pv"), 80 + PRIMED["att_pv"])
                with act.Fori(0, 4) as i:
                    for j in range(2):
                        act.wait_ge(S("y_full"), 2 * i + j + 1)
                        copy(Yhi[:, 2 * i + j, :], mm1[:, :], S("y_hi"))
            if on("wout"):
                with act.Fori(0, 4) as i:
                    for j in range(2):
                        evicted(act, "wout", 2, i, j)
                        copy(tmp[j][:, 0:T], X1[:, 2 * i + j, :], S("n2_sq"), ACT.Square)
                root(act, "n2", P, 0, T)
                act.wait_ge(S("mods"), 6)
                apply_act(act, "n2", KT, T, lambda k: Hb[0][:, k, :], lambda k: sc2[:, k:k + 1], lambda k: modx[:, 24 + k:25 + k])
            if on("mlp"):
                with act.Fori(0, 4) as i:
                    for t in range(8):
                        panels_done(act, "mlp", 16, i, t)
                        g, free = pair_of("mlp", t)
                        if t >= 2:
                            act.wait_ge(S("u_lo"), 8 * i + t - 1)
                        copy(tmp[t % 2][:, 0:T], g, free, ACT.Relu)
                        act.wait_ge(S("u_sq"), 8 * i + t + 1)
                        copy(Uhi[:, t, :], tmp[t % 2][:, 0:T], S("u_hi"))
                panels_done(act, "mlp", 64, 0, 63)
                for k in range(KT):
                    evicted(act, "mlp", 16, 3, 8 + k)
                    copy(Hb[0][:, k, :], X1[:, k, :], S("x2_hi"))
            if on("pool"):
                for g4 in range(4):
                    for t in range(2):
                        panels_done(act, "pool", 5, g4, t)
                        g, free = pair_of("pool", t)
                        act.wait_ge(S("pm_lo"), 2 * g4)
                        copy(pu[t][:, 16:], g, free)
                    for t in range(2):
                        panels_done(act, "pool", 5, g4, 2 + t)
                        g, free = pair_of("pool", 2 + t)
                        if t == 1:
                            evicted(act, "pool", 6, g4, 2)
                        copy(sgm[:, :], g, S("pool_sig"), ACT.Sigmoid)
                        act.wait_ge(S("pm_full"), 2 * g4 + t + 1)
                        copy(PMhi[:, t, :], pm_buf(g4, t)[:, 16:], S("pm_hi"))

            def sums_out(l, i, j):
                h = 4 * l + 2 * i + j
                act.wait_ge(S("mem_pv"), h + 1 + PRIMED["mem_pv"])
                act.wait_ge(S("mem_y"), 4 * (2 * l + i) + PRIMED["mem_y"])
                g, free = pair_of(f"mem{l + 1}", 5 + 2 * j)
                copy(sums_m[j][:, 0:T], g, free)

            def mem_heads(l):
                st = f"mem{l + 1}"
                if l == 0:
                    act.wait_ge(S("pm_lo"), 8)
                    for t in range(2, 6):
                        evicted(act, "pool", 6, 3, t)
                else:
                    act.wait_ge(S("att_y"), 24)
                with act.Fori(0, 2) as i:
                    for j in range(2):
                        panels_done(act, st, 4, i, j)
                        g, free = pair_of(st, j)
                        copy(Qm[j][0][:, :], g, S("mem_qhi"))
                    panels_done(act, st, 4, i, 2)
                    g, free = pair_of(st, 2)
                    copy(tmp[0][:, 0:T], g, S("mem_sig"), ACT.Sigmoid)
                    act.wait_ge(S("att_mt"), mem_f(l, i) + 1)
                    copy(mrow[0][0:16, :], ps[0:16, 4 * HALF:4 * HALF + P], S("att_mhi"), scale=-1.0)
                    act.wait_ge(S("att_mlo"), mem_f(l, i) + 1 + PRIMED["att_mlo"])
                    for j in range(2):
                        for n in range(2):
                            nc.scalar.dma_start(f32(mr[64 * j + n:64 * j + n + 1, :]), f32(mrow[n][8 * j:8 * j + 8, :])).then_inc(S("att_row"), 16)
                    panels_done(act, st, 4, i, 3)
                    g, free = pair_of(st, 3)
                    copy(tmp[1][:, 0:T], g, S("mem_sig"), ACT.Sigmoid)
                    evicted(act, st, 8, i, 2)
                    evicted(act, st, 8, i, 3)
                    for j in range(2):
                        for kt in range(2):
                            u = 2 * j + kt
                            n = mem_u(l, i) + u
                            act.wait_ge(S("att_st"), n + 1)
                            act.wait_ge(S("att_lo"), n - 1 + PRIMED["att_lo"])
                            copy(tmp[kt][:, 0:T], ps[:, (4 + 2 * kt) * HALF:(6 + 2 * kt) * HALF], S("mem_exp"), ACT.Exp, scale=SCALE["mem"])
                            act.wait_ge(S("mem_exp"), 8 * l + 4 * i + u + 1)
                            act.wait_ge(S("mem_pv"), 4 * l + 2 * i + j + PRIMED["mem_pv"])
                            copy(Em[kt][0][:, :], tmp[kt][:, 0:T], S("att_hi"))
                        if j == 1:
                            sums_out(l, i, 0)
                    sums_out(l, i, 1)

            def out_proj(l):
                act.wait_ge(S("mem_pv"), 4 * (l + 1) + PRIMED["mem_pv"])
                act.wait_ge(S("att_lo"), mem_u(l, 2) + PRIMED["att_lo"])
                for f in range(MT):
                    if f == 8:
                        act.wait_ge(S("mem_y"), 8 * l + 8 + PRIMED["mem_y"])
                    copy(Yb[0][:, f, :], Y32[:, f, :], S("yb_hi"))
                act.wait_ge(S("ln_acc"), 8 * (l + 1) + PRIMED["ln_acc"])
                for k in range(KT):
                    act.wait_ge(S("ln_zc"), 8 * l + k + 1)
                    if k >= 2:
                        act.wait_ge(S("ln_sqsum"), 8 * l + k - 1)
                    copy(tmp[k % 2][:, 0:T], Z[:, k, :], S("ln_sq"), ACT.Square)
                root(act, f"ln{l}", P, 0, T)
                gcol, bcol = (lambda k: col("ln_g", 8 * l + k)), (lambda k: col("ln_b", 8 * l + k))
                if l == 0:
                    apply_act(act, "ln0", KT, T, lambda k: Hb[0][:, k, :], gcol, bcol)
                else:
                    for k in range(KT):
                        b = tmp[k % 2][:, 0:T]
                        act.wait_ge(S("ap_t"), APPLY["ln1"] + k + 1)
                        copy(b, b, S("ln2_out"), ACT.Identity, scale=gcol(k), bias=bcol(k))

            if on("mem1"):
                mem_heads(0)
            if on("out1"):
                out_proj(0)
            if on("forget"):
                r = slice(0, FOX)
                act.wait_ge(S("logits_read"), 1)
                copy(tmp[1][r, 0:T], tmp[0][r, 0:T], S("fg"), ACT.Abs)
                act.wait_ge(S("fg"), 1)
                copy(tmp[1][r, 0:T], tmp[1][r, 0:T], S("fg"), ACT.Exp, scale=-1.0)
                act.wait_ge(S("fg"), 2)
                copy(tmp[1][r, 0:T], tmp[1][r, 0:T], S("fg"), ACT.Ln, bias=1.0)
                act.wait_ge(S("cum"), 1)
                copy(nch[0][r, :], ncum[r, :], S("fg"))
            if on("fox"):
                act.wait_ge(S("cum_stored"), 64)
                act.wait_ge(S("consts"), 48)
                copy(maskr[:, :], maskc[:, :], S("identr"))
                rows_hi, rows_send, body = att_act(act, fox)
                with act.Fori(0, 8) as i:
                    for t in range(2):
                        panels_done(act, "fox", 4, i, t)
                        g, free = pair_of("fox", t)
                        for j in range(2):
                            copy((Kf, Qf)[t][j][0][0:64, :], g[64 * j:64 * j + 64, :], S("fox_hi"), scale=(1.0, 64 ** -0.5)[t])
                    panels_done(act, "fox", 4, i, 2)
                    g, free = pair_of("fox", 2)
                    copy(tmp[0][:, 0:T], g, free)
                    act.wait_ge(S("fox_vflip"), i + 1)
                    for j in range(2):
                        c = slice(64 * j, 64 * j + 64)
                        copy(Vf[j][0][:, :, c], PV.rearrange("p (k d) -> p k d", d=P)[:, :, c], S("fox_vhi"))
                    rows_hi(i, 0)
                    rows_send(i, 0)
                    panels_done(act, "fox", 4, i, 3)
                    g, free = pair_of("fox", 3)
                    act.wait_ge(S("att_y"), fox.head(i, 0))
                    copy(rs[:, 0:T], g, S("fox_sig"), ACT.Sigmoid)
                    for j in range(2):
                        body(i, j)
            if on("mem2"):
                mem_heads(1)
            if on("out2"):
                out_proj(1)

        def dve_program(dve):
            def sub(lo, x, hi, sem):
                nc.vector.tensor_tensor(lo, x, f32(hi), ALU.subtract).then_inc(sem, 1)

            def tt(o, a, b, op, sem):
                nc.vector.tensor_tensor(o, a, b, op).then_inc(sem, 1)

            nc.vector.memset(onesf[:, :], 1.0).then_inc(S("ones"), 1)
            c = 0
            for name, places in PRIMED.items():
                for sem in ([S(name)] if name not in ("gate_stored", "g_free") else [S(f"{name}{b}") for b in range(2)]):
                    for _ in range(places):
                        nc.vector.memset(primes[:, c:c + 1], 0.0).then_inc(sem, 1)
                        c += 1
            dve.wait_ge(S("memt_hi"), 1)
            sub(Mlo[:, :, :], Mraw[:, :, :], Mhi[:, :, :], S("memt_lo"))
            dve.wait_ge(S("sigc"), 1)
            tt(silc[:, :], cols[:, 0:16], sigc[:, :], ALU.mult, S("silc"))
            dve.wait_ge(S("silc"), 1)

            def ada(c, dst, sil0, sem, wait_self):
                for k in range(KT):
                    o = dst
                    w_ = adas[c % 2][:, k, :]
                    s_ = silc[:, sil0 + k:sil0 + k + 1]
                    if k == 0:
                        ins = nc.vector.tensor_scalar(o, w_, s_, None, ALU.mult)
                    else:
                        dve.wait_ge(S("ada_link"), wait_self(k))
                        ins = nc.vector.scalar_tensor_tensor(o, w_, s_, o, ALU.mult, ALU.add)
                    ins.then_inc(S("ada_link") if k < KT - 1 else S(sem), 1)

            dve.wait_ge(S("x_loaded"), 16)
            for k in range(KT):
                dve.wait_ge(S("sq"), k + 1)
                if k == 0:
                    nc.vector.tensor_copy(acc[:, 0:T], tmp[0][:, 0:T]).then_inc(S("sq_acc"), 1)
                else:
                    dve.wait_ge(S("sq_acc"), k)
                    tt(acc[:, 0:T], acc[:, 0:T], tmp[k % 2][:, 0:T], ALU.add, S("sq_acc"))
            for k in range(KT):
                dve.wait_ge(S("sq"), 8 + k + 1)
                if k == 0:
                    nc.vector.tensor_copy(acc[:, T:KEYS], tmp[0][:, T:KEYS]).then_inc(S("sq_acc"), 1)
                else:
                    dve.wait_ge(S("sq_acc"), 8 + k)
                    tt(acc[:, T:KEYS], acc[:, T:KEYS], tmp[k % 2][:, T:KEYS], ALU.add, S("sq_acc"))
            with dve.Fori(0, 2) as l:
                for hd in range(MH):
                    dve.wait_ge(S(f"ada_loaded{hd % 2}"), 32 * l + 16 * (hd // 2 + 1))
                    c = 4 * l + hd
                    ada(hd, accc[:, bass.ds(256 * c, 256)], 8, "ada_c", lambda k: 14 * (4 * l + hd) + k)
                    ada(hd, accx[:, bass.ds(256 * c, 256)], 0, "ada_used", lambda k: 14 * (4 * l + hd) + 7 + k)
                    dve.wait_ge(S("mk_hi"), 4 * l + hd + 1)
                    g, free = pair_of("mem", hd)
                    sub(mks[1][:, hd, :], g[:, 0:CTX], mks[0][:, hd, :], free)
                dve.wait_ge(S("mv_hi"), l + 1)
                sub(mvs[1][:, :, :], ps[:, 4 * HALF:6 * HALF].rearrange("p (a b) -> p a b", a=2), mvs[0][:, :, :], S("mv_lo"))
            dve.wait_ge(S("ada_cols"), 1)
            m6 = 6 * HALF
            ab = COLS["ada_b"]
            tt(modx[:, 0:16], ps[:, m6:m6 + 16], cols[:, ab:ab + 16], ALU.add, S("mods"))
            tt(modc[:, 0:16], ps[:, m6 + 48:m6 + 64], cols[:, ab:ab + 16], ALU.add, S("mods"))
            dve.wait_ge(S("mods"), 2)
            n1 = cols[:, COLS["n1"]:COLS["n1"] + 8]
            nc.vector.scalar_tensor_tensor(scx[:, :], modx[:, 8:16], 1.0, n1, ALU.add, ALU.mult).then_inc(S("mods"), 1)
            nc.vector.scalar_tensor_tensor(scc[:, :], modc[:, 8:16], 1.0, n1, ALU.add, ALU.mult).then_inc(S("mods"), 1)
            dve.wait_ge(S("norm_sum"), 1)
            mean_square(dve, "n1", ps[:, 4 * HALF:6 * HALF], D, EPS, P, 0, T)
            mean_square(dve, "n1c", ps[:, 7 * HALF:7 * HALF + CTX], D, EPS, P, T, KEYS)
            apply_dve(dve, "n1", KT, lambda k: XT[:, k, :], T, lambda k: Hlo[:, k, :], lambda k: Hhi[:, k, :])
            apply_dve(dve, "n1c", KT, lambda k: CT[:, k, :], CTX, lambda k: HClo[:, k, :], lambda k: HChi[:, k, :], c0=T)
            if on("f"):
                for c in range(8, 24):
                    dve.wait_ge(S(f"ada_loaded{c % 2}"), 16 * (c // 2 + 1))
                    ada(c, acc2[:, 256 * (c - 8):256 * (c - 7)], 0, "ada_used", lambda k: 112 + 7 * (c - 8) + k)
                for tt_ in range(KT):
                    dve.wait_ge(S("rows_hi"), tt_ + 1)
                    sub(Flo[:, tt_, :], ps[:, tt_ * HALF:(tt_ + 1) * HALF], Fhi[:, tt_, :], S("f_lo"))
                dve.wait_ge(S("lat_s"), 2)
                tt(acc[:, 0:T], tmp[0][:, 0:T], tmp[1][:, 0:T], ALU.add, S("lat_sq"))
                dve.wait_ge(S("ada_cols"), 2)
                tt(modx[:, 16:48], ps[:, m6 + 16:m6 + 48], cols[:, ab + 16:ab + 48], ALU.add, S("mods"))
                dve.wait_ge(S("mods"), 5)
                n2 = cols[:, COLS["n2"]:COLS["n2"] + 8]
                nc.vector.scalar_tensor_tensor(sc2[:, :], modx[:, 32:40], 1.0, n2, ALU.add, ALU.mult).then_inc(S("mods"), 1)
                for n, (c0, width) in enumerate(((7 * HALF, QL), (3 * HALF, P))):
                    dve.wait_ge(S("norm_sum"), 2 + n)
                    nc.vector.tensor_scalar(rlat[n][:, 0:KT + 2 * n], ps[:, c0:c0 + KT + 2 * n], 1.0 / width, EPS, ALU.mult, ALU.add).then_inc(S("norm_ms"), 1)
                for n in range(2):
                    dve.wait_ge(S("norm_root"), NORM["latq"] + 1 + n)
                    nc.vector.reciprocal(rlat[n][:, 0:KT + 2 * n], rlat[n][:, 0:KT + 2 * n]).then_inc(S("norm_rs"), 1)
                dve.wait_ge(S("lat_rows"), 1)
                for k in range(2):
                    tt(ql[:, k, :], ql[:, k, :], ps[:, 4 * HALF:6 * HALF], ALU.mult, S("lat_t"))
                dve.wait_ge(S("lat_rows"), 2)
                tt(kvl[:, :], kvl[:, :], ps[:, 0:KEYS], ALU.mult, S("lat_t"))
                for k in range(2):
                    dve.wait_ge(S("lat_hi"), k + 1)
                    sub(qnlo[:, k, :], ql[:, k, :], qnhi[:, k, :], S("qn_lo"))
                dve.wait_ge(S("lat_hi"), 3)
                sub(kvlo[:, :], kvl[:, :], kvhi[:, :], S("kvn_lo"))
            if on("gates"):
                dve.wait_ge(S("rope_loaded"), 32)
                with dve.Fori(0, 4) as i:
                    for u in range(4):
                        w = (T, KEYS)[u % 2]
                        r = slice(64, QK)
                        n = 4 * i + u
                        dve.wait_ge(S("prep_a"), n + 1)
                        nc.vector.memset(stat[:, 15:16], 0.0).then_inc(S("prep_go"), 1)
                        nc.vector.stream_shuffle(tmp[1][r, 0:w], tmp[0][r, 0:w], SHUFFLE).then_inc(S("prep_swap"), 1)
                        dve.wait_ge(S("prep_swap"), n + 1)
                        tt(tmp[1][r, 0:w], tmp[1][r, 0:w], sinT[r, 0:w], ALU.mult, S("prep_sin"))
                        tt(tmp[0][r, 0:w], tmp[0][r, 0:w], cosT[r, 0:w], ALU.mult, S("prep_cos"))
                        dve.wait_ge(S("prep_cos"), n + 1)
                        tt(tmp[0][r, 0:w], tmp[0][r, 0:w], tmp[1][r, 0:w], ALU.add, S("prep_rot"))
                        dve.wait_ge(S("prep_ss"), n + 1)
                        nc.vector.tensor_scalar(rcol[:, 0:w // P], ps[:, 7 * HALF:7 * HALF + w // P], 1.0 / QK, EPS, ALU.mult,
                                                ALU.add).then_inc(S("prep_ms"), 1)
                        dve.wait_ge(S("prep_root"), n + 1)
                        nc.vector.reciprocal(rcol[:, 0:w // P], rcol[:, 0:w // P]).then_inc(S("prep_rs"), 1)
                        dve.wait_ge(S("prep_rows"), n + 1)
                        dve.wait_ge(S("prep_rot"), n + 1)
                        tt(tmp[0][0:QK, 0:w], tmp[0][0:QK, 0:w], ps[0:QK, 4 * HALF:4 * HALF + w], ALU.mult, S("prep_full"))
                        dve.wait_ge(S("prep_hi"), n + 1)
                        sub(phd[1][0:QK, 0:w], tmp[0][0:QK, 0:w], phd[0][0:QK, 0:w], S("prep_lo"))
            if on("v"):
                dve.wait_ge(S("prep_lo"), 16 + PRIMED["prep_lo"])
                dve.wait_ge(S("prep_stored"), 512 + PRIMED["prep_stored"])
                for n in range(2):
                    dve.wait_ge(S(f"gate_stored{n}"), 128 + PRIMED["gate_stored"])
                for tt_ in range(10):
                    dve.wait_ge(S("rows_hi"), 8 + tt_ + 1)
                    sub(Vlo[:, tt_, :], ps[:, (tt_ % 8) * HALF:(tt_ % 8 + 1) * HALF], Vhi[:, tt_, :], S("v_lo"))
            if on("dft"):
                with dve.Fori(0, 2) as h:
                    for part in range(2):
                        for g in range(NG):
                            dve.wait_ge(S("dft_hi"), 12 * h + 4 * part + g + 1)
                            sub(ABlo[:, g, part, :], ps[:, (4 * part + g) * HALF:(4 * part + g + 1) * HALF], ABhi[:, g, part, :], S("ab_lo"))
                    for g in range(NG):
                        dve.wait_ge(S("dft_hi"), 12 * h + 8 + g + 1)
                        sub(fms[1][:, g, :], ps[:, g * HALF:(g + 1) * HALF], fms[0][:, g, :], S("fm_lo"))
            def ones_beside(Vs, r0):
                for n in range(2):
                    nc.vector.memset(f32(Vs[n][:, :, others(r0)]), 1.0 - n).then_inc(S("beside"), 1)

            if on("mla"):
                for j in range(4):
                    if j == 1:
                        dve.wait_ge(S("fm_lo"), 8 + PRIMED["fm_lo"])
                    Q, K, V, r0 = mla_heads[j]
                    ones_beside(V, r0)
                    for n in range(2):
                        nc.vector.memset(f32(K[n][96:97, :]), 1.0 - n).then_inc(S("beside"), 1)
                scores, rows_lo, body = att_dve(dve, mla)
                with dve.Fori(0, 2) as i:
                    scores(i, 0)
                    rows_lo(i, 0)
                    dve.wait_ge(S("fm_stored"), 64 + PRIMED["fm_stored"])
                    for j in range(4):
                        body(i, j)
            if on("merge"):
                dve.wait_ge(S("att_pv"), 80 + PRIMED["att_pv"])
                with dve.Fori(0, 4) as i:
                    for j in range(2):
                        panels_done(dve, "merge", 2, i, j)
                        dve.wait_ge(S(f"sg_loaded{j}"), 32 * i + 32)
                        dve.wait_ge(S("y_lo"), 2 * i + j + PRIMED["y_lo"])
                        for n, o in enumerate((mm1, mm2)):
                            g, free = pair_of("merge", 2 * j + n)
                            tt(o[:, :], g, sg[j][n][:, :], ALU.mult, free)
                        for n in range(2):
                            evicted(dve, "merge", 4, i, 2 * j + n)
                        tt(mm1[:, :], mm1[:, :], mm2[:, :], ALU.add, S("y_full"))
                        dve.wait_ge(S("y_hi"), 2 * i + j + 1)
                        sub(Ylo[:, 2 * i + j, :], mm1[:, :], Yhi[:, 2 * i + j, :], S("y_lo"))
            if on("wout"):
                dve.wait_ge(S("x_loaded"), 32)
                nc.vector.memset(acc[:, :], 0.0).then_inc(S("zeroed"), 1)
                dve.wait_ge(S("zeroed"), 1)
                with dve.Fori(0, 4) as i:
                    for j in range(2):
                        panels_done(dve, "wout", 2, i, j)
                        g, free = pair_of("wout", j)
                        x_ = X1[:, 2 * i + j, :]
                        nc.vector.scalar_tensor_tensor(x_, g, modx[:, bass.ds(2 * i + (16 + j), 1)], x_, ALU.mult, ALU.add).then_inc(free, 1)
                        dve.wait_ge(S("n2_sq"), 2 * i + j + 1)
                        dve.wait_ge(S("n2_acc"), 2 * i + j + PRIMED["n2_acc"])
                        tt(acc[:, 0:T], acc[:, 0:T], tmp[j][:, 0:T], ALU.add, S("n2_acc"))
                dve.wait_ge(S("norm_sum"), 4)
                mean_square(dve, "n2", ps[:, 4 * HALF:6 * HALF], D, EPS, P, 0, T)
                apply_dve(dve, "n2", KT, lambda k: X1[:, k, :], T, lambda k: Hb[1][:, k, :], lambda k: Hb[0][:, k, :])
            if on("mlp"):
                with dve.Fori(0, 4) as i:
                    def usq(t):
                        evicted(dve, "mlp", 16, i, t)
                        tt(tmp[t % 2][:, 0:T], tmp[t % 2][:, 0:T], tmp[t % 2][:, 0:T], ALU.mult, S("u_sq"))
                        dve.wait_ge(S("u_hi"), 8 * i + t + 1)
                        sub(Ulo[:, t, :], tmp[t % 2][:, 0:T], Uhi[:, t, :], S("u_lo"))
                    for t in range(8):
                        usq(t)
                    for k in range(8):
                        panels_done(dve, "mlp", 16, i, 8 + k)
                        g, free = pair_of("mlp", 8 + k)
                        nc.vector.scalar_tensor_tensor(X1[:, k, :], g, modx[:, 40 + k:41 + k], X1[:, k, :], ALU.mult, ALU.add).then_inc(free, 1)
                for k in range(KT):
                    dve.wait_ge(S("x2_hi"), k + 1)
                    sub(Hb[1][:, k, :], X1[:, k, :], Hb[0][:, k, :], S("x2_lo"))
            if on("pool"):
                dve.wait_ge(S("x2_hi"), 8)
                for b in (*pu, *pa):
                    nc.vector.memset(b[:, 0:16], 0.0).then_inc(S("zeroed"), 1)
                dve.wait_ge(S("zeroed"), 5)
                for g4 in range(4):
                    for t in range(2):
                        evicted(dve, "pool", 6, g4, t)
                        dve.wait_ge(S("pm_lo"), 2 * g4 + t)
                        src = pu[t]
                        for s_ in range(g4 + 1):
                            sh = 1 << s_
                            dst = pa[(s_ + g4) % 2]
                            tt(dst[:, 16:], src[:, 16:], src[:, 16 - sh:16 - sh + T], ALU.add, S("pool_sum"))
                            dve.wait_ge(S("pool_sum"), pool_count(g4, t, s_))
                            src = dst
                        o = pm_buf(g4, t)
                        tt(stat_pool[:, :], src[:, 16:32], poolc[:, g4, :], ALU.mult, S("pool_mean"))
                        nc.vector.scalar_tensor_tensor(o[:, 32:], src[:, 32:], 1.0 / (2 << g4), pu[t][:, 32:], ALU.mult,
                                                       ALU.subtract).then_inc(S("pool_mean"), 1)
                        dve.wait_ge(S("pool_mean"), 2 * (2 * g4 + t) + 1)
                        tt(o[:, 16:32], stat_pool[:, :], pu[t][:, 16:32], ALU.subtract, S("pm_full"))
                        dve.wait_ge(S("pool_mean"), 2 * (2 * g4 + t) + 2)
                        dve.wait_ge(S("pm_full"), 2 * g4 + t + 1)
                        dve.wait_ge(S("pool_sig"), 2 * g4 + t + 1)
                        if g4:
                            evicted(dve, "pool", 6, g4 - 1, 4 + t)
                        g, free = pair_of("pool", 2 + t)
                        tt(sil[t][:, :], g, sgm[:, :], ALU.mult, free)
                        dve.wait_ge(S("pm_hi"), 2 * g4 + t + 1)
                        sub(PMlo[:, t, :], o[:, 16:], PMhi[:, t, :], S("pm_lo"))
                    for t in range(2):
                        panels_done(dve, "pool", 5, g4, 4)
                        g, free = pair_of("pool", 4 + t)
                        evicted(dve, "pool", 6, g4, 2 + t)
                        nc.vector.scalar_tensor_tensor(Y32[:, 2 * g4 + t, :], g, col("pscale", 2 * g4 + t), sil[t][:, :], ALU.mult, ALU.mult).then_inc(free, 1)

            def values_out(l, i, j):
                h = 4 * l + 2 * i + j
                st = f"mem{l + 1}"
                dve.wait_ge(S("mem_pv"), h + 1 + PRIMED["mem_pv"])
                evicted(dve, st, 8, i, 2 + j)
                y = Y32[:, 2 * i + 8 + j, :]
                g, free = pair_of(st, 4 + 2 * j)
                nc.vector.tensor_tensor(y, g, y, ALU.mult).then_inc(free, 1)

            def mem_heads(l):
                st = f"mem{l + 1}"
                if l == 0:
                    for t in range(2, 6):
                        evicted(dve, "pool", 6, 3, t)
                else:
                    dve.wait_ge(S("att_y"), 24)
                with dve.Fori(0, 2) as i:
                    for j in range(2):
                        dve.wait_ge(S("mem_qhi"), 4 * l + 2 * i + j + 1)
                        g, free = pair_of(st, j)
                        sub(Qm[j][1][:, :], g, Qm[j][0][:, :], free)
                    dve.wait_ge(S("att_mlo"), mem_f(l, i) + PRIMED["att_mlo"])
                    for u in range(4):
                        j, h = u // 2, u % 2
                        dve.wait_ge(S("att_s"), mem_c(l, i) - 2 + u + 1)
                        nc.vector.reduce_max(mxf[:, 8 * j + 4 * h:8 * j + 4 * h + 4], ps[:, (4 + 2 * h) * HALF:(6 + 2 * h) * HALF].rearrange(
                            "p (q k) -> p q k", k=256), AXX).then_inc(S("att_max") if u < 3 else S("att_mx"), 1)
                    nc.vector.memset(stat[:, 14:15], 0.0).then_inc(S("att_max"), 1)
                    dve.wait_ge(S("mem_sig"), 4 * l + 2 * i + 1)
                    g, free = pair_of(st, 2)
                    tt(Y32[:, 2 * i + 8, :], g, tmp[0][:, 0:T], ALU.mult, free)
                    dve.wait_ge(S("att_mhi"), mem_f(l, i) + 1)
                    nc.vector.scalar_tensor_tensor(mrow[1][0:16, :], ps[0:16, 4 * HALF:4 * HALF + P], -1.0, f32(mrow[0][0:16, :]), ALU.mult,
                                                   ALU.subtract).then_inc(S("att_mlo"), 1)
                    dve.wait_ge(S("mem_sig"), 4 * l + 2 * i + 2)
                    g, free = pair_of(st, 3)
                    tt(Y32[:, 2 * i + 9, :], g, tmp[1][:, 0:T], ALU.mult, free)
                    for j in range(2):
                        for kt in range(2):
                            dve.wait_ge(S("att_hi"), mem_u(l, i) + 2 * j + kt + 1)
                            sub(Em[kt][1][:, :], tmp[kt][:, 0:T], Em[kt][0][:, :], S("att_lo"))
                        if j == 1:
                            values_out(l, i, 0)
                    values_out(l, i, 1)
                    for j in range(2):
                        h = 4 * l + 2 * i + j
                        evicted(dve, st, 8, i, 5 + 2 * j)
                        nc.vector.reciprocal(sums_m[j][:, 0:T], sums_m[j][:, 0:T]).then_inc(S("mem_y"), 1)
                        dve.wait_ge(S("mem_y"), 4 * (2 * l + i) + 1 + 2 * j + PRIMED["mem_y"])
                        evicted(dve, st, 8, i, 4 + 2 * j)
                        y = Y32[:, 2 * i + 8 + j, :]
                        tt(y, y, sums_m[j][:, 0:T], ALU.mult, S("mem_y"))

            def out_proj(l):
                st = f"out{l + 1}"
                for f in range(MT):
                    dve.wait_ge(S("yb_hi"), MT * l + f + 1)
                    sub(Yb[1][:, f, :], Y32[:, f, :], Yb[0][:, f, :], S("yb_lo"))
                nc.vector.memset(acc[:, :], 0.0).then_inc(S("zeroed"), 1)
                dve.wait_ge(S("zeroed"), 6 + l)
                with dve.Fori(0, 2) as i:
                    for t in range(4):
                        n = 4 * i + t
                        if t % 2 == 0:
                            dve.wait_ge(S("out_mid"), 4 * l + 2 * i + t // 2 + 1)
                        else:
                            panels_done(dve, st, 6, i, 3 * (t // 2) + 2)
                        g, free = pair_of(st, t)
                        b = tmp[t % 2][:, 0:T]
                        dve.wait_ge(S("ln_acc"), 8 * l + n + PRIMED["ln_acc"])
                        nc.vector.scalar_tensor_tensor(b, f32(Hb[0][:, n, :]), ALPHA, g, ALU.mult, ALU.add).then_inc(free, 1)
                        evicted(dve, st, 4, i, t)
                        nc.vector.scalar_tensor_tensor(Z[:, n, :], f32(Hb[1][:, n, :]), ALPHA, b, ALU.mult, ALU.add).then_inc(S("ln_z"), 1)
                        dve.wait_ge(S("ln_z"), 8 * l + n + 1)
                        tt(acc[:, 0:T], acc[:, 0:T], Z[:, n, :], ALU.add, S("ln_acc"))
                dve.wait_ge(S("norm_sum"), l + 5)
                nc.vector.tensor_scalar(rs[:, 0:T], ps[:, 4 * HALF:6 * HALF], 1.0 / D, None, ALU.mult).then_inc(S("ln_mu"), 1)
                dve.wait_ge(S("ln_mu"), l + 1)
                for k in range(KT):
                    tt(Z[:, k, :], Z[:, k, :], rs[:, 0:T], ALU.subtract, S("ln_zc"))
                dve.wait_ge(S("ln_sqsum"), 8 * l + 8)
                mean_square(dve, f"ln{l}", ps[:, 4 * HALF:6 * HALF], D, LN_EPS, P, 0, T)
                if l == 0:
                    apply_dve(dve, "ln0", KT, lambda k: Z[:, k, :], T, lambda k: Hb[1][:, k, :], lambda k: Hb[0][:, k, :])
                else:
                    for k in range(KT):
                        if k >= 2:
                            dve.wait_ge(S(f"out_stored{k % 2}"), 16 * (k // 2))
                        tt(tmp[k % 2][:, 0:T], Z[:, k, :], rs[:, 0:T], ALU.mult, S("ap_t"))

            if on("mem1"):
                mem_heads(0)
            if on("out1"):
                out_proj(0)
            if on("forget"):
                r = slice(0, FOX)
                panels_done(dve, "forget", 1, 0, 0)
                dve.wait_ge(S("ap_lo"), 32)
                nc.vector.tensor_scalar(tmp[0][r, 0:T], ps[r, 4 * HALF:6 * HALF], cols[r, COLS["bf"]:COLS["bf"] + 1], None,
                                        ALU.add).then_inc(S("logits_read"), 1)
                nc.vector.memset(rs[r, 0:T], 1.0).then_inc(S("gate_log"), 1)
                for x_ in (Kf, Qf):
                    for j in range(2):
                        for n in range(2):
                            nc.vector.memset(f32(x_[j][n][64:96, :]), 0.0).then_inc(S("aug"), 1)
                dve.wait_ge(S("aug"), 8)
                for x_ in (Kf, Qf):
                    for j in range(2):
                        for n in range(2):
                            nc.vector.memset(f32(x_[j][n][64:66, :]), 1.0 - n).then_inc(S("aug"), 1)
                for j in range(2):
                    for n in range(2):
                        nc.vector.memset(f32(Kf[j][n][96:97, :]), 1.0 - n).then_inc(S("aug"), 1)
                dve.wait_ge(S("fg"), 3)
                nc.vector.tensor_scalar(tmp[0][r, 0:T], tmp[0][r, 0:T], 0.0, None, ALU.min).then_inc(S("gate_log"), 1)
                dve.wait_ge(S("gate_log"), 2)
                tt(acc[r, 0:T], tmp[1][r, 0:T], tmp[0][r, 0:T], ALU.subtract, S("gate_log"))
                dve.wait_ge(S("gate_log"), 3)
                nc.vector.tensor_tensor_scan(ncum[r, :], rs[r, 0:T], acc[r, 0:T], 0.0, ALU.mult, ALU.add).then_inc(S("cum"), 1)
                dve.wait_ge(S("fg"), 4)
                sub(nch[1][r, :], ncum[r, :], nch[0][r, :], S("cum"))
                dve.wait_ge(S("cum"), 2)
                for n in range(2):
                    nc.vector.tensor_scalar(mch[n][r, :], f32(nch[n][r, :]), -1.0, None, ALU.mult).then_inc(S("cum"), 1)
            if on("fox"):
                dve.wait_ge(S("cum_stored"), 64)
                nc.vector.memset(mx[:, 8:12], -3e38).then_inc(S("beside"), 1)
                for j in range(2):
                    ones_beside(Vf[j], 64 * j)
                scores, rows_lo, body = att_dve(dve, fox)
                with dve.Fori(0, 8) as i:
                    for t in range(2):
                        g, free = pair_of("fox", t)
                        for j in range(2):
                            dve.wait_ge(S("fox_hi"), 4 * i + 2 * t + j + 1)
                            nc.vector.scalar_tensor_tensor((Kf, Qf)[t][j][1][0:64, :], g[64 * j:64 * j + 64, :], (1.0, 64 ** -0.5)[t],
                                                           f32((Kf, Qf)[t][j][0][0:64, :]), ALU.mult, ALU.subtract).then_inc(free if j else S("fox_low"), 1)
                    scores(i, 0)
                    for j in range(2):
                        c = slice(64 * j, 64 * j + 64)
                        dve.wait_ge(S("fox_vhi"), 2 * i + 2)
                        sub(Vf[j][1][:, :, c], PV.rearrange("p (k d) -> p k d", d=P)[:, :, c], Vf[j][0][:, :, c], S("fox_vlo"))
                    rows_lo(i, 0)
                    dve.wait_ge(S("fox_sig"), i + 1)
                    g, free = pair_of("fox", 3)
                    tt(Y32[:, i, :], g, rs[:, 0:T], ALU.mult, free)
                    for j in range(2):
                        body(i, j)
            if on("mem2"):
                mem_heads(1)
            if on("out2"):
                out_proj(1)

        @block.sync
        def _(sp):
            sp_program(sp)

        @block.gpsimd
        def _(gp):
            pool_program(gp)

        @block.tensor
        def _(pe):
            pe_program(pe)

        @block.scalar
        def _(act):
            act_program(act)

        @block.vector
        def _(dve):
            dve_program(dve)


def _tiles(w):
    k, n = w.shape
    return w.reshape(k // P, P, n // P, P).transpose(2, 1, 0, 3).reshape(n // P, P, k)


def _moving(w):
    k, n = w.shape
    return w.reshape(k // 256, 2, P, n).transpose(0, 2, 1, 3).reshape(k // 256, P, 2 * n)


def _padded(a):
    return np.pad(a, ((0, 0), (0, 0), (0, PW - a.shape[2])))


def _feature_major(x):
    n = x.shape[0]
    return np.ascontiguousarray(x.T.reshape(KT, P, n).transpose(1, 0, 2))


def _stream(i):
    w_in, w_in2, w_kv2, kvb, qb = i["w_in"][0], i["w_in_2"], i["w_kv_shared_2"], i["w_kvb"][0], i["w_qb"][0]
    gates = _tiles(w_in[:, 928:])
    parts = []
    for layer in range(2):
        parts += [_tiles(i["w_mem_kv_2"][layer][:, :512]), _moving(i["w_mem_kv_2"][layer][:, 512:])]
    parts += [_tiles(w_in[:, 512:896]), _tiles(w_in[:, 832:960]), _moving(w_in[:, :512])]
    for h in range(NH):
        q = qb[:, QK * h:QK * h + QK].reshape(2, P, QK).transpose(1, 0, 2).reshape(1, P, 2 * QK)
        parts += [_padded(q), gates[2 * h:2 * h + 1], _padded(kvb[None, :, P * h:P * h + P]), gates[2 * h + 1:2 * h + 2]]
    parts.append(_padded(kvb.reshape(P, NH, P)[:, :, NOPE:].reshape(1, P, FW)))
    ang = 2 * np.pi * (np.outer(np.arange(T), np.arange(T)) % T) / T
    cos, sin = np.cos(ang).astype(np.float32), np.sin(ang).astype(np.float32)
    ch = 2 * np.pi * (np.outer(np.arange(P), np.arange(P)) % P) / P
    norm = 1 / math.sqrt(T * P)
    chc, chs = (np.cos(ch) * norm).astype(np.float32), (-np.sin(ch) * norm).astype(np.float32)
    for h in range(2):
        parts += [_moving(cos[:, HALF * h:HALF * h + HALF]), _moving(sin[:, HALF * h:HALF * h + HALF]), _padded(chc[None]), _padded(chs[None])]
    f, a = _tiles(i["w_fourier"][0]), _tiles(i["w_mla_o"][0])
    parts += [np.concatenate([f, a], axis=2), _tiles(i["w_out"][0])]
    for c in range(4):
        parts += [_tiles(i["w_up"][0][:, D * c:D * c + D]), _tiles(i["w_down"][0][D * c:D * c + D])]
    u, u2 = _tiles(w_in2[0]), _tiles(w_in2[1])
    for g in range(4):
        mix = i["pool_w_2"][0, g].reshape(2, P, 2, P).transpose(1, 2, 0, 3).reshape(1, P, 512)
        parts += [u[2 * g:2 * g + 2], u[MT + 2 * g:MT + 2 * g + 2], _padded(mix)]

    def mem(t):
        return np.concatenate([t[8:10], t[MT + 8:MT + 10], t[10:12], t[MT + 10:MT + 12]], axis=0)

    def proj(w):
        return _tiles(w).reshape(8, P, MT, P).transpose(0, 2, 1, 3).reshape(12, 8, P, P).transpose(0, 2, 1, 3).reshape(12, P, PW)

    parts += [mem(u), proj(i["w_out_2"][0])]
    fg = np.pad(w_kv2[:, 2 * D:], ((0, 0), (0, P - FOX)))
    k, v = _tiles(w_kv2[:, :D]), _tiles(w_kv2[:, D:2 * D])
    parts += [_tiles(fg), np.stack([k, u2[:8], v, u2[MT:MT + 8]], axis=1).reshape(32, P, PW), mem(u2), proj(i["w_out_2"][1])]
    parts.append(np.zeros((LEAD, P, PW), np.float32))
    w = np.concatenate(parts, axis=0)
    assert w.shape[0] == NP + LEAD, w.shape
    return w


def _columns(i):
    def c(a):
        a = a.reshape(-1)
        if a.shape[0] < P:
            a = np.pad(a, (0, P - a.shape[0]))
        return a.reshape(-1, P).T

    return np.ascontiguousarray(np.concatenate([c(i[n]) for n in (
        "c", "c_ctx", "ada_b", "norm1_g", "norm2_g", "b_gate", "q_norm_g", "kv_norm_g", "q_gain", "k_gain", "ln_g_2", "ln_b_2",
        "pool_scale_2", "b_forget_2")], axis=1))


def _rope():
    n = np.arange(T)
    freqs = (10000.0 ** (-np.arange(8, dtype=np.float32) / 8)).astype(np.float32)
    row, colu = (n // 64).astype(np.float32), (n % 64).astype(np.float32)
    ar, ac = row[:, None] * freqs, colu[:, None] * freqs
    ang = np.concatenate([ar, ar, ac, ac], axis=1).T.astype(np.float32)
    cos, sin = np.ones((QK, KEYS), np.float32), np.zeros((QK, KEYS), np.float32)
    cos[NOPE:, :T] = np.cos(ang)
    sign = np.array([-1.0] * 8 + [1.0] * 8 + [-1.0] * 8 + [1.0] * 8, np.float32)[:, None]
    sin[NOPE:, :T] = np.sin(ang) * sign
    return cos, sin


def kernel(**inputs):
    from concourse import bacc
    from concourse.bass_utils import run_bass_kernel_spmd

    i = {k: np.asarray(v) for k, v in inputs.items()}
    cos, sin = _rope()
    few = np.array([[1.0 / min(t + 1, 2 << g) for t in range(16)] for g in range(4)], np.float32)
    arrays = {
        "w": _stream(i),
        "ada": np.ascontiguousarray(i["ada_w"][0].reshape(KT, P, 24, 256).transpose(2, 1, 0, 3)),
        "cols": _columns(i),
        "x": _feature_major(i["x"][0]),
        "ctx": _feature_major(i["ctx"][0]),
        "mem": _feature_major(i["mem_2"][0]),
        "ident": np.eye(P, dtype=np.float32),
        "mask": np.where(np.arange(P)[None, :] <= np.arange(P)[:, None], 0.0, -1e30).astype(np.float32),
        "poolc": np.ascontiguousarray(np.broadcast_to(few, (P, 4, 16))),
        "cos": cos,
        "sin": sin,
    }
    nc = bacc.Bacc("TRN2", target_bir_lowering=False, num_devices=1)
    d = {n: nc.dram_tensor(f"in_{n}", a.shape, F, kind="ExternalInput").ap() for n, a in arrays.items()}
    out = nc.dram_tensor("out", (KT, P, T), F, kind="ExternalOutput").ap()
    build(nc, d, out)
    r = run_bass_kernel_spmd(nc, [{f"in_{n}": a for n, a in arrays.items()}], core_ids=[0])
    return np.ascontiguousarray(r.results[0]["out"].reshape(D, T).T).reshape(1, T, D)
```
